# Optimizing a Trainium2 kernel written in Bass

```python
import math
import jax, jax.numpy as jnp
from jax import lax
import numpy as np

D_MODEL = 2048
BATCH = 1
SEQ = 512
DEPTH = 2

GRID_W = 64
Q_BLOCK = 128
NORM_EPS = 1e-6
ROPE_THETA = 10000.0
NEG_INF = -1e30

A_HEADS = 8
A_DQK = 64
A_DV = 2 * A_DQK
A_WIDTH = A_HEADS * A_DV
B_HEADS = 8
B_NOPE = 128
B_ROPE = 64
B_DV = 128
B_Q_RANK = 768
B_KV_RANK = 512
B_WIDTH = B_HEADS * B_DV
C_HEADS = 8
C_DH = 128
C_WIDTH = C_HEADS * C_DH
NA_KH = 8
NA_KW = 16
D_HEADS = 8
D_KV_HEADS = 2
D_DH = 128
D_WIDTH = D_HEADS * D_DH

EVEN_SPLITS = (A_HEADS * 2 * A_DQK, A_HEADS * 2 * A_DQK, A_WIDTH, A_WIDTH,
               B_Q_RANK, B_KV_RANK, B_ROPE, B_WIDTH)
ODD_SPLITS = (C_WIDTH, C_WIDTH, C_WIDTH, C_WIDTH,
              D_HEADS * D_DH, D_KV_HEADS * D_DH, D_KV_HEADS * D_DH, D_WIDTH)
EVEN_IN = sum(EVEN_SPLITS)
ODD_IN = sum(ODD_SPLITS)
N_EVEN = (DEPTH + 1) // 2
N_ODD = DEPTH // 2

kernel_name = "hybrid_diffattn_mla_natten_axialgqa_encoder"

def rms_norm(x, gain):
    xf = x.astype(jnp.float32)
    y = xf * lax.rsqrt(jnp.mean(xf * xf, axis=-1, keepdims=True) + NORM_EPS)
    return (y * gain.astype(jnp.float32)).astype(x.dtype)

def split_cols(h, sizes):
    idx = np.cumsum(sizes)[:-1].tolist()
    return jnp.split(h, idx, axis=-1)

def rope(x, pos):
    half = x.shape[-1] // 2
    inv = ROPE_THETA ** (-jnp.arange(half, dtype=jnp.float32) / half)
    ang = pos.astype(jnp.float32)[:, None] * inv[None, :]
    shape = (1, x.shape[1]) + (1,) * (x.ndim - 3) + (half,)
    cos, sin = jnp.cos(ang).reshape(shape), jnp.sin(ang).reshape(shape)
    xf = x.astype(jnp.float32)
    x1, x2 = xf[..., :half], xf[..., half:]
    return jnp.concatenate([x1 * cos - x2 * sin, x1 * sin + x2 * cos], axis=-1).astype(x.dtype)

def axial_rope(x, row, col):
    half = x.shape[-1] // 2
    return jnp.concatenate([rope(x[..., :half], row), rope(x[..., half:], col)], axis=-1)

def to_blocks(t):
    b, s = t.shape[:2]
    return jnp.moveaxis(t.reshape((b, s // Q_BLOCK, Q_BLOCK) + t.shape[2:]), 1, 0)

def from_blocks(t):
    t = jnp.moveaxis(t, 0, 1)
    return t.reshape((t.shape[0], t.shape[1] * t.shape[2]) + t.shape[3:])

def diff_attention(q, k, v, lam, subln, lambda_init):
    b, s = q.shape[:2]
    q = q.reshape(b, s, A_HEADS, 2, A_DQK)
    k = k.reshape(b, s, A_HEADS, 2, A_DQK)
    v = v.reshape(b, s, A_HEADS, A_DV)
    pos = jnp.arange(s, dtype=jnp.float32)
    slopes = 2.0 ** (-8.0 * jnp.arange(1, A_HEADS + 1, dtype=jnp.float32) / A_HEADS)
    scale = A_DQK ** -0.5

    def block(args):
        qb, pb = args
        sc = jnp.einsum('bqhmd,bkhmd->bhmqk', qb, k).astype(jnp.float32) * scale
        alibi = -slopes[:, None, None] * jnp.abs(pb[:, None] - pos[None, :])[None]
        p = jax.nn.softmax(sc + alibi[None, :, None], axis=-1)
        w = p[:, :, 0] - lam * p[:, :, 1]
        return jnp.einsum('bhqk,bkhd->bqhd', w.astype(v.dtype), v)

    o = from_blocks(lax.map(block, (to_blocks(q), pos.reshape(-1, Q_BLOCK))))
    o = rms_norm(o, subln) * (1.0 - lambda_init)
    return o.reshape(b, s, A_WIDTH)

def latent_attention(cq, ckv, k_rope, q_norm, w_uq, kv_norm, w_ukv):
    b, s = cq.shape[:2]
    pos = jnp.arange(s)
    q = (rms_norm(cq, q_norm) @ w_uq).reshape(b, s, B_HEADS, B_NOPE + B_ROPE)
    q_nope, q_pe = q[..., :B_NOPE], rope(q[..., B_NOPE:], pos)
    kv = (rms_norm(ckv, kv_norm) @ w_ukv).reshape(b, s, B_HEADS, B_NOPE + B_DV)
    k_nope, v = kv[..., :B_NOPE], kv[..., B_NOPE:]
    k_pe = rope(k_rope, pos)
    scale = (B_NOPE + B_ROPE) ** -0.5

    def block(args):
        qn, qp = args
        sc = (jnp.einsum('bqhd,bkhd->bhqk', qn, k_nope)
              + jnp.einsum('bqhr,bkr->bhqk', qp, k_pe))
        p = jax.nn.softmax(sc.astype(jnp.float32) * scale, axis=-1)
        return jnp.einsum('bhqk,bkhd->bqhd', p.astype(v.dtype), v)

    o = from_blocks(lax.map(block, (to_blocks(q_nope), to_blocks(q_pe))))
    return o.reshape(b, s, B_WIDTH)

def neighbourhood_attention(q, k, v, rpb):
    b, s = q.shape[:2]
    rows = s // GRID_W
    kh = min(NA_KH, rows)
    scale = C_DH ** -0.5
    qg = q.reshape(b, rows, GRID_W, C_HEADS, C_DH)
    kg = k.reshape(b, rows, GRID_W, C_HEADS, C_DH)
    vg = v.reshape(b, rows, GRID_W, C_HEADS, C_DH)
    r = jnp.arange(rows)
    r0 = jnp.clip(r - kh // 2, 0, rows - kh)
    row_idx = r0[:, None] + jnp.arange(kh)[None, :]
    kb = kg[:, row_idx]
    vb = vg[:, row_idx]
    c = jnp.arange(GRID_W)
    c0 = jnp.clip(c - NA_KW // 2, 0, GRID_W - NA_KW)
    col_in = (c[None, :] >= c0[:, None]) & (c[None, :] < c0[:, None] + NA_KW)
    dr = row_idx - r[:, None] + NA_KH - 1
    dc = jnp.clip(c[None, :] - c[:, None], -(NA_KW - 1), NA_KW - 1) + NA_KW - 1
    bias = rpb[:, dr[:, None, :, None], dc[None, :, None, :]]
    sc = jnp.einsum('brqhd,brkwhd->bhrqkw', qg, kb).astype(jnp.float32) * scale + bias[None]
    sc = jnp.where(col_in[:, None, :], sc, NEG_INF)
    p = jax.nn.softmax(sc, axis=(-2, -1))
    o = jnp.einsum('bhrqkw,brkwhd->brqhd', p.astype(vb.dtype), vb)
    return o.reshape(b, s, C_WIDTH)

def axial_gqa(q, k, v, q_norm, k_norm):
    b, s = q.shape[:2]
    t = jnp.arange(s)
    row, col = t // GRID_W, t % GRID_W
    q = axial_rope(rms_norm(q.reshape(b, s, D_HEADS, D_DH), q_norm), row, col)
    k = axial_rope(rms_norm(k.reshape(b, s, D_KV_HEADS, D_DH), k_norm), row, col)
    q = q.reshape(b, s, D_KV_HEADS, D_HEADS // D_KV_HEADS, D_DH)
    v = v.reshape(b, s, D_KV_HEADS, D_DH)
    scale = D_DH ** -0.5

    def block(qb):
        sc = jnp.einsum('bqhgd,bkhd->bhgqk', qb, k).astype(jnp.float32) * scale
        p = jax.nn.softmax(sc, axis=-1)
        return jnp.einsum('bhgqk,bkhd->bqhgd', p.astype(v.dtype), v)

    o = from_blocks(lax.map(block, to_blocks(q)))
    return o.reshape(b, s, D_WIDTH)

def even_mixer(h, w_in, w_out, lq1, lk1, lq2, lk2, subln, q_norm, w_uq, kv_norm, w_ukv, lambda_init):
    qa, ka, va, ga, cq, ckv, kr, gb = split_cols(h @ w_in, EVEN_SPLITS)
    lam = (jnp.exp(jnp.sum(lq1.astype(jnp.float32) * lk1.astype(jnp.float32)))
           - jnp.exp(jnp.sum(lq2.astype(jnp.float32) * lk2.astype(jnp.float32))) + lambda_init)
    oa = diff_attention(qa, ka, va, lam, subln, lambda_init) * jax.nn.silu(ga)
    ob = latent_attention(cq, ckv, kr, q_norm, w_uq, kv_norm, w_ukv) * jax.nn.silu(gb)
    return jnp.concatenate([oa, ob], axis=-1) @ w_out

def odd_mixer(h, w_in, w_out, rpb, q_norm, k_norm):
    qc, kc, vc, gc, qd, kd, vd, gd = split_cols(h @ w_in, ODD_SPLITS)
    oc = neighbourhood_attention(qc, kc, vc, rpb) * jax.nn.silu(gc)
    od = axial_gqa(qd, kd, vd, q_norm, k_norm) * jax.nn.silu(gd)
    return jnp.concatenate([oc, od], axis=-1) @ w_out

def setup_inputs(seed: int = 0) -> dict:
    key = jax.random.key(seed)
    ks = jax.random.split(key, 20)

    def nrm(k, shape, scale):
        return jax.random.normal(k, shape, jnp.float32) * scale

    def gain(k, shape):
        return 1.0 + 0.02 * jax.random.normal(k, shape, jnp.float32)

    return {
        "x": nrm(ks[0], (BATCH, SEQ, D_MODEL), 1.0),
        "pre_norm": gain(ks[1], (DEPTH, D_MODEL)),
        "post_norm": gain(ks[2], (DEPTH, D_MODEL)),
        "even_w_in": nrm(ks[3], (N_EVEN, D_MODEL, EVEN_IN), D_MODEL ** -0.5),
        "even_w_out": nrm(ks[4], (N_EVEN, A_WIDTH + B_WIDTH, D_MODEL), (A_WIDTH + B_WIDTH) ** -0.5),
        "diff_lambda_q1": nrm(ks[5], (N_EVEN, A_DQK), 0.1),
        "diff_lambda_k1": nrm(ks[6], (N_EVEN, A_DQK), 0.1),
        "diff_lambda_q2": nrm(ks[7], (N_EVEN, A_DQK), 0.1),
        "diff_lambda_k2": nrm(ks[8], (N_EVEN, A_DQK), 0.1),
        "diff_subln": gain(ks[9], (N_EVEN, A_DV)),
        "mla_q_norm": gain(ks[10], (N_EVEN, B_Q_RANK)),
        "mla_w_uq": nrm(ks[11], (N_EVEN, B_Q_RANK, B_HEADS * (B_NOPE + B_ROPE)), B_Q_RANK ** -0.5),
        "mla_kv_norm": gain(ks[12], (N_EVEN, B_KV_RANK)),
        "mla_w_ukv": nrm(ks[13], (N_EVEN, B_KV_RANK, B_HEADS * (B_NOPE + B_DV)), B_KV_RANK ** -0.5),
        "odd_w_in": nrm(ks[14], (N_ODD, D_MODEL, ODD_IN), D_MODEL ** -0.5),
        "odd_w_out": nrm(ks[15], (N_ODD, C_WIDTH + D_WIDTH, D_MODEL), (C_WIDTH + D_WIDTH) ** -0.5),
        "na_rpb": nrm(ks[16], (N_ODD, C_HEADS, 2 * NA_KH - 1, 2 * NA_KW - 1), 0.1),
        "gqa_q_norm": gain(ks[17], (N_ODD, D_DH)),
        "gqa_k_norm": gain(ks[18], (N_ODD, D_DH)),
    }

def reference(x, pre_norm, post_norm, even_w_in, even_w_out, diff_lambda_q1, diff_lambda_k1,
              diff_lambda_q2, diff_lambda_k2, diff_subln, mla_q_norm, mla_w_uq, mla_kv_norm,
              mla_w_ukv, odd_w_in, odd_w_out, na_rpb, gqa_q_norm, gqa_k_norm):
    for layer in range(DEPTH):
        i = layer // 2
        h = rms_norm(x, pre_norm[layer])
        if layer % 2 == 0:
            lambda_init = 0.8 - 0.6 * math.exp(-0.3 * layer)
            m = even_mixer(h, even_w_in[i], even_w_out[i], diff_lambda_q1[i], diff_lambda_k1[i],
                           diff_lambda_q2[i], diff_lambda_k2[i], diff_subln[i], mla_q_norm[i],
                           mla_w_uq[i], mla_kv_norm[i], mla_w_ukv[i], lambda_init)
        else:
            m = odd_mixer(h, odd_w_in[i], odd_w_out[i], na_rpb[i], gqa_q_norm[i], gqa_k_norm[i])
        x = x + rms_norm(m, post_norm[layer])
    return x


_drawn_inputs = setup_inputs


def setup_inputs(seed=0):
    import zlib

    import numpy as np

    out = dict(_drawn_inputs(seed))
    spreads = {}
    factors = {'diff_lambda_q1': 64.0,
     'mla_q_norm': 8.0,
     'mla_kv_norm': 8.0,
     'gqa_q_norm': 8.0,
     'gqa_k_norm': 8.0,
     'diff_lambda_k2': 3.291,
     'diff_subln': 5.172,
     'na_rpb': 6.976}
    for name, (base, spread) in spreads.items():
        noise = np.random.default_rng([zlib.crc32(name.encode()), seed]).standard_normal(out[name].shape)
        drawn = base * np.exp(spread * noise) if base else spread * noise
        out[name] = __import__('jax').numpy.asarray(drawn.astype(out[name].dtype))
    for name, factor in factors.items():
        out[name] = (out[name] * factor).astype(out[name].dtype)
    return out
```

```python
import concourse.bass as bass
from concourse import mybir
from contextlib import ExitStack
import numpy as np

F32 = mybir.dt.float32
F32R = mybir.dt.float32r
ALU = mybir.AluOpType
ACT = mybir.ActivationFunctionType
AX = mybir.AxisListType

P = 128
SEQ = 512
DM = 2048
ST = SEQ // P
KT = DM // P
H = 8
GRID_W = 64
ROWS = SEQ // GRID_W
NA_KH, NA_KW = 8, 16
DR, DC = 2 * NA_KH - 1, 2 * NA_KW - 1
CW = (DR - 1) * GRID_W
Q_RANK, KV_RANK, ROPE_D = 768, 512, 64
QB, KVB = Q_RANK // P, KV_RANK // P
LAMBDA_INIT = 0.8 - 0.6
EPS = 1e-6
NEG = -1e30
SCALE_A = 64 ** -0.5
SCALE_B = 192 ** -0.5
SCALE_CD = 128 ** -0.5

RING = 4
AHEAD = 2
SLOT = 576

U_A = 0
U_PREP = U_A + H * KT
U_B = U_PREP + 5 * KT
U_OUT0 = U_B + H * 4
U_C = U_OUT0 + 4 * KT
U_D = U_C + H * KT
D_GROUP = KT + 3 * (KT // 2)
U_OUT1 = U_D + 2 * D_GROUP
U_END = U_OUT1 + 4 * KT

ORDER = ([("A", i) for i in range(H)] + [("prep", i) for i in range(5)] + [("B", i) for i in range(H)]
         + [("out0", i) for i in range(4)] + [("C", i) for i in range(H)] + [("D", i) for i in range(H)]
         + [("out1", i) for i in range(4)])


def count_before(test, part, i):
    if isinstance(i, int):
        return sum(test(*c) for c in ORDER[:ORDER.index((part, i))])
    return count_before(test, part, 0) + (i if test(part, 0) else 0)


def closing(bank, part, i):
    for u, place_in, places, blocks in ktiles(part, i):
        for b in blocks:
            if b[0] == bank and b[4]:
                return u, place_in == places - 1 and b is blocks[-1]
    return None


def use_of(bank, part, i):
    return count_before(lambda p, j: closing(bank, p, j) is not None, part, i)


def proj_of(bank, part, i):
    return count_before(lambda p, j: closing(bank, p, j) is not None and not closing(bank, p, j)[1], part, i)


def s_before(t, part):
    return 8 * t if part == "A" else 32 + 4 * t


def nmax_before(t, part):
    return 4 * (t - 8) if part == "B" else 4 * (t - 16)


def rot_of(t, part):
    return t - 8 if part == "B" else t - 16


def kv_of(t, part):
    return t if part != "D" else 24 + (t - 24) // 4


def units_of(part, i):
    if part == "D":
        return U_D + i // 4 * D_GROUP + (KT + (i % 4 - 1) * KT // 2 if i % 4 else 0), 0, 0
    return {"A": U_A, "prep": U_PREP, "B": U_B, "out0": U_OUT0, "C": U_C, "out1": U_OUT1}[part], \
        4 if part == "B" else KT, i


def i_is_zero(i):
    return isinstance(i, int) and i == 0


def raw_count(u):
    total = 0
    for v in range(u % RING, u + 1, RING):
        in_d = U_D <= v < U_OUT1
        total += (3 if (v - U_D) % D_GROUP < KT else 4) if in_d else 1
    return 16 * total


def wait(eng, sem, value):
    if isinstance(value, int) and value <= 0:
        return
    eng.wait_ge(sem, value)


def wait_apart(eng, sem, value):
    eng.wait_ge(sem, value)
    eng.nop(nofuse=True)


def q_bank(i):
    return 2 if i % 4 == 2 else 0


def ktiles(part, i):
    if part == "B":
        out = [(s // 3, s % 3, 3, [(2, s % 3 * 192, P, s == 0, s == QB - 1, s),
                                   (3, s % 3 * 192 + P, ROPE_D, s == 0, s == QB - 1, s)]) for s in range(QB)]
        out += [(2 + s // 2, s % 2, 2, [(0, s % 2 * 256, P, s == 0, s == KVB - 1, QB + s),
                                        (1, s % 2 * 256 + P, P, s == 0, s == KVB - 1, QB + s)]) for s in range(KVB)]
        return out
    if part == "D" and i % 4:
        return [(s // 2, s % 2, 2, [(q_bank(i) + b, s % 2 * 256 + b * P, P, s == 0, s == KT - 1, s)
                                    for b in range(2)]) for s in range(KT)]
    blocks = [(b, b * P, P) for b in range(4)]
    if part == "prep" and i == 2:
        blocks = [(0, 0, P), (1, P, P), (2, 2 * P, ROPE_D)]
    first = blocks[2:] + blocks[:2] if part == "D" and i == 4 else blocks
    return [(s, 0, 1, [(*b, s == 0, s == KT - 1, s) for b in (blocks if s else first)]) for s in range(KT)]


def unit_width(u):
    if U_PREP + 2 * KT <= u < U_PREP + 3 * KT:
        return 2 * P + ROPE_D
    if U_B <= u < U_OUT0 and (u - U_B) % 4 < 2:
        return SLOT
    return 512


WOVEN = {
    "A": {0: ["v"], 1: ["s0", "s1"], 2: ["s2", "s3"], 3: ["s4", "s5"], 4: ["s6", "s7"], 6: ["pt0", "pt1"],
          7: ["pv0", "pt2"], 8: ["pv1", "pt3"], 9: ["pv2"], 10: ["pv3"], 12: ["stat"], 14: ["spread"],
          15: ["gate"]},
    "C": {0: ["v"], 1: ["s0"], 2: ["s1"], 3: ["s2"], 4: ["s3"], 6: ["pt0", "pt1"],
          7: ["pv0", "pt2"], 8: ["pv1", "pt3"], 9: ["pv2"], 10: ["pv3"], 11: ["gate"]},
    "B": {0: ["v"], 1: ["s0"], 2: ["s1"], 3: ["s2"], 4: ["s3"], 6: ["own q", "pt0", "pt1"],
          7: ["own rot", "pv0", "pt2"], 8: ["pv1", "pt3"], 9: ["pv2", "pv3"], "end": ["gate"]},
    "Bfirst": {6: ["own q"], 7: ["own rot"]},
    "D": {1: ["rot"], 2: ["stat"], 5: ["s0"], 6: ["s1"], 7: ["s2"], 8: ["s3"], 10: ["pt0", "pt1"],
          11: ["pv0", "pt2"], 12: ["pv1", "pt3"], 13: ["pv2"], 14: ["pv3", "gate"]},
    "Dkv": {1: ["krot", "kstat"], 2: ["rot", "stat"], 5: ["kspread"], 6: ["v"], 7: ["s0"], 8: ["s1"], 9: ["s2"],
            10: ["s3"], 12: ["pt0", "pt1"], 13: ["pv0", "pt2"], 14: ["pv1", "pt3"],
            15: ["pv2", "pv3", "gate"]},
    "table": {s: [f"tab{s}"] for s in range(16)},
    "lstat": {0: ["krope"], **{s + 1: [f"lstat{s}"] for s in range(QB + KVB)}},
    "lnorm": {0: ["lspreadq"], 1: ["lnorm0"], 2: ["lnorm1"], 3: ["lnorm2"], 4: ["lnorm3"], 5: ["lnorm4"],
              6: ["lnorm5"], 7: ["lspreadk"], 8: ["lnorm6"], 9: ["lnorm7"], 10: ["lnorm8"], 11: ["lnorm9"]},
    None: {},
}


def build(nc, x, pre_norm, post_norm, even_w_in, even_w_out, lq1, lk1, lq2, lk2, subln, q_norm, w_uq,
          kv_norm, w_ukv, odd_w_in, odd_w_out, rpb, gq_norm, gk_norm, c_alibi, c_small, c_shift,
          c_rope_b, c_rope_d, x1, tables, out):
    ctx = ExitStack()
    with ctx:
        top = [(nc.sbuf_base + 31) // 32 * 32]

        def region(size):
            at = top[0]
            top[0] += size
            assert top[0] <= nc.sbuf_usable_end, top[0]
            return at

        def place(name, at, shape, dt=F32):
            return nc.alloc_sbuf_tensor_at(name, shape, dt, offset=at)

        def sem(name):
            return ctx.enter_context(nc.semaphore(name))

        KB = 1024
        X, O, W = region(64 * KB), region(64 * KB), region(42 * KB)

        xT_hi = place("xT_hi", X, [P, KT, SEQ], F32R)
        xT_lo = place("xT_lo", X + 32 * KB, [P, KT, SEQ], F32R)
        resid = place("resid", X, [P, ST, DM])
        oT_hi = place("oT_hi", O, [P, 2 * H, SEQ], F32R)
        oT_lo = place("oT_lo", O + 32 * KB, [P, 2 * H, SEQ], F32R)
        gates_b = place("gates_b", O + 16 * KB, [P, H, SEQ])
        lsq = place("lsq", O + 48 * KB, [P, 2, SEQ])
        th_b = place("th_b", O + 52 * KB, [P, SEQ])
        ldiag = place("ldiag", O + 54 * KB, [P, ST, P])
        krt = place("krt", O + 56 * KB, [ROPE_D, 4, SEQ])
        xrow = place("xrow", O, [P, ST, DM])
        hrow = place("hrow", O + 32 * KB, [P, ST, DM])
        table_all = place("table_all", O, [P, H, DR - 1, GRID_W])
        lat_hi = place("lat_hi", W, [P, QB + KVB, SEQ], F32R)
        lat_lo = place("lat_lo", W + 20 * KB, [P, QB + KVB, SEQ], F32R)
        lat_raw = place("lat_raw", W + 20 * KB, [P, QB + KVB, SEQ])
        lat_tmp = place("lat_tmp", W + 40 * KB, [P, SEQ])
        mrow = place("mrow", W, [P, ST, DM])
        post_gain = place("post_gain", W + 32 * KB, [P, DM])
        squares = place("squares", W + 40 * KB, [P, SEQ])

        class Work:
            pass

        def work(tag, at):
            w = Work()
            a = [at]

            def b(name, shape, dt=F32):
                t = place(f"{name}_{tag}", a[0], shape, dt)
                a[0] += int(np.prod(shape[1:])) * 4
                return t
            w.q_hi, w.q_lo = b("q_hi", [P, SEQ], F32R), b("q_lo", [P, SEQ], F32R)
            w.k_hi, w.k_lo = b("k_hi", [P, SEQ], F32R), b("k_lo", [P, SEQ], F32R)
            w.v_hi, w.v_lo = b("v_hi", [P, ST, P], F32R), b("v_lo", [P, ST, P], F32R)
            w.vT = b("vT", [P, SEQ])
            w.p = b("p", [P, ST, SEQ])
            w.pT_hi, w.pT_lo = b("pT_hi", [P, 2, SEQ], F32R), b("pT_lo", [P, 2, SEQ], F32R)
            w.g = b("g", [P, SEQ])
            w.diag = place(f"diag_{tag}", a[0], [P, ST, P])
            w.th = b("th", [P, SEQ])
            w.sb = place(f"sb_{tag}", a[0], [P, 2, SEQ])
            w.e = place(f"e_{tag}", a[0] + 2 * SEQ * 4, [P, 2, SEQ])
            w.rq, w.rq_sin, w.rk, w.rk_sin = (b(f"r{j}", [P, SEQ]) for j in range(4))
            w.end = a[0]
            return w

        w_acd = work("w", W)
        assert w_acd.end <= W + 42 * KB, (w_acd.end - W)
        w_b = work("x", X + 20 * KB)
        pe_hi = place("pe_hi", X, [ROPE_D, SEQ], F32R)
        pe_lo = place("pe_lo", X + 2 * KB, [ROPE_D, SEQ], F32R)
        res_b = place("res_b", X + 8 * KB, [P, SEQ])
        assert w_b.end <= X + 64 * KB

        raw_at, split_at = region(RING * SLOT * 4), region(2 * RING * SLOT * 4)
        raw = place("raw", raw_at, [P, RING, SLOT])
        w_hi = place("w_hi", split_at, [P, RING, SLOT], F32R)
        w_lo = place("w_lo", split_at + RING * SLOT * 4, [P, RING, SLOT], F32R)

        def small(name, cols, dt=F32, parts=P):
            return place(name, region((cols * 4 + 31) // 32 * 32), [parts, cols], dt)
        bias_at = region(CW * 4)
        bias = place("bias", bias_at, [P, CW])
        rope_at = region(2 * SEQ * 4)
        rope = place("rope", rope_at, [P, 2, SEQ])
        kpe_at = X + 4 * KB
        kpe_hi = place("kpe_hi", kpe_at, [ROPE_D, SEQ], F32R)
        kpe_lo = place("kpe_lo", kpe_at + 2 * KB, [ROPE_D, SEQ], F32R)
        consts = small("consts", 2 * P + GRID_W)
        ident = consts[:, 0:P]
        rotT = consts[:, P:2 * P]
        mask = consts[:, 2 * P:2 * P + GRID_W]
        ones = small("ones", P)
        gains = small("gains", 2 * KT + QB + KVB + 3)
        pre_gain = gains[:, 0:2 * KT]
        lat_gain = gains[:, 2 * KT:2 * KT + QB + KVB]
        sub_gain = gains[:, 2 * KT + QB + KVB:2 * KT + QB + KVB + 1]
        gq_gain = gains[:, 2 * KT + QB + KVB + 1:2 * KT + QB + KVB + 2]
        gk_gain = gains[:, 2 * KT + QB + KVB + 2:2 * KT + QB + KVB + 3]
        st = small("st", 106)
        esum = st[:, 0:8]
        rsum = st[:, 8:16]
        nmax = st[:, 16:24]
        mixc = st[:, 24:28]
        var = st[:, 28:36]
        var2 = st[:, 36:44]
        rstd = st[:, 44:52]
        rscale = st[:, 52:56]
        rowsq = st[:, 56:72]
        rowvar = st[:, 72:76]
        rowstd = st[:, 76:80]
        prevar = st[:, 94:98]
        prestd = st[:, 98:102]
        tmpvar = st[:, 102:106]
        neglam = st[:, 80:81]
        lam = st[:, 81:85]
        gate_gain = st[:, 85:86]
        kstd = st[:, 86:90]
        nm = st[:, 90:94]
        expo = small("expo", 8)

        lamv = place("lamv", W, [P, 4, 64])
        lamp = place("lamp", W + KB, [P, 2, 64])
        rpb_rows = place("rpb_rows", W + 2 * KB, [H * DR, DC])
        rpbT = place("rpbT", W + 3 * KB, [DC, H, DR])
        shift = place("shift", W + 4 * KB, [32, 2 * GRID_W - 1])
        sq_junk = place("sq_junk", W + 8 * KB, [P, DM])

        bank = [ctx.enter_context(nc.psum_tensor(f"bank{i}", [P, 512], F32)) for i in range(8)]
        B_S, B_T, B_O = (4, 5), 6, 7
        tb, ob = bank[B_T], bank[B_O]
        krb, rb = bank[B_S[0]], bank[B_S[1]]

        raw_in = [sem(f"raw_in{i}") for i in range(RING)]
        hi_made, lo_made = sem("hi_made"), sem("lo_made")
        w_used = sem("w_used")
        proj = [sem(f"proj{i}") for i in range(4)]
        bank_free = [sem(f"bank_free{i}") for i in range(4)]
        consts_in, x_in, lam_in = sem("consts_in"), sem("x_in"), sem("lam_in")
        resid_in, gain_in = sem("resid_in"), sem("gain_in")
        rope_in, bias_in = sem("rope_in"), sem("bias_in")
        ones_set = sem("ones_set")
        x1_out, out_out, tables_out = sem("x1_out"), sem("out_out"), sem("tables_out")
        m_copied, m_total, m_var, m_pow, m_scaled = (
            sem(n) for n in ("m_copied", "m_total", "m_var", "m_pow", "m_scaled"))
        x_made, x_sq, x_var, x_pow, h_made = (sem(n) for n in ("x_made", "x_sq", "x_var", "x_pow", "h_made"))
        xt_turned, xt_hi, xt_lo = sem("xt_turned"), sem("xt_hi"), sem("xt_lo")
        q_hi_s, q_lo_s, k_hi_s, k_lo_s = sem("q_hi_s"), sem("q_lo_s"), sem("k_hi_s"), sem("k_lo_s")
        pe_hi_s, pe_lo_s, kpe_hi_s, kpe_lo_s = sem("pe_hi_s"), sem("pe_lo_s"), sem("kpe_hi_s"), sem("kpe_lo_s")
        v_turned, v_hi_s, v_lo_s = sem("v_turned"), sem("v_hi_s"), sem("v_lo_s")
        th_made = sem("th_made")
        scored, s_read, nmaxed, exped = sem("scored"), sem("s_read"), sem("nmaxed"), sem("exped")
        recip_s, mixc_s, p_made = sem("recip_s"), sem("mixc_s"), sem("p_made")
        p_turned, pT_hi_s, pT_lo_s, pv_done = sem("p_turned"), sem("pT_hi_s"), sem("pT_lo_s"), sem("pv_done")
        o_read, o_gated, o_hi_s, o_lo_s = sem("o_read"), sem("o_gated"), sem("o_hi_s"), sem("o_lo_s")
        o_sq, a_stat, a_var, a_pow, a_diag, a_spread = (
            sem(n) for n in ("o_sq", "a_stat", "a_var", "a_pow", "a_diag", "a_spread"))
        r_in, r_rot, r_cos, r_sin, r_sum = (sem(n) for n in ("r_in", "r_rot", "r_cos", "r_sin", "r_sum"))
        kr_in, kr_rot, kr_cos, kr_sin, kr_sum = (sem(n) for n in ("kr_in", "kr_rot", "kr_cos", "kr_sin", "kr_sum"))
        d_stat, d_var, d_pow = (sem(n) for n in ("d_stat", "d_var", "d_pow"))
        k_stat, k_var, k_pow, k_diag, k_spread, k_scaled = (
            sem(n) for n in ("k_stat", "k_var", "k_pow", "k_diag", "k_spread", "k_scaled"))
        l_sq, l_stat, l_var, l_pow, l_diag, l_spread, l_mul, l_hi, l_lo = (
            sem(n) for n in ("l_sq", "l_stat", "l_var", "l_pow", "l_diag", "l_spread", "l_mul",
                             "l_hi", "l_lo"))
        rpb_turned, rpb_copied, t_done, t_evac = (sem(n) for n in ("rpb_turned", "rpb_copied", "t_done", "t_evac"))
        lam_dot, lam_exp, lam_sum = sem("lam_dot"), sem("lam_exp"), sem("lam_sum")

        win0, wout0, win1, wout1 = even_w_in[0], even_w_out[0], odd_w_in[0], odd_w_out[0]
        block = ctx.enter_context(nc.Block())

        def block_done(eng, b, part, i):
            u, with_unit = closing(b, part, i)
            if with_unit:
                first, turn_units, turn = units_of(part, i)
                eng.wait_ge(w_used, first + turn * turn_units + u + 1)
            else:
                eng.wait_ge(proj[b], proj_of(b, part, i) + 1)

        def block_out(eng, b, part, i):
            eng.wait_ge(bank_free[b], use_of(b, part, i) + 1)

        def chunk_of(t, part):
            return t - {"A": 0, "B": H, "C": 2 * H, "D": 3 * H}[part]

        def turned(j):
            return bank[B_S[0] if j % 2 else B_T]

        def gate_out(eng, t, part):
            if part == "B":
                block_out(eng, 3, "prep", 4)
            else:
                c = chunk_of(t, part)
                block_out(eng, q_bank(c) + 1 if part == "D" else 3, part, c)

        def work_of(part):
            return w_b if part == "B" else w_acd

        def o_slot(t, part):
            return t if part in ("A", "B") else t - 2 * H

        @block.sync
        def _(sp):
            def unit(n, slot, *pieces):
                wait(sp, lo_made, n - RING + 1)
                for c0, c1, src in pieces:
                    dst = raw[:, slot, c0:c1]
                    if len(src.shape) == 3:
                        dst = dst.rearrange("p (b c) -> p b c", b=src.shape[1])
                    sp.dma_start(dst, src).then_inc(raw_in[slot], 16)

            def head_units(w, first, i):
                for s in range(KT):
                    cols = w[s * P:(s + 1) * P, 0:4 * H * P].rearrange("p (b c) -> p b c", b=4)
                    unit(first + i * KT + s, s % RING, (0, 512, cols[:, :, bass.ds(i * P, P)]))

            for t in range(ST):
                sp.dma_start(xrow[:, t, :], x[0, t * P:(t + 1) * P, :]).then_inc(x_in, 16)
            head_units(win0, U_A, 0)
            with sp.Fori(1, H) as i:
                head_units(win0, U_A, i)
            for c in range(5):
                c0 = 4 * H * P + (c * 512 if c < 3 else Q_RANK + KV_RANK + ROPE_D + (c - 3) * 512)
                width = 2 * P + ROPE_D if c == 2 else 512
                for s in range(KT):
                    unit(U_PREP + c * KT + s, s % RING, (0, width, win0[s * P:(s + 1) * P, c0:c0 + width]))

            def latent_units(i):
                for s in range(2):
                    src = w_uq[0, s * 384:(s + 1) * 384, bass.ds(i * 192, 192)]
                    unit(U_B + i * 4 + s, s, (0, 576, src.rearrange("(k p) c -> p k c", p=P)))
                for s in range(2):
                    src = w_ukv[0, s * 256:(s + 1) * 256, bass.ds(i * 256, 256)]
                    unit(U_B + i * 4 + 2 + s, 2 + s, (0, 512, src.rearrange("(k p) c -> p k c", p=P)))
            latent_units(0)
            with sp.Fori(1, H) as i:
                latent_units(i)

            def out_units(w, first):
                with sp.Fori(0, 4) as c:
                    for s in range(KT):
                        unit(first + c * KT + s, s % RING, (0, 512, w[s * P:(s + 1) * P, bass.ds(c * 512, 512)]))
            out_units(wout0, U_OUT0)
            with sp.Fori(0, H) as i:
                head_units(win1, U_C, i)
            q0 = 4 * H * P
            k0, g0 = q0 + H * P, q0 + H * P + 4 * P
            for g in range(2):
                for j in range(4):
                    h = 4 * g + j

                    def cols(s, c0):
                        return win1[s * P:(s + 1) * P, c0:c0 + P]
                    if j == 0:
                        for s in range(KT):
                            kv = win1[s * P:(s + 1) * P, k0:k0 + 4 * P].rearrange("p (b c) -> p b c", b=2)
                            unit(U_D + g * D_GROUP + s, s % RING, (0, P, cols(s, q0 + h * P)),
                                 (P, 2 * P, cols(s, g0 + h * P)), (2 * P, 4 * P, kv[:, :, g * P:(g + 1) * P]))
                    else:
                        for s in range(0, KT, 2):
                            unit(U_D + g * D_GROUP + KT + (j - 1) * KT // 2 + s // 2, s // 2 % RING,
                                 (0, P, cols(s, q0 + h * P)), (P, 2 * P, cols(s, g0 + h * P)),
                                 (2 * P, 3 * P, cols(s + 1, q0 + h * P)), (3 * P, 4 * P, cols(s + 1, g0 + h * P)))
            out_units(wout1, U_OUT1)

        @block.gpsimd
        def _(pool):
            pool.dma_start(consts[:, :], c_small[:, :]).then_inc(consts_in, 16)
            for dst, src, k in ((gains[:, 0:KT], pre_norm[0], KT), (gains[:, KT:2 * KT], pre_norm[1], KT),
                                (lat_gain[:, 0:QB], q_norm[0], QB), (lat_gain[:, QB:QB + KVB], kv_norm[0], KVB),
                                (sub_gain, subln[0], 1), (gq_gain, gq_norm[0], 1), (gk_gain, gk_norm[0], 1)):
                pool.dma_start(dst, src.rearrange("(k p) -> p k", p=P), allow_slow_non_contiguous=True
                               ).then_inc(consts_in, 16)
            pool.dma_start(shift[:, :], c_shift[:, :]).then_inc(consts_in, 16)
            pool.dma_start(rpb_rows[:, :], rpb[0].rearrange("h r c -> (h r) c")).then_inc(consts_in, 16)
            for j, v in enumerate((lq1, lk1, lq2, lk2)):
                pool.dma_start(lamv[:, j, :], v[0:1, :].to_broadcast([P, 64])).then_inc(lam_in, 16)
            pool.dma_start(bias[:, :], c_alibi[0]).then_inc(bias_in, 16)
            pool.dma_start(rope[0:ROPE_D, :, :], c_rope_b.rearrange("a p s -> p a s")).then_inc(rope_in, 16)
            pool.memset(ones[:, :], 1.0).then_inc(ones_set, 1)
            pool.memset(expo[:, :], -0.5).then_inc(ones_set, 1)
            pool.wait_ge(ones_set, 2)

            def inv_root(dst, src, scale, tmp, mid, mid_value, done):
                pool.tensor_scalar(tmp, src, scale, EPS, ALU.mult, ALU.add).then_inc(mid, 1)
                pool.wait_ge(mid, mid_value)
                pool.tensor_tensor(dst, tmp, expo[:, 0:src.shape[1]], ALU.pow).then_inc(done, 1)

            def diagonals(diag, column, done):
                for j in range(ST):
                    pool.tensor_scalar(diag[:, j, :], ident, column[:, j:j + 1], 0.0, ALU.mult, ALU.add
                                       ).then_inc(done, 1)

            def pre_rows(layer):
                for t in range(ST):
                    n = layer * ST + t + 1
                    pool.wait_ge(x_sq, n)
                    inv_root(prestd[:, t:t + 1], prevar[:, t:t + 1], 1.0 / DM, tmpvar[:, t:t + 1], x_var, n, x_pow)

            def post_rows(layer):
                pool.wait_ge(m_total, layer + 1)
                inv_root(rowstd, rowvar, 1.0 / DM, tmpvar, m_var, layer + 1, m_pow)

            def post_loads(layer):
                pool.wait_ge(o_lo_s, 2 * H * (layer + 1))
                pool.dma_start(post_gain[:, :], post_norm[layer:layer + 1, :].to_broadcast([P, DM])
                               ).then_inc(gain_in, 16)
                pool.wait_ge(w_used, U_OUT0 if layer == 0 else U_OUT1)
                pool.dma_start(resid[:, :, :], (x[0] if layer == 0 else x1).rearrange("(t p) d -> p t d", p=P)
                               ).then_inc(resid_in, 16)

            pre_rows(0)
            pool.wait_ge(t_evac, KT)
            pool.dma_start(tables.rearrange("h p c -> p h c"),
                           table_all[:, :, :, :].rearrange("p h j c -> p h (j c)")).then_inc(tables_out, 16)

            def next_bias(src, i, t, part):
                pool.wait_ge(s_read, s_before(t + 1, part))
                pool.dma_start(bias[:, :], src[bass.ds(i, 1), :, :].rearrange("a p c -> (a p) c")
                               ).then_inc(bias_in, 16)

            def a_factors(t):
                wait_apart(pool, a_var, 2 * t + 2)
                pool.tensor_scalar(var2[:, 0:ST], var[:, 0:ST], 1.0 / P, EPS, ALU.mult, ALU.add).then_inc(a_pow, 1)
                pool.wait_ge(a_pow, 3 * t + 1)
                pool.tensor_tensor(rstd[:, ST:2 * ST], var2[:, 0:ST], expo[:, 0:ST], ALU.pow).then_inc(a_pow, 1)
                pool.wait_ge(a_pow, 3 * t + 2)
                pool.tensor_tensor(rstd[:, 0:ST], rstd[:, ST:2 * ST], rsum[:, 0:ST], ALU.mult).then_inc(a_pow, 1)
                gate_out(pool, t, "A")
                wait_apart(pool, a_pow, 3 * t + 3)
                diagonals(w_acd.diag, rstd, a_diag)

            with pool.Fori(1, H) as i:
                next_bias(c_alibi, i, i - 1, "A")
                a_factors(i - 1)
            a_factors(H - 1)

            block_out(pool, 2, "prep", 2)
            pool.wait_ge(rope_in, 16)
            pool.tensor_tensor(krt[:, 1, :], krt[:, 0, :], rope[0:ROPE_D, 0, :], ALU.mult).then_inc(kr_cos, 1)
            pool.wait_ge(kr_sin, 1)
            pool.wait_ge(kr_cos, 1)
            pool.tensor_tensor(krt[:, 3, :], krt[:, 1, :], krt[:, 2, :], ALU.add).then_inc(kr_sum, 1)
            pool.wait_ge(l_var, 1)
            inv_root(rstd[:, 0:ST], var[:, 0:ST], 1.0 / Q_RANK, var2[:, 0:ST], l_pow, 1, l_pow)
            inv_root(rstd[:, ST:2 * ST], var[:, ST:2 * ST], 1.0 / KV_RANK, var2[:, ST:2 * ST], l_pow, 3, l_pow)
            pool.wait_ge(l_pow, 4)
            diagonals(ldiag, rstd[:, 0:ST], l_diag)
            pool.wait_ge(l_spread, 1)
            diagonals(ldiag, rstd[:, ST:2 * ST], l_diag)

            with pool.Fori(0, H) as i:
                block_out(pool, 3, "B", i)
                pool.wait_ge(r_rot, i + 1)
                pool.tensor_tensor(w_b.rk[0:ROPE_D, :], w_b.rq[0:ROPE_D, :], rope[0:ROPE_D, 0, :], ALU.mult
                                   ).then_inc(r_cos, 1)
                pool.wait_ge(r_sin, i + 1)
                pool.wait_ge(r_cos, i + 1)
                pool.tensor_tensor(w_b.rk_sin[0:ROPE_D, :], w_b.rk[0:ROPE_D, :], w_b.rq_sin[0:ROPE_D, :], ALU.add
                                   ).then_inc(r_sum, 1)
            pool.dma_start(rope[:, :, :], c_rope_d.rearrange("a p s -> p a s")).then_inc(rope_in, 16)
            pool.wait_ge(tables_out, 16)
            pool.dma_start(bias[:, :], tables[0]).then_inc(bias_in, 16)
            post_loads(0)
            post_rows(0)
            pre_rows(1)
            with pool.Fori(1, H) as i:
                next_bias(tables, i, 2 * H - 1 + i, "C")

            pool.wait_ge(rope_in, 32)
            for n in range(H):
                g = n // 4
                if n % 4 == 0:
                    pool.wait_ge(kr_rot, g + 2)
                    pool.tensor_tensor(w_acd.rk[:, :], w_acd.rk[:, :], rope[:, 0, :], ALU.mult).then_inc(kr_cos, 1)
                    pool.wait_ge(kr_sin, g + 2)
                    pool.wait_ge(kr_cos, g + 2)
                    pool.tensor_tensor(w_acd.rk[:, :], w_acd.rk[:, :], w_acd.rk_sin[:, :], ALU.add
                                       ).then_inc(kr_sum, 1)
                    pool.wait_ge(k_var, g + 1)
                    inv_root(kstd, var[:, ST:2 * ST], 1.0 / P, var2[:, ST:2 * ST], k_pow, 2 * g + 1, k_pow)
                    pool.wait_ge(k_pow, 2 * g + 2)
                    gate_out(pool, 3 * H + n, "D")
                    diagonals(w_acd.diag, kstd, k_diag)
                pool.wait_ge(r_rot, H + n + 1)
                pool.tensor_tensor(w_acd.rq[:, :], w_acd.rq[:, :], rope[:, 0, :], ALU.mult).then_inc(r_cos, 1)
                pool.wait_ge(r_sin, H + n + 1)
                pool.wait_ge(r_cos, H + n + 1)
                pool.tensor_tensor(w_acd.rq[:, :], w_acd.rq[:, :], w_acd.rq_sin[:, :], ALU.add).then_inc(r_sum, 1)
                pool.wait_ge(d_var, n + 1)
                inv_root(rstd[:, 0:ST], var[:, 0:ST], 1.0 / P, var2[:, 0:ST], d_pow, 3 * n + 1, d_pow)
                pool.wait_ge(d_pow, 3 * n + 2)
                pool.tensor_scalar(rscale, rstd[:, 0:ST], SCALE_CD, 0.0, ALU.mult, ALU.add).then_inc(d_pow, 1)
            post_loads(1)
            post_rows(1)

        def unit_of(first, turn_units, i, s):
            n = first + i * turn_units + s
            return n, (n if isinstance(n, int) else first + s % turn_units)

        @block.scalar
        def _(act):
            def split(first, turn_units, i, s):
                n, like = unit_of(first, turn_units, i, s)
                if isinstance(n, int) and n >= U_END:
                    return
                slot, width = s % RING, unit_width(like)
                if isinstance(n, int):
                    act.wait_ge(raw_in[slot], raw_count(n))
                else:
                    act.wait_ge(raw_in[slot], raw_count(first + s) + i * (16 * turn_units // RING))
                wait(act, w_used, n - RING + 1)
                act.activation(w_hi[:, slot, 0:width], raw[:, slot, 0:width], ACT.Copy).then_inc(hi_made, 1)

            def rows_norm(layer):
                for t in range(ST):
                    if layer == 0:
                        act.wait_ge(x_in, 16 * ST)
                    else:
                        act.wait_ge(x_made, t + 1)
                        act.dma_start(x1[t * P:(t + 1) * P, :], xrow[:, t, :]).then_inc(x1_out, 16)
                    wait(act, x_sq, ST * layer + t)
                    junk = sq_junk[:, :] if layer == 0 else resid[:, 0, :]
                    act.activation(junk, xrow[:, t, :], ACT.Square, accum_out=prevar[:, t:t + 1]).then_inc(x_sq, 1)

            def turn_hi(layer):
                act.wait_ge(consts_in, 160)
                for k in range(KT):
                    n = layer * KT + k
                    act.wait_ge(xt_turned, n + 1)
                    act.activation(xT_hi[:, k, :], bank[4 + k % 4][:, :], ACT.Copy, scale=pre_gain[:, n:n + 1]
                                   ).then_inc(xt_hi, 1)

            def item(what, part, t):
                w = work_of(part)
                if what == "v":
                    act.wait_ge(v_turned, kv_of(t, part) + 1)
                    act.activation(w.v_hi[:, :, :], tb[:, :].rearrange("p (a b) -> p a b", a=ST), ACT.Copy
                                   ).then_inc(v_hi_s, 1)
                elif what[0] == "s" and what[1:].isdigit():
                    j = int(what[1:])
                    n = s_before(t, part) + j
                    if part == "A":
                        act.wait_ge(s_read, n + 1)
                        if j >= 2:
                            act.wait_ge(p_made, 4 * t + j // 2)
                        cell = j % 2 * 4 + j // 2
                        act.activation(w.e[:, j % 2, :], w.sb[:, j % 2, :], ACT.Exp, bias=nmax[:, j:j + 1],
                                       scale=-1.0, accum_out=esum[:, cell:cell + 1]).then_inc(exped, 1)
                    elif part == "C":
                        act.wait_ge(s_read, n + 1)
                        act.wait_ge(p_turned, 4 * t)
                        act.activation(w.p[:, j, :], w.sb[:, j % 2, :], ACT.Exp, bias=nmax[:, j:j + 1],
                                       scale=-1.0, accum_out=esum[:, j:j + 1]).then_inc(exped, 1)
                    else:
                        act.wait_ge(nmaxed, nmax_before(t, part) + j + 1)
                        act.wait_ge(p_turned, 4 * t)
                        act.activation(w.p[:, j, :], bank[B_S[j % 2]][:, :], ACT.Exp, bias=nmax[:, j:j + 1],
                                       scale=SCALE_B if part == "B" else rscale[:, j:j + 1],
                                       accum_out=esum[:, j:j + 1]).then_inc(exped, 1)
                elif what[:2] == "pt":
                    j = int(what[2:])
                    act.wait_ge(p_turned, 4 * t + j + 1)
                    if j >= 2:
                        act.wait_ge(pv_done, 4 * t + j - 1)
                    act.activation(w.pT_hi[:, j % 2, :], turned(j)[:, :], ACT.Copy).then_inc(pT_hi_s, 1)
                elif what == "stat" and part == "A":
                    act.wait_ge(pv_done, 4 * t + 4)
                    act.activation(w.vT[:, :], ob[:, :], ACT.Square).then_inc(o_sq, 1)
                elif what == "rot":
                    act.wait_ge(r_sum, rot_of(t, part) + 1)
                    if part == "B":
                        act.activation(pe_hi[:, :], w.rk_sin[0:ROPE_D, :], ACT.Copy).then_inc(pe_hi_s, 1)
                    else:
                        act.activation(w.q_hi[:, :], w.rq[:, :], ACT.Copy).then_inc(q_hi_s, 1)
                elif what == "kspread":
                    act.wait_ge(k_scaled, (t - 24) // 4 + 1)
                    act.activation(w.k_hi[:, :], w.rk_sin[:, :], ACT.Copy).then_inc(k_hi_s, 1)
                elif what == "gate":
                    act.wait_ge(o_gated, t + 1)
                    if part == "A":
                        act.wait_ge(tables_out, 16)
                    if part == "C":
                        act.wait_ge(x1_out, 16 * ST)
                    act.activation(oT_hi[:, bass.ds(o_slot(t, part), 1), :].rearrange("p a s -> p (a s)"),
                                   (res_b if part == "B" else w.g)[:, :], ACT.Copy).then_inc(o_hi_s, 1)
                elif what[:5] == "lstat":
                    j = int(what[5:])
                    wait(act, l_stat, j - 1)
                    block_out(act, j % 4, "prep", j // 4)
                    act.activation(lsq[:, j % 2, :], lat_raw[:, j, :], ACT.Square).then_inc(l_sq, 1)
                elif what[:5] == "lnorm":
                    j = int(what[5:])
                    act.wait_ge(l_mul, j + 1)
                    act.activation(lat_hi[:, j, :], lat_tmp[:, :], ACT.Copy).then_inc(l_hi, 1)

            def evac(part, i):
                w = work_of(part)

                def done(b):
                    block_done(act, b, part, i)
                if part in ("A", "C"):
                    t = i if part == "A" else 2 * H + i
                    done(0)
                    if part == "A" and isinstance(i, int):
                        act.wait_ge(t_done, KT)
                    wait(act, scored, s_before(t, part))
                    act.activation(w.q_hi[:, :], bank[0][:, :], ACT.Copy).then_inc(q_hi_s, 1)
                    done(1)
                    act.activation(w.k_hi[:, :], bank[1][:, :], ACT.Copy).then_inc(k_hi_s, 1)
                    done(2)
                    if part == "A":
                        wait(act, a_stat, t)
                    wait(act, v_turned, t)
                    act.activation(w.vT[:, :], bank[2][:, :], ACT.Copy).then_inc(bank_free[2], 1)
                    done(3)
                    if part == "A":
                        wait(act, a_spread, t)
                    act.activation(w.th[:, :], bank[3][:, :], ACT.Tanh, scale=0.5).then_inc(th_made, 1)
                elif part == "prep" and i < 3:
                    if i == 0:
                        act.wait_ge(o_lo_s, H)
                    for b in range(4 if i < 2 else 2):
                        done(b)
                        act.activation(lat_raw[:, 4 * i + b, :], bank[b][:, :], ACT.Copy
                                       ).then_inc(bank_free[b], 1)
                    if i == 2:
                        done(2)
                        act.activation(krt[:, 0, :], bank[2][0:ROPE_D, :], ACT.Copy).then_inc(bank_free[2], 1)
                elif part == "prep":
                    for b in range(4):
                        done(b)
                        if b:
                            block_out(act, b - 1, "prep", i)
                        elif i > 3:
                            block_out(act, 3, "prep", i - 1)
                        act.activation(th_b[:, :], bank[b][:, :], ACT.Tanh, scale=0.5).then_inc(th_made, 1)
                elif part == "B":
                    done(0)
                    act.activation(w.k_hi[:, :], bank[0][:, :], ACT.Copy).then_inc(k_hi_s, 1)
                    done(1)
                    act.activation(w.vT[:, :], bank[1][:, :], ACT.Copy).then_inc(bank_free[1], 1)
                elif part == "D":
                    t = 3 * H + i
                    b = q_bank(i)
                    done(b)
                    act.wait_ge(exped, s_before(t, part))
                    wait(act, p_turned, 4 * t)
                    act.activation(w.rq[:, :], bank[b][:, :], ACT.Copy, scale=gq_gain).then_inc(r_in, 1)
                    act.activation(w.p[:, 0, :], bank[b][:, :], ACT.Square).then_inc(bank_free[b], 1)
                    done(b + 1)
                    act.activation(w.th[:, :], bank[b + 1][:, :], ACT.Tanh, scale=0.5).then_inc(th_made, 1)
                    if i % 4 == 0:
                        done(2)
                        act.activation(w.rk[:, :], bank[2][:, :], ACT.Copy, scale=gk_gain).then_inc(kr_in, 1)
                        act.activation(w.p[:, 1, :], bank[2][:, :], ACT.Square
                                       ).then_inc(bank_free[2], 1)
                        done(3)
                        act.activation(w.vT[:, :], bank[3][:, :], ACT.Copy).then_inc(bank_free[3], 1)
                else:
                    layer = 0 if part == "out0" else 1
                    for b in range(ST):
                        if b:
                            block_out(act, b - 1, part, i)
                        elif not i_is_zero(i):
                            block_out(act, 3, part, i - 1)
                        act.wait_ge(m_copied, 16 * layer + 4 * i + b + 1)
                        act.activation(squares[:, :], bank[b][:, :], ACT.Square,
                                       accum_out=rowsq[:, bass.ds(i + 4 * b, 1)]
                                       ).then_inc(bank_free[b], 1)

            def queries_out(i):
                w, t = w_b, H + i
                block_done(act, 3, "B", i)
                if isinstance(i, int):
                    act.wait_ge(w_used, U_B)
                act.wait_ge(scored, s_before(t, "B"))
                act.activation(w.rq[0:ROPE_D, :], bank[3][0:ROPE_D, :], ACT.Copy).then_inc(bank_free[3], 1)
                block_done(act, 2, "B", i)
                act.activation(w.q_hi[:, :], bank[2][:, :], ACT.Copy).then_inc(q_hi_s, 1)
                if isinstance(i, int):
                    act.wait_ge(kr_sum, 1)
                    act.activation(kpe_hi[:, :], krt[:, 3, :], ACT.Copy).then_inc(kpe_hi_s, 1)

            def chunk(part, i, woven, att, t):
                first, turn_units, turn = units_of(part, i)
                late = part == "D" and i % 4 > 0
                for s, (u, place_in, _, _) in enumerate(ktiles(part, i)):
                    if place_in == 0 and not late:
                        split(first, turn_units, turn, u + AHEAD)
                    for what in WOVEN[woven].get(s, []):
                        if what == "own q":
                            queries_out(i)
                        elif what == "own rot":
                            item("rot", "B", H + i)
                        else:
                            item(what, att, t)
                    if place_in == 0 and late:
                        split(first, turn_units, turn, u + AHEAD)
                evac(part, i)
                for what in WOVEN[woven].get("end", []):
                    item(what, att, t)

            act.wait_ge(lam_dot, 2)
            act.activation(lam[:, 2:4], lam[:, 0:2], ACT.Exp).then_inc(lam_exp, 1)
            rows_norm(0)
            split(U_A, KT, 0, 0)
            split(U_A, KT, 0, 1)
            turn_hi(0)
            chunk("A", 0, "table", None, None)
            with act.Fori(1, H) as i:
                chunk("A", i, "A", "A", i - 1)
            chunk("prep", 0, "A", "A", H - 1)
            chunk("prep", 1, None, None, None)
            chunk("prep", 2, None, None, None)
            chunk("prep", 3, "lstat", None, None)
            chunk("prep", 4, "lnorm", None, None)
            chunk("B", 0, "Bfirst", None, None)
            with act.Fori(1, H) as i:
                chunk("B", i, "B", "B", i + (H - 1))
            chunk("out0", 0, "C", "B", 2 * H - 1)
            with act.Fori(1, 4) as c:
                chunk("out0", c, None, None, None)
            rows_norm(1)
            turn_hi(1)
            chunk("C", 0, None, None, None)
            with act.Fori(1, H - 1) as i:
                chunk("C", i, "C", "C", i + (2 * H - 1))
            chunk("C", H - 1, "C", "C", 3 * H - 2)
            for n in range(H):
                chunk("D", n, "C" if n == 0 else "Dkv" if n % 4 == 1 else "D", "D" if n else "C", 3 * H - 1 + n)
            chunk("out1", 0, "D", "D", 4 * H - 1)
            with act.Fori(1, 3) as c:
                chunk("out1", c, None, None, None)
            chunk("out1", 3, None, None, None)
            for t in range(ST):
                act.wait_ge(x_made, ST + t + 1)
                act.dma_start(out[0, t * P:(t + 1) * P, :], xrow[:, t, :]).then_inc(out_out, 16)
            act.wait_ge(out_out, 16 * ST)

        @block.vector
        def _(dve):
            def split(first, turn_units, i, s):
                n, like = unit_of(first, turn_units, i, s)
                if isinstance(n, int) and n >= U_END:
                    return
                slot, width = s % RING, unit_width(like)
                dve.wait_ge(hi_made, n + 1)
                wait(dve, w_used, n - RING + 1)
                dve.tensor_tensor(w_lo[:, slot, 0:width], raw[:, slot, 0:width],
                                  w_hi[:, slot, 0:width].bitcast(F32), ALU.subtract).then_inc(lo_made, 1)

            def rest(dst, src, hi):
                return dve.tensor_tensor(dst, src, hi.bitcast(F32), ALU.subtract)

            def normed_rows(layer):
                for t in range(ST):
                    n = layer * ST + t + 1
                    dve.wait_ge(x_pow, n)
                    dve.tensor_scalar(hrow[:, t, :], xrow[:, t, :], prestd[:, t:t + 1], None, ALU.mult
                                      ).then_inc(h_made, 1)

            def turn_lo(layer):
                for k in range(KT):
                    n = layer * KT + k
                    dve.wait_ge(xt_hi, n + 1)
                    dve.scalar_tensor_tensor(xT_lo[:, k, :], bank[4 + k % 4][:, :], pre_gain[:, n:n + 1],
                                             xT_hi[:, k, :].bitcast(F32), ALU.mult, ALU.subtract).then_inc(xt_lo, 1)

            def new_rows(layer):
                for b in range(ST):
                    block_out(dve, b, "out0" if layer == 0 else "out1", 3)
                dve.tensor_reduce(rowvar, rowsq.rearrange("p (t c) -> p t c", t=ST), AX.X, ALU.add
                                  ).then_inc(m_total, 1)
                dve.wait_ge(m_pow, layer + 1)
                dve.wait_ge(gain_in, 16 * (layer + 1))
                dve.wait_ge(resid_in, 16 * (layer + 1))
                for t in range(ST):
                    n = layer * ST + t + 1
                    dve.scalar_tensor_tensor(mrow[:, t, :], mrow[:, t, :], rowstd[:, t:t + 1], post_gain[:, :],
                                             ALU.mult, ALU.mult).then_inc(m_scaled, 1)
                    dve.wait_ge(m_scaled, n)
                    dve.tensor_tensor(xrow[:, t, :], mrow[:, t, :], resid[:, t, :], ALU.add).then_inc(x_made, 1)

            def normalise(w, t, j, n):
                dve.wait_ge(exped, n)
                dve.reciprocal(rsum[:, j:j + 1], esum[:, j:j + 1]).then_inc(recip_s, 1)
                dve.wait_ge(recip_s, 4 * t + j + 1)
                dve.tensor_scalar(w.p[:, j, :], w.p[:, j, :], rsum[:, j:j + 1], None, ALU.mult).then_inc(p_made, 1)

            def mix(w, t, j, n):
                dve.wait_ge(exped, n)
                dve.reciprocal(rsum.rearrange("p (m j) -> p m j", m=2)[:, :, j],
                               esum.rearrange("p (m j) -> p m j", m=2)[:, :, j]).then_inc(recip_s, 1)
                dve.wait_ge(recip_s, 4 * t + j + 1)
                dve.scalar_tensor_tensor(mixc[:, j:j + 1], esum[:, j:j + 1], neglam, rsum[:, ST + j:ST + j + 1],
                                         ALU.mult, ALU.mult).then_inc(mixc_s, 1)
                dve.wait_ge(mixc_s, 4 * t + j + 1)
                dve.scalar_tensor_tensor(w.p[:, j, :], w.e[:, 1, :], mixc[:, j:j + 1], w.e[:, 0, :],
                                         ALU.mult, ALU.add).then_inc(p_made, 1)

            def item(what, part, t):
                w = work_of(part)
                if what == "v":
                    dve.wait_ge(v_hi_s, kv_of(t, part) + 1)
                    rest(w.v_lo[:, :, :], tb[:, :].rearrange("p (a b) -> p a b", a=ST), w.v_hi[:, :, :]
                         ).then_inc(v_lo_s, 1)
                elif what[0] == "s" and what[1:].isdigit():
                    j = int(what[1:])
                    n = s_before(t, part) + j
                    if part == "A" and j >= 2 and j % 2 == 0:
                        mix(w, t, j // 2 - 1, n)
                    if part == "C" and j >= 1:
                        normalise(w, t, j - 1, n)
                    if part in ("A", "C"):
                        if j == 0:
                            dve.wait_ge(bias_in, 16 * (t + 1) if part == "A" else 16 * (t - (H - 1)))
                        if j >= 2:
                            dve.wait_ge(exped, n - 1)
                        wait_apart(dve, scored, n + 1)
                        tile = j // 2 if part == "A" else j
                        if part == "A":
                            table = bias[:, (ST - 1 - tile) * P:(ST - 1 - tile) * P + SEQ]
                        else:
                            table = bias[:, (ROWS - 2 - 2 * tile) * GRID_W:(ROWS - 2 - 2 * tile) * GRID_W + SEQ]
                        dve.tensor_tensor_reduce(w.sb[:, j % 2, :], bank[B_S[j % 2]][:, :], table,
                                                 -(SCALE_A if part == "A" else SCALE_CD), 3e38, ALU.add, ALU.min,
                                                 nmax[:, j:j + 1]).then_inc(s_read, 1)
                    else:
                        dve.wait_ge(scored, n + 1)
                        dve.tensor_reduce(nm[:, j:j + 1], bank[B_S[j % 2]][:, :], AX.X, ALU.max, negate=True
                                          ).then_inc(s_read, 1)
                        dve.wait_ge(s_read, n + 1)
                        if part == "D":
                            dve.wait_ge(d_pow, 3 * (t - 3 * H) + 3)
                        dve.tensor_scalar(nmax[:, j:j + 1], nm[:, j:j + 1],
                                          SCALE_B if part == "B" else rscale[:, j:j + 1], None, ALU.mult
                                          ).then_inc(nmaxed, 1)
                        if j >= 1:
                            normalise(w, t, j - 1, n)
                    if part == "A" and j == 7:
                        mix(w, t, 3, n + 1)
                    if part != "A" and j == 3:
                        normalise(w, t, 3, n + 1)
                elif what[:2] == "pt":
                    j = int(what[2:])
                    dve.wait_ge(pT_hi_s, 4 * t + j + 1)
                    if j >= 2:
                        dve.wait_ge(pv_done, 4 * t + j - 1)
                    rest(w.pT_lo[:, j % 2, :], turned(j)[:, :], w.pT_hi[:, j % 2, :]).then_inc(pT_lo_s, 1)
                elif what == "stat" and part == "A":
                    dve.wait_ge(a_stat, t + 1)
                    dve.tensor_tensor(var2[:, ST:2 * ST], tb[:, 0:ST], rsum[:, 0:ST], ALU.mult).then_inc(a_var, 1)
                    dve.wait_ge(a_var, 2 * t + 1)
                    dve.tensor_tensor(var[:, 0:ST], var2[:, ST:2 * ST], rsum[:, 0:ST], ALU.mult).then_inc(a_var, 1)
                elif what == "stat":
                    dve.wait_ge(d_stat, t - 3 * H + 1)
                    dve.tensor_copy(var[:, 0:ST], tb[:, 0:ST]).then_inc(d_var, 1)
                elif what == "kstat":
                    dve.wait_ge(k_stat, (t - 3 * H) // 4 + 1)
                    dve.tensor_copy(var[:, ST:2 * ST], tb[:, 0:ST]).then_inc(k_var, 1)
                elif what == "rot":
                    n = rot_of(t, part)
                    rows = ROPE_D if part == "B" else P
                    dve.wait_ge(r_rot, n + 1)
                    dve.wait_ge(rope_in, 16 if part == "B" else 32)
                    dve.tensor_tensor(w.rq_sin[0:rows, :], rb[0:rows, :], rope[0:rows, 1, :], ALU.mult
                                      ).then_inc(r_sin, 1)
                    if part == "B":
                        dve.wait_ge(pe_hi_s, n + 1)
                        rest(pe_lo[:, :], w.rk_sin[0:rows, :], pe_hi[:, :]).then_inc(pe_lo_s, 1)
                    else:
                        dve.wait_ge(q_hi_s, t + 1)
                        rest(w.q_lo[:, :], w.rq[:, :], w.q_hi[:, :]).then_inc(q_lo_s, 1)
                elif what == "krot":
                    dve.wait_ge(kr_rot, (t - 3 * H) // 4 + 2)
                    dve.wait_ge(rope_in, 32)
                    dve.tensor_tensor(w.rk_sin[:, :], krb[:, :], rope[:, 1, :], ALU.mult).then_inc(kr_sin, 1)
                elif what == "kspread":
                    g = (t - 3 * H) // 4
                    dve.wait_ge(k_spread, g + 1)
                    dve.wait_ge(kr_sum, g + 2)
                    dve.tensor_tensor(w.rk_sin[:, :], w.rk[:, :], tb[:, :], ALU.mult).then_inc(k_scaled, 1)
                    dve.wait_ge(k_hi_s, kv_of(t, part) + 1)
                    rest(w.k_lo[:, :], w.rk_sin[:, :], w.k_hi[:, :]).then_inc(k_lo_s, 1)
                elif what == "gate":
                    dve.wait_ge(pv_done, 4 * t + 4)
                    gate_out(dve, t, part)
                    slot = bass.ds(o_slot(t, part), 1)
                    if part == "A":
                        dve.scalar_tensor_tensor(w.g[:, :], ob[:, :], gate_gain, w.g[:, :], ALU.mult, ALU.mult
                                                 ).then_inc(o_read, 1)
                        dve.wait_ge(o_read, t + 1)
                        dve.wait_ge(a_spread, t + 1)
                        dve.tensor_tensor(w.g[:, :], w.g[:, :], tb[:, :], ALU.mult).then_inc(o_gated, 1)
                        dve.wait_ge(tables_out, 16)
                        src = w.g
                    elif part == "B":
                        dve.wait_ge(o_lo_s, t)
                        gate = gates_b[:, bass.ds(t - H, 1), :].rearrange("p a s -> p (a s)")
                        dve.scalar_tensor_tensor(res_b[:, :], ob[:, :], 0.5, gate, ALU.mult, ALU.mult
                                                 ).then_inc(o_gated, 1)
                        src = res_b
                    else:
                        dve.scalar_tensor_tensor(w.g[:, :], ob[:, :], 0.5, w.g[:, :], ALU.mult, ALU.mult
                                                 ).then_inc(o_gated, 1)
                        src = w.g
                    dve.wait_ge(o_hi_s, t + 1)
                    rest(oT_lo[:, slot, :].rearrange("p a s -> p (a s)"), src[:, :],
                         oT_hi[:, slot, :].rearrange("p a s -> p (a s)")).then_inc(o_lo_s, 1)
                elif what[:3] == "tab":
                    s = int(what[3:])
                    if s == 0:
                        dve.wait_ge(xt_turned, KT)
                    dve.wait_ge(t_done, s + 1)
                    dst = table_all[:, :, :, 4 * s:4 * s + 4].rearrange("p h j c -> p (h j) c")
                    seen = mask[:, 4 * s:4 * s + 4].rearrange("p (a c) -> p a c", a=1).to_broadcast(
                        [P, H * (DR - 1), 4])
                    cols = bank[B_S[s % 2]][:, 0:4 * H * (DR - 1)].rearrange("p (c n) -> p n c", c=4)
                    dve.tensor_tensor(dst, cols, seen, ALU.add).then_inc(t_evac, 1)
                elif what == "krope":
                    dve.wait_ge(kr_rot, 1)
                    dve.wait_ge(rope_in, 16)
                    dve.tensor_tensor(krt[:, 2, :], tb[0:ROPE_D, :], rope[0:ROPE_D, 1, :], ALU.mult
                                      ).then_inc(kr_sin, 1)
                elif what[:5] == "lstat":
                    if int(what[5:]) == QB + KVB - 1:
                        dve.wait_ge(l_stat, QB + KVB)
                        dve.tensor_copy(var[:, 0:2 * ST], tb[:, 0:2 * ST]).then_inc(l_var, 1)
                elif what[:5] == "lnorm":
                    j = int(what[5:])
                    dve.wait_ge(l_spread, 1 if j < QB else 2)
                    wait(dve, l_lo, j)
                    dve.scalar_tensor_tensor(lat_tmp[:, :], lat_raw[:, j, :], lat_gain[:, j:j + 1], tb[:, :],
                                             ALU.mult, ALU.mult).then_inc(l_mul, 1)
                    dve.wait_ge(l_hi, j + 1)
                    rest(lat_lo[:, j, :], lat_tmp[:, :], lat_hi[:, j, :]).then_inc(l_lo, 1)

            def gate_of(dst, th, src, n):
                dve.wait_ge(th_made, n)
                return dve.scalar_tensor_tensor(dst, th, 1.0, src, ALU.add, ALU.mult)

            def evac(part, i):
                w = work_of(part)
                if part in ("A", "C"):
                    t = i if part == "A" else 2 * H + i
                    dve.wait_ge(q_hi_s, t + 1)
                    rest(w.q_lo[:, :], bank[0][:, :], w.q_hi[:, :]).then_inc(bank_free[0], 1)
                    dve.wait_ge(k_hi_s, t + 1)
                    rest(w.k_lo[:, :], bank[1][:, :], w.k_hi[:, :]).then_inc(bank_free[1], 1)
                    wait(dve, o_lo_s, t)
                    gate_of(w.g[:, :], w.th[:, :], bank[3][:, :], t + 1).then_inc(bank_free[3], 1)
                elif part == "prep" and i >= 3:
                    for b in range(4):
                        h = 4 * (i - 3) + b
                        gate_of(gates_b[:, h, :], th_b[:, :], bank[b][:, :], H + h + 1
                                ).then_inc(bank_free[b], 1)
                elif part == "B":
                    t = H + i
                    dve.wait_ge(k_hi_s, t + 1)
                    rest(w.k_lo[:, :], bank[0][:, :], w.k_hi[:, :]).then_inc(bank_free[0], 1)
                elif part == "D":
                    t = 3 * H + i
                    dve.wait_ge(o_lo_s, t)
                    b = q_bank(i) + 1
                    gate_of(w.g[:, :], w.th[:, :], bank[b][:, :], t + 1).then_inc(bank_free[b], 1)
                elif part in ("out0", "out1"):
                    layer = 0 if part == "out0" else 1
                    for b in range(ST):
                        block_done(dve, b, part, i)
                        dve.tensor_copy(mrow[:, b, bass.ds(i * 512, 512)], bank[b][:, :]).then_inc(m_copied, 1)

            def queries_out(i):
                dve.wait_ge(q_hi_s, H + i + 1)
                rest(w_b.q_lo[:, :], bank[2][:, :], w_b.q_hi[:, :]).then_inc(bank_free[2], 1)
                if isinstance(i, int):
                    dve.wait_ge(kpe_hi_s, 1)
                    rest(kpe_lo[:, :], krt[:, 3, :], kpe_hi[:, :]).then_inc(kpe_lo_s, 1)

            def chunk(part, i, woven, att, t):
                first, turn_units, turn = units_of(part, i)
                late = part == "D" and i % 4 > 0
                for s, (u, place_in, _, _) in enumerate(ktiles(part, i)):
                    if place_in == 0 and not late:
                        split(first, turn_units, turn, u + AHEAD)
                    for what in WOVEN[woven].get(s, []):
                        if what == "own q":
                            queries_out(i)
                        elif what == "own rot":
                            item("rot", "B", H + i)
                        else:
                            item(what, att, t)
                    if place_in == 0 and late:
                        split(first, turn_units, turn, u + AHEAD)
                evac(part, i)
                for what in WOVEN[woven].get("end", []):
                    item(what, att, t)

            dve.wait_ge(lam_in, 64)
            for j in range(2):
                dve.tensor_tensor_reduce(lamp[:, j, :], lamv[:, 2 * j, :], lamv[:, 2 * j + 1, :], 1.0, 0.0, ALU.mult,
                                         ALU.add, lam[:, j:j + 1]).then_inc(lam_dot, 1)
            dve.wait_ge(consts_in, 160)
            dve.tensor_scalar(gate_gain, sub_gain, 0.5 * (1.0 - LAMBDA_INIT), None, ALU.mult).then_inc(lam_sum, 1)
            dve.wait_ge(lam_exp, 1)
            dve.tensor_tensor(lam[:, 0:1], lam[:, 3:4], lam[:, 2:3], ALU.subtract).then_inc(lam_sum, 1)
            dve.wait_ge(lam_sum, 2)
            dve.tensor_scalar(neglam, lam[:, 0:1], -LAMBDA_INIT, None, ALU.add).then_inc(lam_sum, 1)
            dve.wait_ge(lam_sum, 3)
            dve.wait_ge(rpb_turned, 1)
            dve.tensor_copy(rpbT[:, :, :].rearrange("p h r -> p (h r)"), tb[0:DC, 0:H * DR]).then_inc(rpb_copied, 1)
            normed_rows(0)
            split(U_A, KT, 0, 0)
            split(U_A, KT, 0, 1)
            turn_lo(0)
            chunk("A", 0, "table", None, None)
            with dve.Fori(1, H) as i:
                chunk("A", i, "A", "A", i - 1)
            chunk("prep", 0, "A", "A", H - 1)
            chunk("prep", 1, None, None, None)
            chunk("prep", 2, None, None, None)
            chunk("prep", 3, "lstat", None, None)
            chunk("prep", 4, "lnorm", None, None)
            chunk("B", 0, "Bfirst", None, None)
            with dve.Fori(1, H) as i:
                chunk("B", i, "B", "B", i + (H - 1))
            chunk("out0", 0, "C", "B", 2 * H - 1)
            with dve.Fori(1, 4) as c:
                chunk("out0", c, None, None, None)
            new_rows(0)
            normed_rows(1)
            turn_lo(1)
            chunk("C", 0, None, None, None)
            with dve.Fori(1, H) as i:
                chunk("C", i, "C", "C", i + (2 * H - 1))
            for n in range(H):
                chunk("D", n, "C" if n == 0 else "Dkv" if n % 4 == 1 else "D", "D" if n else "C", 3 * H - 1 + n)
            chunk("out1", 0, "D", "D", 4 * H - 1)
            with dve.Fori(1, 3) as c:
                chunk("out1", c, None, None, None)
            chunk("out1", 3, None, None, None)
            new_rows(1)

        @block.tensor
        def _(pe):
            def three(dst, l_hi_, l_lo_, r_hi_, r_lo_, start, stop):
                pe.matmul(dst, l_hi_, r_hi_, start=start, stop=False)
                pe.matmul(dst, l_hi_, r_lo_, start=False, stop=False)
                return pe.matmul(dst, l_lo_, r_hi_, start=False, stop=stop)

            def turn_rows(layer):
                pe.wait_ge(h_made, ST * (layer + 1))
                for k in range(KT):
                    n = layer * KT + k
                    if k >= 4:
                        pe.wait_ge(xt_lo, n - 3)
                    for t in range(ST):
                        mm = pe.transpose(bank[4 + k % 4][:, t * P:(t + 1) * P], hrow[:, t, k * P:(k + 1) * P], ident)
                    mm.then_inc(xt_turned, 1)

            def spread(diag, done):
                for j in range(ST):
                    mm = pe.matmul(tb[:, j * P:(j + 1) * P], ones[:, :], diag[:, j, :], start=True, stop=True)
                mm.then_inc(done, 1)

            def sum_partitions(squares_, done):
                for j in range(ST):
                    mm = pe.matmul(tb[:, j:j + 1], squares_[:, j * P:(j + 1) * P], ones[:, 0:1], start=True, stop=True)
                mm.then_inc(done, 1)

            def tb_free(what, part, t):
                if part == "A":
                    if what == "pt0":
                        pe.wait_ge(v_lo_s, t + 1)
                    elif what == "stat":
                        pe.wait_ge(pT_lo_s, 4 * t + 4)
                    elif what == "spread":
                        pe.wait_ge(a_var, 2 * t + 1)
                elif part == "C":
                    if what == "v":
                        pe.wait_ge(pT_lo_s, 4 * t)
                    elif what == "pt0":
                        pe.wait_ge(v_lo_s, t + 1)
                elif part == "B":
                    if what == "v":
                        pe.wait_ge(pT_lo_s, 4 * t)
                        pe.wait_ge(l_mul, QB + KVB)
                    elif what == "rot":
                        pe.wait_ge(exped, s_before(t, part))
                    elif what == "pt0":
                        pe.wait_ge(v_lo_s, t + 1)
                else:
                    n, g = t - 3 * H, (t - 3 * H) // 4
                    if what in ("krot", "kstat") or (what == "stat" and n % 4):
                        pe.wait_ge(pT_lo_s, 4 * t)
                    elif what == "stat":
                        pe.wait_ge(k_var, g + 1)
                    elif what == "rot":
                        pe.wait_ge(exped, s_before(t, part))
                    elif what == "kspread":
                        pe.wait_ge(d_var, n + 1)
                    elif what == "v":
                        pe.wait_ge(k_scaled, g + 1)
                    elif what == "pt0":
                        pe.wait_ge(v_lo_s if n % 4 == 0 else d_var, kv_of(t, part) + 1 if n % 4 == 0 else n + 1)

            def item(what, part, t):
                w = work_of(part)
                if part is not None:
                    tb_free(what, part, t)
                if what == "v":
                    c = chunk_of(t, part)
                    block_out(pe, {"A": 2, "B": 1, "C": 2, "D": 3}[part], part, c // 4 * 4 if part == "D" else c)
                    for j in range(ST):
                        mm = pe.transpose(tb[:, j * P:(j + 1) * P], w.vT[:, j * P:(j + 1) * P], ident)
                    mm.then_inc(v_turned, 1)
                elif what[0] == "s" and what[1:].isdigit():
                    j = int(what[1:])
                    n = s_before(t, part) + j
                    dst = bank[B_S[j % 2]][:, :]
                    if j == 0:
                        if part == "D":
                            pe.wait_ge(q_lo_s, t - 3 * H + 1)
                            pe.wait_ge(k_lo_s, (t - 3 * H) // 4 + 1)
                        else:
                            block_out(pe, 2 if part == "B" else 0, part, chunk_of(t, part))
                            block_out(pe, 0 if part == "B" else 1, part, chunk_of(t, part))
                        if part == "B":
                            pe.wait_ge(pe_lo_s, t - H + 1)
                            pe.wait_ge(kpe_lo_s, 1)
                        if part == "A":
                            pe.wait_ge(t_evac, KT)
                    if j >= 2:
                        pe.wait_ge(s_read if part in ("A", "C") else exped, n - 1)
                    if part == "A":
                        rows = slice(64 * (j % 2), 64 * (j % 2) + 64)
                        cols = slice(j // 2 * P, j // 2 * P + P)
                        mm = three(dst, w.q_hi[rows, cols], w.q_lo[rows, cols], w.k_hi[rows, :], w.k_lo[rows, :],
                                   True, True)
                    else:
                        cols = slice(j * P, j * P + P)
                        mm = three(dst, w.q_hi[:, cols], w.q_lo[:, cols], w.k_hi[:, :], w.k_lo[:, :],
                                   True, part != "B")
                        if part == "B":
                            mm = three(dst, pe_hi[:, cols], pe_lo[:, cols], kpe_hi[:, :], kpe_lo[:, :], False, True)
                    mm.then_inc(scored, 1)
                elif what[:2] == "pt":
                    j = int(what[2:])
                    if j == 0:
                        pe.wait_ge(p_made, 4 * t + 4)
                    elif j >= 2:
                        pe.wait_ge(pT_lo_s, 4 * t + j - 1)
                    for q in range(ST):
                        mm = pe.transpose(turned(j)[:, q * P:(q + 1) * P], w.p[:, q, j * P:(j + 1) * P], ident)
                    mm.then_inc(p_turned, 1)
                elif what[:2] == "pv":
                    j = int(what[2:])
                    pe.wait_ge(pT_lo_s, 4 * t + j + 1)
                    if j == 0:
                        if part != "A":
                            pe.wait_ge(o_gated, t)
                        pe.wait_ge(v_lo_s, kv_of(t, part) + 1)
                    three(ob[:, :], w.v_hi[:, j, :], w.v_lo[:, j, :], w.pT_hi[:, j % 2, :], w.pT_lo[:, j % 2, :],
                          j == 0, j == ST - 1).then_inc(pv_done, 1)
                elif what == "stat" and part == "A":
                    pe.wait_ge(o_sq, t + 1)
                    sum_partitions(w.vT, a_stat)
                elif what == "spread":
                    pe.wait_ge(a_diag, 4 * t + 4)
                    spread(w.diag, a_spread)
                elif what == "rot":
                    if part == "B":
                        block_out(pe, 3, part, chunk_of(t, part))
                    else:
                        pe.wait_ge(r_in, t - 3 * H + 1)
                    rows = ROPE_D if part == "B" else P
                    pe.matmul(rb[:, :], rotT[0:rows, :], w.rq[0:rows, :], start=True, stop=True
                              ).then_inc(r_rot, 1)
                elif what == "stat":
                    block_out(pe, q_bank(t - 3 * H), part, t - 3 * H)
                    sum_partitions(w.p[:, 0, :], d_stat)
                elif what == "krot":
                    pe.wait_ge(kr_in, (t - 3 * H) // 4 + 1)
                    pe.matmul(krb[:, :], rotT, w.rk[:, :], start=True, stop=True).then_inc(kr_rot, 1)
                elif what == "kstat":
                    block_out(pe, 2, part, t - 3 * H)
                    sum_partitions(w.p[:, 1, :], k_stat)
                elif what == "kspread":
                    pe.wait_ge(k_diag, 4 * ((t - 3 * H) // 4) + 4)
                    spread(w.diag, k_spread)
                elif what[:3] == "tab":
                    s = int(what[3:])
                    if s == 0:
                        pe.wait_ge(rpb_copied, 1)
                        pe.wait_ge(xt_lo, KT)
                    if s >= 2:
                        pe.wait_ge(t_evac, s - 1)
                    n = H * (DR - 1)
                    for c in range(4):
                        col = 4 * s + c
                        pick = shift[0:DC, GRID_W - 1 - col:2 * GRID_W - 1 - col]
                        for half in range(2):
                            mm = pe.matmul(bank[B_S[s % 2]][half * GRID_W:(half + 1) * GRID_W, c * n:(c + 1) * n],
                                           pick, rpbT[:, :, 1 - half:DR - half], start=True, stop=True)
                    mm.then_inc(t_done, 1)
                elif what == "krope":
                    pe.wait_ge(o_gated, H)
                    block_out(pe, 2, "prep", 2)
                    pe.matmul(tb[0:ROPE_D, :], rotT[0:ROPE_D, 0:ROPE_D], krt[:, 0, :], start=True, stop=True
                              ).then_inc(kr_rot, 1)
                elif what[:5] == "lstat":
                    j = int(what[5:])
                    if j == 0:
                        pe.wait_ge(kr_sin, 1)
                    pe.wait_ge(l_sq, j + 1)
                    col = 0 if j < QB else ST
                    for q in range(ST):
                        mm = pe.matmul(tb[:, col + q:col + q + 1], lsq[:, j % 2, q * P:(q + 1) * P], ones[:, 0:1],
                                       start=(j == 0 and q == 0), stop=(j in (QB - 1, QB + KVB - 1)),
                                       skip_group_check=True)
                    mm.then_inc(l_stat, 1)
                elif what == "lspreadq":
                    pe.wait_ge(l_var, 1)
                    pe.wait_ge(l_diag, 4)
                    spread(ldiag, l_spread)
                elif what == "lspreadk":
                    pe.wait_ge(l_mul, QB)
                    pe.wait_ge(l_diag, 8)
                    spread(ldiag, l_spread)

            def chunk(part, i, woven, att, t):
                first, turn_units, turn = units_of(part, i)
                for s, (u, place_in, places, blocks) in enumerate(ktiles(part, i)):
                    slot = u % RING
                    if place_in == 0:
                        pe.wait_ge(lo_made, first + turn * turn_units + u + 1)
                    if part in ("out0", "out1"):
                        if i_is_zero(i) and s in (0, KT - 1):
                            pe.wait_ge(o_lo_s, (0 if part == "out0" else 2 * H) + (KT - 1 if s == 0 else KT))
                    elif part in ("A", "C") and i_is_zero(i):
                        pe.wait_ge(xt_lo, (0 if part == "A" else KT) + s + 1)
                    elif part == "B" and i_is_zero(i) and s == 0:
                        pe.wait_ge(l_lo, QB + KVB)
                    for n, (b, c0, width, opens, closes, k) in enumerate(blocks):
                        if opens:
                            wait(pe, bank_free[b], use_of(b, part, i))
                        if part in ("out0", "out1"):
                            rows = slice(b * P, (b + 1) * P)
                            mm = three(bank[b][:, :], oT_hi[:, k, rows], oT_lo[:, k, rows],
                                       w_hi[:, slot, 0:512], w_lo[:, slot, 0:512], opens, closes)
                        else:
                            x_hi, x_lo = (lat_hi, lat_lo) if part == "B" else (xT_hi, xT_lo)
                            mm = three(bank[b][0:width, :], w_hi[:, slot, c0:c0 + width], w_lo[:, slot, c0:c0 + width],
                                       x_hi[:, k, :], x_lo[:, k, :], opens, closes)
                        if closes and not (place_in == places - 1 and n == len(blocks) - 1):
                            mm.then_inc(proj[b], 1)
                    if place_in == places - 1:
                        mm.then_inc(w_used, 1)
                    for what in WOVEN[woven].get(s, []):
                        if what == "own rot":
                            item("rot", "B", H + i)
                        elif what != "own q":
                            item(what, att, t)

            pe.wait_ge(consts_in, 160)
            pe.wait_ge(ones_set, 2)
            pe.transpose(tb[0:DC, 0:H * DR], rpb_rows[:, :], ident[0:H * DR, 0:H * DR]).then_inc(rpb_turned, 1)
            pe.wait_ge(rpb_copied, 1)
            turn_rows(0)
            chunk("A", 0, "table", None, None)
            with pe.Fori(1, H) as i:
                chunk("A", i, "A", "A", i - 1)
            chunk("prep", 0, "A", "A", H - 1)
            chunk("prep", 1, None, None, None)
            chunk("prep", 2, None, None, None)
            chunk("prep", 3, "lstat", None, None)
            chunk("prep", 4, "lnorm", None, None)
            chunk("B", 0, "Bfirst", None, None)
            with pe.Fori(1, H) as i:
                chunk("B", i, "B", "B", i + (H - 1))
            chunk("out0", 0, "C", "B", 2 * H - 1)
            with pe.Fori(1, 4) as c:
                chunk("out0", c, None, None, None)
            turn_rows(1)
            chunk("C", 0, None, None, None)
            with pe.Fori(1, H) as i:
                chunk("C", i, "C", "C", i + (2 * H - 1))
            for n in range(H):
                chunk("D", n, "C" if n == 0 else "Dkv" if n % 4 == 1 else "D", "D" if n else "C", 3 * H - 1 + n)
            chunk("out1", 0, "D", "D", 4 * H - 1)
            with pe.Fori(1, 4) as c:
                chunk("out1", c, None, None, None)


_INS = ["x", "pre_norm", "post_norm", "even_w_in", "even_w_out", "diff_lambda_q1", "diff_lambda_k1",
        "diff_lambda_q2", "diff_lambda_k2", "diff_subln", "mla_q_norm", "mla_w_uq", "mla_kv_norm", "mla_w_ukv",
        "odd_w_in", "odd_w_out", "na_rpb", "gqa_q_norm", "gqa_k_norm"]


def constants():
    f = np.float32
    p = np.arange(P)
    slopes = 2.0 ** (-8.0 * np.arange(1, H + 1) / H)
    dist = np.abs(p[:, None] - (np.arange(CW)[None, :] - (ST - 1) * P))
    alibi = (-slopes[:, None, None] / SCALE_A * dist[None]).astype(f)
    rot = np.zeros((P, P), f)
    for b in range(0, P, 64):
        for d in range(32):
            rot[b + d, b + 32 + d] = -1.0
            rot[b + 32 + d, b + d] = 1.0
    c = np.arange(GRID_W)
    c0 = np.clip(c - NA_KW // 2, 0, GRID_W - NA_KW)
    seen = (c[None, :] >= c0[:, None]) & (c[None, :] < c0[:, None] + NA_KW)
    mask = np.where(seen, 0.0, NEG).astype(f)
    small = np.concatenate([np.eye(P, dtype=f), rot.T, np.concatenate([mask, mask])], axis=1)
    shift = np.zeros((32, 2 * GRID_W - 1), f)
    for m in range(DC):
        shift[m, GRID_W - 1 + NA_KW - 1 - m] = 1.0 / SCALE_CD
    tok = np.arange(SEQ)

    def angles(pos):
        inv = f(10000.0) ** (-np.arange(32, dtype=f) / f(32))
        a = pos.astype(f)[None, :] * inv[:, None]
        a = np.concatenate([a, a])
        return np.cos(a).astype(f), np.sin(a).astype(f)
    cb, sb = angles(tok)
    cr, sr = angles(tok // GRID_W)
    cc, sc = angles(tok % GRID_W)
    return {"c_alibi": alibi, "c_small": small, "c_shift": shift, "c_rope_b": np.stack([cb, sb]),
            "c_rope_d": np.stack([np.concatenate([cr, cc]), np.concatenate([sr, sc])])}


def kernel(**inputs):
    import concourse.bacc as bacc
    from concourse.bass_utils import run_bass_kernel_spmd

    nc = bacc.Bacc("TRN2", target_bir_lowering=False, num_devices=1)
    arrays = {name: np.ascontiguousarray(inputs[name]) for name in _INS}
    arrays.update(constants())
    args = [nc.dram_tensor(f"in_{n}", a.shape, F32, kind="ExternalInput").ap() for n, a in arrays.items()]
    args.append(nc.dram_tensor("x1_dram", (SEQ, DM), F32, kind="Internal").ap())
    args.append(nc.dram_tensor("tables_dram", (H, P, CW), F32, kind="Internal").ap())
    args.append(nc.dram_tensor("out_dram", (1, SEQ, DM), F32, kind="ExternalOutput").ap())
    build(nc, *args)
    r = run_bass_kernel_spmd(nc, [{f"in_{n}": a for n, a in arrays.items()}], core_ids=[0])
    return r.results[0]["out_dram"]
```

```python
import concourse.bass as bass
from concourse import mybir
from contextlib import ExitStack
import numpy as np

F32 = mybir.dt.float32
F32R = mybir.dt.float32r
ALU = mybir.AluOpType
ACT = mybir.ActivationFunctionType
AX = mybir.AxisListType

P = 128
SEQ = 512
DM = 2048
ST = SEQ // P
KT = DM // P
H = 8
GRID_W = 64
ROWS = SEQ // GRID_W
NA_KH, NA_KW = 8, 16
DR, DC = 2 * NA_KH - 1, 2 * NA_KW - 1
CW = (DR - 1) * GRID_W
Q_RANK, KV_RANK, ROPE_D = 768, 512, 64
QB, KVB = Q_RANK // P, KV_RANK // P
LAMBDA_INIT = 0.8 - 0.6
EPS = 1e-6
NEG = -1e30
SCALE_A = 64 ** -0.5
SCALE_B = 192 ** -0.5
SCALE_CD = 128 ** -0.5

RING = 4
EARLY_TABS = 7
AHEAD = 2
SLOT = 576

U_A = 0
U_PREP = U_A + H * KT
U_B = U_PREP + 5 * KT
U_OUT0 = U_B + H * 4
U_C = U_OUT0 + 4 * KT
U_D = U_C + H * KT
D_GROUP = KT + 3 * (KT // 2)
U_OUT1 = U_D + 2 * D_GROUP
U_END = U_OUT1 + 4 * KT

ORDER = ([("A", i) for i in range(H)] + [("prep", i) for i in range(5)] + [("B", i) for i in range(H)]
         + [("out0", i) for i in range(4)] + [("C", i) for i in range(H)] + [("D", i) for i in range(H)]
         + [("out1", i) for i in range(4)])


def count_before(test, part, i):
    if isinstance(i, int):
        return sum(test(*c) for c in ORDER[:ORDER.index((part, i))])
    return count_before(test, part, 0) + (i if test(part, 0) else 0)


def closing(bank, part, i):
    for u, place_in, places, blocks in ktiles(part, i):
        for b in blocks:
            if b[0] == bank and b[4]:
                return u, place_in == places - 1 and b is blocks[-1]
    return None


def use_of(bank, part, i):
    return count_before(lambda p, j: closing(bank, p, j) is not None, part, i)


def proj_of(bank, part, i):
    return count_before(lambda p, j: closing(bank, p, j) is not None and not closing(bank, p, j)[1], part, i)


def s_before(t, part):
    return 8 * t if part == "A" else 32 + 4 * t


def nmax_before(t, part):
    return 4 * (t - 8) if part == "B" else 4 * (t - 16)


def rot_of(t, part):
    return t - 8 if part == "B" else t - 16


def kv_of(t, part):
    return t if part != "D" else 24 + (t - 24) // 4


def units_of(part, i):
    if part == "D":
        return U_D + i // 4 * D_GROUP + (KT + (i % 4 - 1) * KT // 2 if i % 4 else 0), 0, 0
    return {"A": U_A, "prep": U_PREP, "B": U_B, "out0": U_OUT0, "C": U_C, "out1": U_OUT1}[part], \
        4 if part == "B" else KT, i


def i_is_zero(i):
    return isinstance(i, int) and i == 0


def raw_count(u):
    total = 0
    for v in range(u % RING, u + 1, RING):
        in_d = U_D <= v < U_OUT1
        total += (3 if (v - U_D) % D_GROUP < KT else 4) if in_d else 1
    return 16 * total


def wait(eng, sem, value):
    if isinstance(value, int) and value <= 0:
        return
    eng.wait_ge(sem, value)


def wait_apart(eng, sem, value):
    eng.wait_ge(sem, value)
    eng.nop(nofuse=True)


def q_bank(i):
    return 2 if i % 4 == 2 else 0


def gate_banks(i):
    return (2, 3, 0, 1) if i == 4 else (0, 1, 2, 3)


def ktiles(part, i):
    if part == "B":
        out = [(s // 3, s % 3, 3, [(2, s % 3 * 192, P, s == 0, s == QB - 1, s),
                                   (3, s % 3 * 192 + P, ROPE_D, s == 0, s == QB - 1, s)]) for s in range(QB)]
        out += [(2 + s // 2, s % 2, 2, [(0, s % 2 * 256, P, s == 0, s == KVB - 1, QB + s),
                                        (1, s % 2 * 256 + P, P, s == 0, s == KVB - 1, QB + s)]) for s in range(KVB)]
        return out
    if part == "D" and i % 4:
        return [(s // 2, s % 2, 2, [(q_bank(i) + b, s % 2 * 256 + b * P, P, s == 0, s == KT - 1, s)
                                    for b in range(2)]) for s in range(KT)]
    blocks = [(b, b * P, P) for b in range(4)]
    if part == "prep" and i == 2:
        blocks = [(0, 0, P), (1, P, P), (2, 2 * P, ROPE_D)]
    if part == "prep" and i == 4:
        blocks = blocks[2:] + blocks[:2]

    def some(s, chosen):
        return [(*b, s == 0, s == KT - 1, s) for b in chosen]
    out = [(s, 0, 1, some(s, blocks)) for s in range(KT)]
    if isinstance(i, int) and (part, i) in (("D", 4), ("out0", 0), ("out1", 0)):
        out[:2] = [(u, place_in, 2, some(u, blocks[2:] if place_in == 0 else blocks[:2]))
                   for place_in in range(2) for u in range(2)]
    return out


def unit_width(u):
    if U_PREP + 2 * KT <= u < U_PREP + 3 * KT:
        return 2 * P + ROPE_D
    if U_B <= u < U_OUT0 and (u - U_B) % 4 < 2:
        return SLOT
    return 512


WOVEN = {
    "A": {0: ["v"], 1: ["s0", "s1"], 2: ["s2", "s3"], 3: ["s4", "s5"], 4: ["s6", "s7"], 6: ["pt0", "pt1"],
          7: ["pv0", "pt2"], 8: ["pv1", "pt3"], 9: ["pv2"], 10: ["pv3"], 11: ["stat"], 13: ["spread"],
          14: ["gate"]},
    "C": {0: ["v"], 1: ["s0"], 2: ["s1"], 3: ["s2"], 4: ["s3"], 6: ["pt0", "pt1"],
          7: ["pv0", "pt2"], 8: ["pv1", "pt3"], 9: ["pv2"], 10: ["pv3"], 11: ["gate"]},
    "B": {0: ["v"], 1: ["s0"], 2: ["s1"], 3: ["s2"], 4: ["s3"], 6: ["own q", "pt0", "pt1"],
          7: ["own rot", "pv0", "pt2"], 8: ["pv1", "pt3"], 9: ["pv2", "pv3"], "end": ["gate"]},
    "Bfirst": {6: ["own q"], 7: ["own rot"]},
    "D": {1: ["rot"], 2: ["stat"], 4: ["rsum"], 5: ["s0"], 6: ["s1"], 7: ["s2"], 8: ["s3"], 10: ["pt0", "pt1"],
          11: ["pv0", "pt2"], 12: ["pv1", "pt3"], 13: ["pv2"], 14: ["pv3", "gate"]},
    "Dkv": {1: ["krot", "kstat"], 2: ["rot", "stat"], 4: ["rsum"], 5: ["kspread"], 6: ["v"], 7: ["s0"], 8: ["s1"], 9: ["s2"],
            10: ["s3"], 12: ["pt0", "pt1"], 13: ["pv0", "pt2"], 14: ["pv1", "pt3"],
            15: ["pv2", "pv3", "gate"]},
    "turn0": {**{s: [f"turn{2 * s + 4}", f"turn{2 * s + 5}"] for s in range(6)},
              **{s: [f"tab{s}"] for s in range(EARLY_TABS, 16)}},
    "turn1": {s: [f"turn{s + 4}"] + ({0: ["h2"], 4: ["h3"]}.get(s, [])) for s in range(12)},
    "lstat": {0: ["krope"], **{s + 1: [f"lstat{s}"] for s in range(QB + KVB)}, QB + KVB + 2: ["lstat"]},
    "lnorm": {0: ["lspreadq"], 1: ["lnorm0"], 2: ["lnorm1"], 3: ["lnorm2"], 4: ["lnorm3"], 5: ["lnorm4"],
              6: ["lnorm5"], 7: ["lspreadk"], 8: ["lnorm6"], 9: ["lnorm7"], 10: ["lnorm8"], 11: ["lnorm9"]},
    None: {},
}


def build(nc, x, pre_norm, post_norm, even_w_in, even_w_out, lq1, lk1, lq2, lk2, subln, q_norm, w_uq,
          kv_norm, w_ukv, odd_w_in, odd_w_out, rpb, gq_norm, gk_norm, c_alibi, c_small, c_shift,
          c_rope_b, c_rope_d, x1, tables, out):
    ctx = ExitStack()
    with ctx:
        top = [(nc.sbuf_base + 31) // 32 * 32]

        def region(size):
            at = top[0]
            top[0] += size
            assert top[0] <= nc.sbuf_usable_end, top[0]
            return at

        def place(name, at, shape, dt=F32):
            return nc.alloc_sbuf_tensor_at(name, shape, dt, offset=at)

        def sem(name):
            return ctx.enter_context(nc.semaphore(name))

        KB = 1024
        X, O, W = region(64 * KB), region(64 * KB), region(42 * KB)

        xT_hi = place("xT_hi", X, [P, KT, SEQ], F32R)
        xT_lo = place("xT_lo", X + 32 * KB, [P, KT, SEQ], F32R)
        resid = place("resid", X, [P, ST, DM])
        oT_hi = place("oT_hi", O, [P, 2 * H, SEQ], F32R)
        oT_lo = place("oT_lo", O + 32 * KB, [P, 2 * H, SEQ], F32R)
        gates_b = place("gates_b", O + 16 * KB, [P, H, SEQ])
        lsq = place("lsq", O + 48 * KB, [P, 2, SEQ])
        th_b = (place("th_b", O + 52 * KB, [P, SEQ])[:, :], lsq[:, 0, :])
        ldiag = place("ldiag", O + 54 * KB, [P, ST, P])
        krt = place("krt", O + 56 * KB, [ROPE_D, 4, SEQ])
        xrow = place("xrow", O, [P, ST, DM])
        hrow = place("hrow", O + 32 * KB, [P, ST, DM])
        table_all = place("table_all", O, [P, H, DR - 1, GRID_W])
        lat_hi = place("lat_hi", W, [P, QB + KVB, SEQ], F32R)
        lat_lo = place("lat_lo", W + 20 * KB, [P, QB + KVB, SEQ], F32R)
        lat_raw = place("lat_raw", W + 20 * KB, [P, QB + KVB, SEQ])
        lsum = place("lsum", W, [P, 2, SEQ])
        lat_tmp = place("lat_tmp", W + 40 * KB, [P, SEQ])
        mrow = place("mrow", W, [P, ST, DM])
        post_gain = place("post_gain", W + 32 * KB, [P, DM])
        squares = place("squares", W + 40 * KB, [P, SEQ])

        class Work:
            pass

        def work(tag, at):
            w = Work()
            a = [at]

            def b(name, shape, dt=F32):
                t = place(f"{name}_{tag}", a[0], shape, dt)
                a[0] += int(np.prod(shape[1:])) * 4
                return t
            w.q_hi, w.q_lo = b("q_hi", [P, SEQ], F32R), b("q_lo", [P, SEQ], F32R)
            w.k_hi, w.k_lo = b("k_hi", [P, SEQ], F32R), b("k_lo", [P, SEQ], F32R)
            w.v_hi, w.v_lo = b("v_hi", [P, ST, P], F32R), b("v_lo", [P, ST, P], F32R)
            w.vT = b("vT", [P, SEQ])
            w.p = b("p", [P, ST, SEQ])
            w.pT_hi, w.pT_lo = b("pT_hi", [P, 2, SEQ], F32R), b("pT_lo", [P, 2, SEQ], F32R)
            w.g = b("g", [P, SEQ])
            w.diag = place(f"diag_{tag}", a[0], [P, ST, P])
            w.th = b("th", [P, SEQ])
            w.sb = place(f"sb_{tag}", a[0], [P, 2, SEQ])
            w.e = place(f"e_{tag}", a[0] + 2 * SEQ * 4, [P, 2, SEQ])
            w.rq, w.rq_sin, w.rk, w.rk_sin = (b(f"r{j}", [P, SEQ]) for j in range(4))
            w.end = a[0]
            return w

        w_acd = work("w", W)
        assert w_acd.end <= W + 42 * KB, (w_acd.end - W)
        w_b = work("x", X + 20 * KB)
        pe_hi = place("pe_hi", X, [ROPE_D, SEQ], F32R)
        pe_lo = place("pe_lo", X + 2 * KB, [ROPE_D, SEQ], F32R)
        res_b = place("res_b", X + 8 * KB, [P, SEQ])
        assert w_b.end <= X + 64 * KB

        raw_at, split_at = region(RING * SLOT * 4), region(2 * RING * SLOT * 4)
        raw = place("raw", raw_at, [P, RING, SLOT])
        w_hi = place("w_hi", split_at, [P, RING, SLOT], F32R)
        w_lo = place("w_lo", split_at + RING * SLOT * 4, [P, RING, SLOT], F32R)

        def small(name, cols, dt=F32, parts=P):
            return place(name, region((cols * 4 + 31) // 32 * 32), [parts, cols], dt)
        bias_at = region(CW * 4)
        bias = place("bias", bias_at, [P, CW])
        rope_at = region(2 * SEQ * 4)
        rope = place("rope", rope_at, [P, 2, SEQ])
        kpe_at = X + 4 * KB
        kpe_hi = place("kpe_hi", kpe_at, [ROPE_D, SEQ], F32R)
        kpe_lo = place("kpe_lo", kpe_at + 2 * KB, [ROPE_D, SEQ], F32R)
        consts = small("consts", 2 * P + GRID_W)
        ident = consts[:, 0:P]
        rotT = consts[:, P:2 * P]
        mask = consts[:, 2 * P:2 * P + GRID_W]
        ones = small("ones", P)
        gains = small("gains", 2 * KT + QB + KVB + 3)
        pre_gain = gains[:, 0:2 * KT]
        lat_gain = gains[:, 2 * KT:2 * KT + QB + KVB]
        sub_gain = gains[:, 2 * KT + QB + KVB:2 * KT + QB + KVB + 1]
        gq_gain = gains[:, 2 * KT + QB + KVB + 1:2 * KT + QB + KVB + 2]
        gk_gain = gains[:, 2 * KT + QB + KVB + 2:2 * KT + QB + KVB + 3]
        st = small("st", 106)
        esum = st[:, 0:8]
        rsum = st[:, 8:16]
        nmax = st[:, 16:24]
        mixc = st[:, 24:28]
        var = st[:, 28:36]
        var2 = st[:, 36:44]
        rstd = st[:, 44:52]
        rscale = st[:, 52:56]
        rowsq = st[:, 56:72]
        rowvar = st[:, 72:76]
        rowstd = st[:, 76:80]
        prevar = st[:, 94:98]
        prestd = st[:, 98:102]
        tmpvar = st[:, 102:106]
        neglam = st[:, 80:81]
        lam = st[:, 81:85]
        gate_gain = st[:, 85:86]
        kstd = st[:, 86:90]
        nm = st[:, 90:94]
        expo = small("expo", 8)

        xrow0 = place("xrow0", W, [P, ST, DM])
        sq_junk = place("sq_junk", W + 32 * KB, [P, DM])
        lamv = place("lamv", W + 40 * KB, [P, 4, 64])
        lamp = place("lamp", W + 41 * KB, [P, 2, 64])
        rpb_rows = place("rpb_rows", O + 28 * KB, [H * DR, DC])
        rpbT = place("rpbT", O + 29 * KB, [DC, H, DR])
        shift = place("shift", O + 30 * KB, [32, 2 * GRID_W - 1])

        bank = [ctx.enter_context(nc.psum_tensor(f"bank{i}", [P, 512], F32)) for i in range(8)]
        B_S, B_T, B_O = (4, 5), 6, 7
        tb, ob = bank[B_T], bank[B_O]
        krb, rb = bank[B_S[0]], bank[B_S[1]]

        raw_in = [sem(f"raw_in{i}") for i in range(RING)]
        hi_made, lo_made = sem("hi_made"), sem("lo_made")
        w_used = sem("w_used")
        proj = [sem(f"proj{i}") for i in range(4)]
        bank_free = [sem(f"bank_free{i}") for i in range(4)]
        consts_in, norm_in, rpb_in, lam_in = sem("consts_in"), sem("norm_in"), sem("rpb_in"), sem("lam_in")
        x_in = [sem(f"x_in{t}") for t in range(ST)]
        resid_in, gain_in = sem("resid_in"), sem("gain_in")
        rope_in, bias_in = sem("rope_in"), sem("bias_in")
        ones_set = sem("ones_set")
        x1_out, out_out, tables_out = sem("x1_out"), sem("out_out"), sem("tables_out")
        m_copied, m_total, m_var, m_pow, last_made = (
            sem(n) for n in ("m_copied", "m_total", "m_var", "m_pow", "last_made"))
        x_made, x_sq, x_var, x_pow, h_made = (sem(n) for n in ("x_made", "x_sq", "x_var", "x_pow", "h_made"))
        xt_turned, xt_hi, xt_lo = sem("xt_turned"), sem("xt_hi"), sem("xt_lo")
        q_hi_s, q_lo_s, k_hi_s, k_lo_s = sem("q_hi_s"), sem("q_lo_s"), sem("k_hi_s"), sem("k_lo_s")
        pe_hi_s, pe_lo_s, kpe_hi_s, kpe_lo_s = sem("pe_hi_s"), sem("pe_lo_s"), sem("kpe_hi_s"), sem("kpe_lo_s")
        v_turned, v_hi_s, v_lo_s = sem("v_turned"), sem("v_hi_s"), sem("v_lo_s")
        th_made = sem("th_made")
        scored, s_read, nmaxed, exped = sem("scored"), sem("s_read"), sem("nmaxed"), sem("exped")
        recip_s, mixc_s, p_made = sem("recip_s"), sem("mixc_s"), sem("p_made")
        p_turned, pT_hi_s, pT_lo_s, pv_done = sem("p_turned"), sem("pT_hi_s"), sem("pT_lo_s"), sem("pv_done")
        o_read, o_gated, o_hi_s, o_lo_s = sem("o_read"), sem("o_gated"), sem("o_hi_s"), sem("o_lo_s")
        o_sq, a_stat, a_var, a_pow, a_diag, a_spread = (
            sem(n) for n in ("o_sq", "a_stat", "a_var", "a_pow", "a_diag", "a_spread"))
        r_in, r_rot, r_cos, r_sin, r_sum = (sem(n) for n in ("r_in", "r_rot", "r_cos", "r_sin", "r_sum"))
        kr_in, kr_rot, kr_cos, kr_sin, kr_sum = (sem(n) for n in ("kr_in", "kr_rot", "kr_cos", "kr_sin", "kr_sum"))
        d_stat, d_var, d_pow = (sem(n) for n in ("d_stat", "d_var", "d_pow"))
        k_stat, k_var, k_pow, k_diag, k_spread, k_scaled = (
            sem(n) for n in ("k_stat", "k_var", "k_pow", "k_diag", "k_spread", "k_scaled"))
        l_sq, l_add, l_stat, l_var, l_pow, l_diag, l_spread, l_mul, l_hi, l_lo = (
            sem(n) for n in ("l_sq", "l_add", "l_stat", "l_var", "l_pow", "l_diag", "l_spread", "l_mul",
                             "l_hi", "l_lo"))
        rpb_turned, rpb_copied, t_done, t_evac = (sem(n) for n in ("rpb_turned", "rpb_copied", "t_done", "t_evac"))
        lam_dot, lam_exp, lam_sum = sem("lam_dot"), sem("lam_exp"), sem("lam_sum")

        win0, wout0, win1, wout1 = even_w_in[0], even_w_out[0], odd_w_in[0], odd_w_out[0]
        block = ctx.enter_context(nc.Block())

        def block_done(eng, b, part, i):
            u, with_unit = closing(b, part, i)
            if with_unit:
                first, turn_units, turn = units_of(part, i)
                eng.wait_ge(w_used, first + turn * turn_units + u + 1)
            else:
                eng.wait_ge(proj[b], proj_of(b, part, i) + 1)

        def block_out(eng, b, part, i):
            eng.wait_ge(bank_free[b], use_of(b, part, i) + 1)

        def chunk_of(t, part):
            return t - {"A": 0, "B": H, "C": 2 * H, "D": 3 * H}[part]

        def turned(j):
            return bank[B_S[0] if j % 2 else B_T]

        def gate_out(eng, t, part):
            if part == "B":
                block_out(eng, gate_banks(4)[3], "prep", 4)
            else:
                c = chunk_of(t, part)
                block_out(eng, q_bank(c) + 1 if part == "D" else 3, part, c)

        def work_of(part):
            return w_b if part == "B" else w_acd

        def o_slot(t, part):
            return t if part in ("A", "B") else t - 2 * H

        @block.sync
        def _(sp):
            def unit(n, slot, *pieces):
                wait(sp, lo_made, n - RING + 1)
                for c0, c1, src in pieces:
                    dst = raw[:, slot, c0:c1]
                    if len(src.shape) == 3:
                        dst = dst.rearrange("p (b c) -> p b c", b=src.shape[1])
                    sp.dma_start(dst, src).then_inc(raw_in[slot], 16)

            def head_units(w, first, i):
                for s in range(KT):
                    cols = w[s * P:(s + 1) * P, 0:4 * H * P].rearrange("p (b c) -> p b c", b=4)
                    unit(first + i * KT + s, s % RING, (0, 512, cols[:, :, bass.ds(i * P, P)]))

            sp.dma_start(rpb_rows[:, :], rpb[0].rearrange("h r c -> (h r) c")).then_inc(rpb_in, 16)
            sp.dma_start(consts[:, :], c_small[:, :]).then_inc(rpb_in, 16)
            sp.dma_start(shift[:, :], c_shift[:, :]).then_inc(rpb_in, 16)
            for t in range(ST):
                sp.dma_start(xrow0[:, t, :], x[0, t * P:(t + 1) * P, :]).then_inc(x_in[t], 16)
            head_units(win0, U_A, 0)
            with sp.Fori(1, H) as i:
                head_units(win0, U_A, i)
            for c in range(5):
                c0 = 4 * H * P + (c * 512 if c < 3 else Q_RANK + KV_RANK + ROPE_D + (c - 3) * 512)
                width = 2 * P + ROPE_D if c == 2 else 512
                for s in range(KT):
                    unit(U_PREP + c * KT + s, s % RING, (0, width, win0[s * P:(s + 1) * P, c0:c0 + width]))

            def latent_units(i):
                for s in range(2):
                    src = w_uq[0, s * 384:(s + 1) * 384, bass.ds(i * 192, 192)]
                    unit(U_B + i * 4 + s, s, (0, 576, src.rearrange("(k p) c -> p k c", p=P)))
                for s in range(2):
                    src = w_ukv[0, s * 256:(s + 1) * 256, bass.ds(i * 256, 256)]
                    unit(U_B + i * 4 + 2 + s, 2 + s, (0, 512, src.rearrange("(k p) c -> p k c", p=P)))
            latent_units(0)
            with sp.Fori(1, H) as i:
                latent_units(i)

            def out_units(w, first):
                with sp.Fori(0, 4) as c:
                    for s in range(KT):
                        unit(first + c * KT + s, s % RING, (0, 512, w[s * P:(s + 1) * P, bass.ds(c * 512, 512)]))
            out_units(wout0, U_OUT0)
            with sp.Fori(0, H) as i:
                head_units(win1, U_C, i)
            q0 = 4 * H * P
            k0, g0 = q0 + H * P, q0 + H * P + 4 * P
            for g in range(2):
                for j in range(4):
                    h = 4 * g + j

                    def cols(s, c0):
                        return win1[s * P:(s + 1) * P, c0:c0 + P]
                    if j == 0:
                        for s in range(KT):
                            kv = win1[s * P:(s + 1) * P, k0:k0 + 4 * P].rearrange("p (b c) -> p b c", b=2)
                            unit(U_D + g * D_GROUP + s, s % RING, (0, P, cols(s, q0 + h * P)),
                                 (P, 2 * P, cols(s, g0 + h * P)), (2 * P, 4 * P, kv[:, :, g * P:(g + 1) * P]))
                    else:
                        for s in range(0, KT, 2):
                            unit(U_D + g * D_GROUP + KT + (j - 1) * KT // 2 + s // 2, s // 2 % RING,
                                 (0, P, cols(s, q0 + h * P)), (P, 2 * P, cols(s, g0 + h * P)),
                                 (2 * P, 3 * P, cols(s + 1, q0 + h * P)), (3 * P, 4 * P, cols(s + 1, g0 + h * P)))
            out_units(wout1, U_OUT1)

        @block.gpsimd
        def _(pool):
            pool.memset(ones[:, :], 1.0).then_inc(ones_set, 1)
            pool.memset(expo[:, :], -0.5).then_inc(ones_set, 1)
            for dst, src, k in ((lat_gain[:, 0:QB], q_norm[0], QB), (lat_gain[:, QB:QB + KVB], kv_norm[0], KVB),
                                (sub_gain, subln[0], 1), (gq_gain, gq_norm[0], 1), (gk_gain, gk_norm[0], 1)):
                pool.dma_start(dst, src.rearrange("(k p) -> p k", p=P), allow_slow_non_contiguous=True
                               ).then_inc(consts_in, 16)
            for j, v in enumerate((lq1, lk1, lq2, lk2)):
                pool.dma_start(lamv[:, j, :], v[0:1, :].to_broadcast([P, 64])).then_inc(lam_in, 16)
            pool.dma_start(bias[:, :], c_alibi[0]).then_inc(bias_in, 16)
            pool.dma_start(rope[0:ROPE_D, :, :], c_rope_b.rearrange("a p s -> p a s")).then_inc(rope_in, 16)
            pool.wait_ge(ones_set, 2)

            def inv_root(dst, src, scale, tmp, mid, mid_value, done):
                pool.tensor_scalar(tmp, src, scale, EPS, ALU.mult, ALU.add).then_inc(mid, 1)
                pool.wait_ge(mid, mid_value)
                pool.tensor_tensor(dst, tmp, expo[:, 0:src.shape[1]], ALU.pow).then_inc(done, 1)

            def diagonals(diag, column, done):
                for j in range(ST):
                    pool.tensor_scalar(diag[:, j, :], ident, column[:, j:j + 1], 0.0, ALU.mult, ALU.add
                                       ).then_inc(done, 1)

            def pre_rows(layer):
                for t in range(ST):
                    n = layer * ST + t + 1
                    pool.wait_ge(x_sq, n)
                    inv_root(prestd[:, t:t + 1], prevar[:, t:t + 1], 1.0 / DM, tmpvar[:, t:t + 1], x_var, n, x_pow)

            def post_rows(layer):
                pool.wait_ge(m_total, layer + 1)
                inv_root(rowstd, rowvar, 1.0 / DM, tmpvar, m_var, layer + 1, m_pow)

            def post_loads(layer):
                if layer == 0:
                    pool.wait_ge(w_used, U_OUT0)
                else:
                    pool.wait_ge(o_lo_s, 4 * H)
                pool.dma_start(post_gain[:, :], post_norm[layer:layer + 1, :].to_broadcast([P, DM])
                               ).then_inc(gain_in, 16)
                if layer == 0:
                    pool.wait_ge(o_lo_s, 2 * H)
                else:
                    pool.wait_ge(w_used, U_OUT1)
                for t in range(ST):
                    pool.wait_ge(w_used, (U_OUT0 if layer == 0 else U_OUT1) + KT + 6 * t)
                    pool.dma_start(resid[:, t, :], (x[0] if layer == 0 else x1)[t * P:(t + 1) * P, :]
                                   ).then_inc(resid_in, 16)

            pre_rows(0)
            pool.wait_ge(t_evac, KT)
            pool.dma_start(tables.rearrange("h p c -> p h c"),
                           table_all[:, :, :, :].rearrange("p h j c -> p h (j c)")).then_inc(tables_out, 16)

            def next_bias(src, i, t, part):
                pool.wait_ge(s_read, s_before(t + 1, part))
                pool.dma_start(bias[:, :], src[bass.ds(i, 1), :, :].rearrange("a p c -> (a p) c")
                               ).then_inc(bias_in, 16)

            def a_factors(t):
                wait_apart(pool, a_var, 2 * t + 2)
                pool.tensor_scalar(var2[:, 0:ST], var[:, 0:ST], 1.0 / P, EPS, ALU.mult, ALU.add).then_inc(a_pow, 1)
                pool.wait_ge(a_pow, 3 * t + 1)
                pool.tensor_tensor(rstd[:, ST:2 * ST], var2[:, 0:ST], expo[:, 0:ST], ALU.pow).then_inc(a_pow, 1)
                pool.wait_ge(a_pow, 3 * t + 2)
                pool.tensor_tensor(rstd[:, 0:ST], rstd[:, ST:2 * ST], rsum[:, 0:ST], ALU.mult).then_inc(a_pow, 1)
                gate_out(pool, t, "A")
                wait_apart(pool, a_pow, 3 * t + 3)
                diagonals(w_acd.diag, rstd, a_diag)

            with pool.Fori(1, H) as i:
                next_bias(c_alibi, i, i - 1, "A")
                a_factors(i - 1)
            a_factors(H - 1)

            block_out(pool, 2, "prep", 2)
            pool.wait_ge(rope_in, 16)
            pool.tensor_tensor(krt[:, 1, :], krt[:, 0, :], rope[0:ROPE_D, 0, :], ALU.mult).then_inc(kr_cos, 1)
            pool.wait_ge(kr_sin, 1)
            pool.wait_ge(kr_cos, 1)
            pool.tensor_tensor(krt[:, 3, :], krt[:, 1, :], krt[:, 2, :], ALU.add).then_inc(kr_sum, 1)
            pool.wait_ge(l_var, 1)
            inv_root(rstd[:, 0:ST], var[:, 0:ST], 1.0 / Q_RANK, var2[:, 0:ST], l_pow, 1, l_pow)
            inv_root(rstd[:, ST:2 * ST], var[:, ST:2 * ST], 1.0 / KV_RANK, var2[:, ST:2 * ST], l_pow, 3, l_pow)
            pool.wait_ge(l_pow, 4)
            diagonals(ldiag, rstd[:, 0:ST], l_diag)
            pool.wait_ge(l_spread, 1)
            diagonals(ldiag, rstd[:, ST:2 * ST], l_diag)

            with pool.Fori(0, H) as i:
                block_out(pool, 3, "B", i)
                pool.wait_ge(r_rot, i + 1)
                pool.tensor_tensor(w_b.rk[0:ROPE_D, :], w_b.rq[0:ROPE_D, :], rope[0:ROPE_D, 0, :], ALU.mult
                                   ).then_inc(r_cos, 1)
                pool.wait_ge(r_sin, i + 1)
                pool.wait_ge(r_cos, i + 1)
                pool.tensor_tensor(w_b.rk_sin[0:ROPE_D, :], w_b.rk[0:ROPE_D, :], w_b.rq_sin[0:ROPE_D, :], ALU.add
                                   ).then_inc(r_sum, 1)
            pool.dma_start(rope[:, :, :], c_rope_d.rearrange("a p s -> p a s")).then_inc(rope_in, 16)
            pool.wait_ge(tables_out, 16)
            pool.dma_start(bias[:, :], tables[0]).then_inc(bias_in, 16)
            post_loads(0)
            post_rows(0)
            pre_rows(1)
            with pool.Fori(1, H) as i:
                next_bias(tables, i, 2 * H - 1 + i, "C")

            pool.wait_ge(rope_in, 32)
            for n in range(H):
                g = n // 4
                if n % 4 == 0:
                    pool.wait_ge(kr_rot, g + 2)
                    pool.tensor_tensor(w_acd.rk[:, :], w_acd.rk[:, :], rope[:, 0, :], ALU.mult).then_inc(kr_cos, 1)
                    pool.wait_ge(kr_sin, g + 2)
                    pool.wait_ge(kr_cos, g + 2)
                    pool.tensor_tensor(w_acd.rk[:, :], w_acd.rk[:, :], w_acd.rk_sin[:, :], ALU.add
                                       ).then_inc(kr_sum, 1)
                    pool.wait_ge(k_var, g + 1)
                    inv_root(kstd, var[:, ST:2 * ST], 1.0 / P, var2[:, ST:2 * ST], k_pow, 2 * g + 1, k_pow)
                    pool.wait_ge(k_pow, 2 * g + 2)
                    gate_out(pool, 3 * H + n, "D")
                    diagonals(w_acd.diag, kstd, k_diag)
                pool.wait_ge(r_rot, H + n + 1)
                pool.tensor_tensor(w_acd.rq[:, :], w_acd.rq[:, :], rope[:, 0, :], ALU.mult).then_inc(r_cos, 1)
                pool.wait_ge(r_sin, H + n + 1)
                pool.wait_ge(r_cos, H + n + 1)
                pool.tensor_tensor(w_acd.rq[:, :], w_acd.rq[:, :], w_acd.rq_sin[:, :], ALU.add).then_inc(r_sum, 1)
                pool.wait_ge(d_var, n + 1)
                inv_root(rstd[:, 0:ST], var[:, 0:ST], 1.0 / P, var2[:, 0:ST], d_pow, 3 * n + 1, d_pow)
                pool.wait_ge(d_pow, 3 * n + 2)
                pool.tensor_scalar(rscale, rstd[:, 0:ST], SCALE_CD, 0.0, ALU.mult, ALU.add).then_inc(d_pow, 1)
            post_loads(1)
            post_rows(1)
            pool.wait_ge(m_pow, 2)
            pool.wait_ge(resid_in, 16 * ST * 2)
            pool.tensor_scalar(mrow[:, ST - 1, :], mrow[:, ST - 1, :], rowstd[:, ST - 1:ST], 0.0, ALU.mult, ALU.add
                               ).then_inc(last_made, 1)
            pool.wait_ge(last_made, 1)
            pool.tensor_tensor(xrow[:, ST - 1, :], mrow[:, ST - 1, :], resid[:, ST - 1, :], ALU.add
                               ).then_inc(last_made, 1)

        def unit_of(first, turn_units, i, s):
            n = first + i * turn_units + s
            return n, (n if isinstance(n, int) else first + s % turn_units)

        @block.scalar
        def _(act):
            def split(first, turn_units, i, s):
                n, like = unit_of(first, turn_units, i, s)
                if isinstance(n, int) and n >= U_END:
                    return
                slot, width = s % RING, unit_width(like)
                if isinstance(n, int):
                    act.wait_ge(raw_in[slot], raw_count(n))
                else:
                    act.wait_ge(raw_in[slot], raw_count(first + s) + i * (16 * turn_units // RING))
                wait(act, w_used, n - RING + 1)
                act.activation(w_hi[:, slot, 0:width], raw[:, slot, 0:width], ACT.Copy).then_inc(hi_made, 1)

            def rows_norm(layer):
                for t in range(ST):
                    if layer == 0:
                        act.wait_ge(x_in[t], 16)
                    else:
                        act.wait_ge(x_made, t + 1)
                        act.dma_start(x1[t * P:(t + 1) * P, :], xrow[:, t, :]).then_inc(x1_out, 16)
                    wait(act, x_sq, ST * layer + t)
                    rows, junk = (xrow0, sq_junk[:, :]) if layer == 0 else (xrow, resid[:, 0, :])
                    act.activation(junk, rows[:, t, :], ACT.Square, accum_out=prevar[:, t:t + 1]).then_inc(x_sq, 1)

            def item(what, part, t):
                w = work_of(part)
                if what[:4] == "turn":
                    k = int(what[4:])
                    n = t * KT + k
                    act.wait_ge(xt_turned, n + 1)
                    act.activation(xT_hi[:, k, :], bank[4 + k % 4][:, :], ACT.Copy, scale=pre_gain[:, n:n + 1]
                                   ).then_inc(xt_hi, 1)
                    return
                if what in ("h0", "h1", "h2", "h3"):
                    return
                if what == "v":
                    act.wait_ge(v_turned, kv_of(t, part) + 1)
                    act.activation(w.v_hi[:, :, :], tb[:, :].rearrange("p (a b) -> p a b", a=ST), ACT.Copy
                                   ).then_inc(v_hi_s, 1)
                elif what[0] == "s" and what[1:].isdigit():
                    j = int(what[1:])
                    n = s_before(t, part) + j
                    if part == "A":
                        act.wait_ge(s_read, n + 1)
                        if j >= 2:
                            act.wait_ge(p_made, 4 * t + j // 2)
                        cell = j % 2 * 4 + j // 2
                        act.activation(w.e[:, j % 2, :], w.sb[:, j % 2, :], ACT.Exp, bias=nmax[:, j:j + 1],
                                       scale=-1.0, accum_out=esum[:, cell:cell + 1]).then_inc(exped, 1)
                    elif part == "C":
                        act.wait_ge(s_read, n + 1)
                        act.wait_ge(p_turned, 4 * t)
                        act.activation(w.p[:, j, :], w.sb[:, j % 2, :], ACT.Exp, bias=nmax[:, j:j + 1],
                                       scale=-1.0, accum_out=esum[:, j:j + 1]).then_inc(exped, 1)
                    else:
                        act.wait_ge(nmaxed, nmax_before(t, part) + j + 1)
                        act.wait_ge(p_turned, 4 * t)
                        act.activation(w.p[:, j, :], bank[B_S[j % 2]][:, :], ACT.Exp, bias=nmax[:, j:j + 1],
                                       scale=SCALE_B if part == "B" else rscale[:, j:j + 1],
                                       accum_out=esum[:, j:j + 1]).then_inc(exped, 1)
                elif what[:2] == "pt":
                    j = int(what[2:])
                    act.wait_ge(p_turned, 4 * t + j + 1)
                    if j >= 2:
                        act.wait_ge(pv_done, 4 * t + j - 1)
                    act.activation(w.pT_hi[:, j % 2, :], turned(j)[:, :], ACT.Copy).then_inc(pT_hi_s, 1)
                elif what == "stat" and part == "A":
                    act.wait_ge(pv_done, 4 * t + 4)
                    act.activation(w.vT[:, :], ob[:, :], ACT.Square).then_inc(o_sq, 1)
                elif what == "rsum":
                    act.wait_ge(r_sum, rot_of(t, part) + 1)
                    if part == "B":
                        act.activation(pe_hi[:, :], w.rk_sin[0:ROPE_D, :], ACT.Copy).then_inc(pe_hi_s, 1)
                    else:
                        act.activation(w.q_hi[:, :], w.rq[:, :], ACT.Copy).then_inc(q_hi_s, 1)
                elif what == "kspread":
                    act.wait_ge(k_scaled, (t - 24) // 4 + 1)
                    act.activation(w.k_hi[:, :], w.rk_sin[:, :], ACT.Copy).then_inc(k_hi_s, 1)
                elif what == "gate":
                    act.wait_ge(o_gated, t + 1)
                    if part == "A":
                        act.wait_ge(tables_out, 16)
                    if part == "C":
                        act.wait_ge(x1_out, 16 * ST)
                    act.activation(oT_hi[:, bass.ds(o_slot(t, part), 1), :].rearrange("p a s -> p (a s)"),
                                   (res_b if part == "B" else w.g)[:, :], ACT.Copy).then_inc(o_hi_s, 1)
                elif what[:5] == "lstat" and what != "lstat":
                    j = int(what[5:])
                    block_out(act, j % 4, "prep", j // 4)
                    if j in (0, QB):
                        dst = lsum[:, int(j == QB), :]
                    else:
                        dst = lsq[:, j % 2, :]
                        wait(act, l_add, j - 2 if j < QB else max(QB - 1, j - 3))
                    act.activation(dst, lat_raw[:, j, :], ACT.Square).then_inc(l_sq, 1)
                elif what[:5] == "lnorm":
                    j = int(what[5:])
                    act.wait_ge(l_mul, j + 1)
                    act.activation(lat_hi[:, j, :], lat_tmp[:, :], ACT.Copy).then_inc(l_hi, 1)

            def evac(part, i):
                w = work_of(part)

                def done(b):
                    block_done(act, b, part, i)
                if part in ("A", "C"):
                    t = i if part == "A" else 2 * H + i
                    done(0)
                    wait(act, scored, s_before(t, part))
                    act.activation(w.q_hi[:, :], bank[0][:, :], ACT.Copy).then_inc(q_hi_s, 1)
                    done(1)
                    act.activation(w.k_hi[:, :], bank[1][:, :], ACT.Copy).then_inc(k_hi_s, 1)
                    done(2)
                    if part == "A":
                        wait(act, a_stat, t)
                    wait(act, v_turned, t)
                    act.activation(w.vT[:, :], bank[2][:, :], ACT.Copy).then_inc(bank_free[2], 1)
                    done(3)
                    if part == "A":
                        wait(act, a_spread, t)
                    act.activation(w.th[:, :], bank[3][:, :], ACT.Tanh, scale=0.5).then_inc(th_made, 1)
                elif part == "prep" and i < 3:
                    if i == 0:
                        act.wait_ge(o_lo_s, H)
                    for b in range(4 if i < 2 else 2):
                        done(b)
                        act.activation(lat_raw[:, 4 * i + b, :], bank[b][:, :], ACT.Copy
                                       ).then_inc(bank_free[b], 1)
                    if i == 2:
                        done(2)
                        act.activation(krt[:, 0, :], bank[2][0:ROPE_D, :], ACT.Copy).then_inc(bank_free[2], 1)
                elif part == "prep":
                    for j, b in enumerate(gate_banks(i)):
                        done(b)
                        if j >= 2:
                            block_out(act, gate_banks(i)[j - 2], "prep", i)
                        elif i > 3:
                            block_out(act, gate_banks(i - 1)[j + 2], "prep", i - 1)
                        act.activation(th_b[j % 2], bank[b][:, :], ACT.Tanh, scale=0.5).then_inc(th_made, 1)
                elif part == "B":
                    done(0)
                    act.activation(w.k_hi[:, :], bank[0][:, :], ACT.Copy).then_inc(k_hi_s, 1)
                    done(1)
                    act.activation(w.vT[:, :], bank[1][:, :], ACT.Copy).then_inc(bank_free[1], 1)
                elif part == "D":
                    t = 3 * H + i
                    b = q_bank(i)
                    done(b)
                    act.wait_ge(exped, s_before(t, part))
                    wait(act, p_turned, 4 * t)
                    act.activation(w.rq[:, :], bank[b][:, :], ACT.Copy, scale=gq_gain).then_inc(r_in, 1)
                    act.activation(w.p[:, 0, :], bank[b][:, :], ACT.Square).then_inc(bank_free[b], 1)
                    done(b + 1)
                    act.activation(w.th[:, :], bank[b + 1][:, :], ACT.Tanh, scale=0.5).then_inc(th_made, 1)
                    if i % 4 == 0:
                        done(2)
                        act.activation(w.rk[:, :], bank[2][:, :], ACT.Copy, scale=gk_gain).then_inc(kr_in, 1)
                        act.activation(w.p[:, 1, :], bank[2][:, :], ACT.Square
                                       ).then_inc(bank_free[2], 1)
                        done(3)
                        act.activation(w.vT[:, :], bank[3][:, :], ACT.Copy).then_inc(bank_free[3], 1)
                else:
                    layer = 0 if part == "out0" else 1
                    for b in range(ST):
                        if b:
                            block_out(act, b - 1, part, i)
                        elif not i_is_zero(i):
                            block_out(act, 3, part, i - 1)
                        act.wait_ge(m_copied, 16 * layer + 4 * i + b + 1)
                        act.activation(squares[:, :], bank[b][:, :], ACT.Square,
                                       accum_out=rowsq[:, bass.ds(i + 4 * b, 1)]
                                       ).then_inc(bank_free[b], 1)

            def queries_out(i):
                w, t = w_b, H + i
                block_done(act, 3, "B", i)
                if isinstance(i, int):
                    act.wait_ge(w_used, U_B)
                act.wait_ge(scored, s_before(t, "B"))
                act.activation(w.rq[0:ROPE_D, :], bank[3][0:ROPE_D, :], ACT.Copy).then_inc(bank_free[3], 1)
                block_done(act, 2, "B", i)
                act.activation(w.q_hi[:, :], bank[2][:, :], ACT.Copy).then_inc(q_hi_s, 1)
                if isinstance(i, int):
                    act.wait_ge(kr_sum, 1)
                    act.activation(kpe_hi[:, :], krt[:, 3, :], ACT.Copy).then_inc(kpe_hi_s, 1)

            def chunk(part, i, woven, att, t):
                first, turn_units, turn = units_of(part, i)
                late = part == "D" and i % 4 > 0
                for s, (u, place_in, _, _) in enumerate(ktiles(part, i)):
                    if place_in == 0 and not late:
                        split(first, turn_units, turn, u + AHEAD)
                    for what in WOVEN[woven].get(s, []):
                        if what == "own q":
                            queries_out(i)
                        elif what == "own rot":
                            item("rot", "B", H + i)
                            item("rsum", "B", H + i)
                        else:
                            item(what, att, t)
                    if place_in == 0 and late:
                        split(first, turn_units, turn, u + AHEAD)
                evac(part, i)
                for what in WOVEN[woven].get("end", []):
                    item(what, att, t)

            for layer in range(2):
                act.dma_start(gains[:, layer * KT:(layer + 1) * KT], pre_norm[layer].rearrange("(k p) -> p k", p=P),
                              allow_slow_non_contiguous=True).then_inc(norm_in, 16)
            rows_norm(0)
            split(U_A, KT, 0, 0)
            split(U_A, KT, 0, 1)
            act.wait_ge(norm_in, 32)
            for k in range(4):
                item(f"turn{k}", None, 0)
            chunk("A", 0, "turn0", None, 0)
            act.wait_ge(lam_dot, 2)
            act.activation(lam[:, 2:4], lam[:, 0:2], ACT.Exp).then_inc(lam_exp, 1)
            act.wait_ge(consts_in, 16 * 5)
            with act.Fori(1, H) as i:
                chunk("A", i, "A", "A", i - 1)
            chunk("prep", 0, "A", "A", H - 1)
            chunk("prep", 1, None, None, None)
            chunk("prep", 2, None, None, None)
            chunk("prep", 3, "lstat", None, None)
            chunk("prep", 4, "lnorm", None, None)
            chunk("B", 0, "Bfirst", None, None)
            with act.Fori(1, H) as i:
                chunk("B", i, "B", "B", i + (H - 1))
            chunk("out0", 0, "C", "B", 2 * H - 1)
            with act.Fori(1, 4) as c:
                chunk("out0", c, None, None, None)
            rows_norm(1)
            for k in range(4):
                item(f"turn{k}", None, 1)
            chunk("C", 0, "turn1", None, 1)
            with act.Fori(1, H - 1) as i:
                chunk("C", i, "C", "C", i + (2 * H - 1))
            chunk("C", H - 1, "C", "C", 3 * H - 2)
            for n in range(H):
                chunk("D", n, "C" if n == 0 else "Dkv" if n % 4 == 1 else "D", "D" if n else "C", 3 * H - 1 + n)
            chunk("out1", 0, "D", "D", 4 * H - 1)
            with act.Fori(1, 3) as c:
                chunk("out1", c, None, None, None)
            chunk("out1", 3, None, None, None)
            for t in range(ST):
                if t < ST - 1:
                    act.wait_ge(x_made, ST + t + 1)
                else:
                    act.wait_ge(last_made, 2)
                act.dma_start(out[0, t * P:(t + 1) * P, :], xrow[:, t, :]).then_inc(out_out, 16)
            act.wait_ge(out_out, 16 * ST)

        @block.vector
        def _(dve):
            def split(first, turn_units, i, s):
                n, like = unit_of(first, turn_units, i, s)
                if isinstance(n, int) and n >= U_END:
                    return
                slot, width = s % RING, unit_width(like)
                dve.wait_ge(hi_made, n + 1)
                wait(dve, w_used, n - RING + 1)
                dve.tensor_tensor(w_lo[:, slot, 0:width], raw[:, slot, 0:width],
                                  w_hi[:, slot, 0:width].bitcast(F32), ALU.subtract).then_inc(lo_made, 1)

            def rest(dst, src, hi):
                return dve.tensor_tensor(dst, src, hi.bitcast(F32), ALU.subtract)

            def new_rows(layer):
                for b in range(ST):
                    block_out(dve, b, "out0" if layer == 0 else "out1", 3)
                dve.tensor_reduce(rowvar, rowsq.rearrange("p (t c) -> p t c", t=ST), AX.X, ALU.add
                                  ).then_inc(m_total, 1)
                dve.wait_ge(m_pow, layer + 1)
                dve.wait_ge(resid_in, 16 * ST * (layer + 1))
                for t in range(ST if layer == 0 else ST - 1):
                    dve.scalar_tensor_tensor(xrow[:, t, :], mrow[:, t, :], rowstd[:, t:t + 1], resid[:, t, :],
                                             ALU.mult, ALU.add).then_inc(x_made, 1)

            def normalise(w, t, j, n):
                dve.wait_ge(exped, n)
                dve.reciprocal(rsum[:, j:j + 1], esum[:, j:j + 1]).then_inc(recip_s, 1)
                dve.wait_ge(recip_s, 4 * t + j + 1)
                dve.tensor_scalar(w.p[:, j, :], w.p[:, j, :], rsum[:, j:j + 1], None, ALU.mult).then_inc(p_made, 1)

            def mix(w, t, j, n):
                dve.wait_ge(exped, n)
                dve.reciprocal(rsum.rearrange("p (m j) -> p m j", m=2)[:, :, j],
                               esum.rearrange("p (m j) -> p m j", m=2)[:, :, j]).then_inc(recip_s, 1)
                dve.wait_ge(recip_s, 4 * t + j + 1)
                dve.scalar_tensor_tensor(mixc[:, j:j + 1], esum[:, j:j + 1], neglam, rsum[:, ST + j:ST + j + 1],
                                         ALU.mult, ALU.mult).then_inc(mixc_s, 1)
                dve.wait_ge(mixc_s, 4 * t + j + 1)
                dve.scalar_tensor_tensor(w.p[:, j, :], w.e[:, 1, :], mixc[:, j:j + 1], w.e[:, 0, :],
                                         ALU.mult, ALU.add).then_inc(p_made, 1)

            def item(what, part, t):
                w = work_of(part)
                if what[:4] == "turn":
                    k = int(what[4:])
                    n = t * KT + k
                    dve.wait_ge(xt_hi, n + 1)
                    dve.scalar_tensor_tensor(xT_lo[:, k, :], bank[4 + k % 4][:, :], pre_gain[:, n:n + 1],
                                             xT_hi[:, k, :].bitcast(F32), ALU.mult, ALU.subtract).then_inc(xt_lo, 1)
                    return
                if what[:4] == "norm":
                    j = int(what[4:])
                    dve.wait_ge(x_pow, j + 1)
                    dve.tensor_scalar(xrow0[:, j, :], xrow0[:, j, :], prestd[:, j:j + 1], None, ALU.mult
                                      ).then_inc(h_made, 1)
                    return
                if what in ("h0", "h1", "h2", "h3"):
                    cols = slice(int(what[1]) * 512, int(what[1]) * 512 + 512)
                    for j in range(ST):
                        dve.wait_ge(x_pow, ST + j + 1)
                        dve.tensor_scalar(hrow[:, j, cols], xrow[:, j, cols], prestd[:, j:j + 1], None, ALU.mult
                                          ).then_inc(h_made, 1)
                    return
                if what == "v":
                    dve.wait_ge(v_hi_s, kv_of(t, part) + 1)
                    rest(w.v_lo[:, :, :], tb[:, :].rearrange("p (a b) -> p a b", a=ST), w.v_hi[:, :, :]
                         ).then_inc(v_lo_s, 1)
                elif what[0] == "s" and what[1:].isdigit():
                    j = int(what[1:])
                    n = s_before(t, part) + j
                    if part == "A" and j >= 2 and j % 2 == 0:
                        mix(w, t, j // 2 - 1, n)
                    if part == "C" and j >= 1:
                        normalise(w, t, j - 1, n)
                    if part in ("A", "C"):
                        if j == 0:
                            dve.wait_ge(bias_in, 16 * (t + 1) if part == "A" else 16 * (t - (H - 1)))
                        if j >= 2:
                            dve.wait_ge(exped, n - 1)
                        wait_apart(dve, scored, n + 1)
                        tile = j // 2 if part == "A" else j
                        if part == "A":
                            table = bias[:, (ST - 1 - tile) * P:(ST - 1 - tile) * P + SEQ]
                        else:
                            table = bias[:, (ROWS - 2 - 2 * tile) * GRID_W:(ROWS - 2 - 2 * tile) * GRID_W + SEQ]
                        dve.tensor_tensor_reduce(w.sb[:, j % 2, :], bank[B_S[j % 2]][:, :], table,
                                                 -(SCALE_A if part == "A" else SCALE_CD), 3e38, ALU.add, ALU.min,
                                                 nmax[:, j:j + 1]).then_inc(s_read, 1)
                    else:
                        dve.wait_ge(scored, n + 1)
                        dve.tensor_reduce(nm[:, j:j + 1], bank[B_S[j % 2]][:, :], AX.X, ALU.max, negate=True
                                          ).then_inc(s_read, 1)
                        dve.wait_ge(s_read, n + 1)
                        if part == "D":
                            dve.wait_ge(d_pow, 3 * (t - 3 * H) + 3)
                        dve.tensor_scalar(nmax[:, j:j + 1], nm[:, j:j + 1],
                                          SCALE_B if part == "B" else rscale[:, j:j + 1], None, ALU.mult
                                          ).then_inc(nmaxed, 1)
                        if j >= 1:
                            normalise(w, t, j - 1, n)
                    if part == "A" and j == 7:
                        mix(w, t, 3, n + 1)
                    if part != "A" and j == 3:
                        normalise(w, t, 3, n + 1)
                elif what[:2] == "pt":
                    j = int(what[2:])
                    dve.wait_ge(pT_hi_s, 4 * t + j + 1)
                    if j >= 2:
                        dve.wait_ge(pv_done, 4 * t + j - 1)
                    rest(w.pT_lo[:, j % 2, :], turned(j)[:, :], w.pT_hi[:, j % 2, :]).then_inc(pT_lo_s, 1)
                elif what == "stat" and part == "A":
                    dve.wait_ge(a_stat, t + 1)
                    dve.tensor_tensor(var2[:, ST:2 * ST], tb[:, 0:ST], rsum[:, 0:ST], ALU.mult).then_inc(a_var, 1)
                    dve.wait_ge(a_var, 2 * t + 1)
                    dve.tensor_tensor(var[:, 0:ST], var2[:, ST:2 * ST], rsum[:, 0:ST], ALU.mult).then_inc(a_var, 1)
                elif what == "stat":
                    dve.wait_ge(d_stat, t - 3 * H + 1)
                    dve.tensor_copy(var[:, 0:ST], tb[:, 0:ST]).then_inc(d_var, 1)
                elif what == "kstat":
                    dve.wait_ge(k_stat, (t - 3 * H) // 4 + 1)
                    dve.tensor_copy(var[:, ST:2 * ST], tb[:, 0:ST]).then_inc(k_var, 1)
                elif what == "rot":
                    n = rot_of(t, part)
                    rows = ROPE_D if part == "B" else P
                    dve.wait_ge(r_rot, n + 1)
                    dve.wait_ge(rope_in, 16 if part == "B" else 32)
                    dve.tensor_tensor(w.rq_sin[0:rows, :], rb[0:rows, :], rope[0:rows, 1, :], ALU.mult
                                      ).then_inc(r_sin, 1)
                elif what == "rsum":
                    n = rot_of(t, part)
                    rows = ROPE_D if part == "B" else P
                    if part == "B":
                        dve.wait_ge(pe_hi_s, n + 1)
                        rest(pe_lo[:, :], w.rk_sin[0:rows, :], pe_hi[:, :]).then_inc(pe_lo_s, 1)
                    else:
                        dve.wait_ge(q_hi_s, t + 1)
                        rest(w.q_lo[:, :], w.rq[:, :], w.q_hi[:, :]).then_inc(q_lo_s, 1)
                elif what == "krot":
                    dve.wait_ge(kr_rot, (t - 3 * H) // 4 + 2)
                    dve.wait_ge(rope_in, 32)
                    dve.tensor_tensor(w.rk_sin[:, :], krb[:, :], rope[:, 1, :], ALU.mult).then_inc(kr_sin, 1)
                elif what == "kspread":
                    g = (t - 3 * H) // 4
                    dve.wait_ge(k_spread, g + 1)
                    dve.wait_ge(kr_sum, g + 2)
                    dve.tensor_tensor(w.rk_sin[:, :], w.rk[:, :], tb[:, :], ALU.mult).then_inc(k_scaled, 1)
                    dve.wait_ge(k_hi_s, kv_of(t, part) + 1)
                    rest(w.k_lo[:, :], w.rk_sin[:, :], w.k_hi[:, :]).then_inc(k_lo_s, 1)
                elif what == "gate":
                    dve.wait_ge(pv_done, 4 * t + 4)
                    gate_out(dve, t, part)
                    slot = bass.ds(o_slot(t, part), 1)
                    if part == "A":
                        dve.scalar_tensor_tensor(w.g[:, :], ob[:, :], gate_gain, w.g[:, :], ALU.mult, ALU.mult
                                                 ).then_inc(o_read, 1)
                        dve.wait_ge(o_read, t + 1)
                        dve.wait_ge(a_spread, t + 1)
                        dve.tensor_tensor(w.g[:, :], w.g[:, :], tb[:, :], ALU.mult).then_inc(o_gated, 1)
                        dve.wait_ge(tables_out, 16)
                        src = w.g
                    elif part == "B":
                        dve.wait_ge(o_lo_s, t)
                        gate = gates_b[:, bass.ds(t - H, 1), :].rearrange("p a s -> p (a s)")
                        dve.scalar_tensor_tensor(res_b[:, :], ob[:, :], 0.5, gate, ALU.mult, ALU.mult
                                                 ).then_inc(o_gated, 1)
                        src = res_b
                    else:
                        dve.scalar_tensor_tensor(w.g[:, :], ob[:, :], 0.5, w.g[:, :], ALU.mult, ALU.mult
                                                 ).then_inc(o_gated, 1)
                        src = w.g
                    dve.wait_ge(o_hi_s, t + 1)
                    rest(oT_lo[:, slot, :].rearrange("p a s -> p (a s)"), src[:, :],
                         oT_hi[:, slot, :].rearrange("p a s -> p (a s)")).then_inc(o_lo_s, 1)
                elif what[:3] == "tab":
                    s = int(what[3:])
                    dve.wait_ge(t_done, s + 1)
                    dst = table_all[:, :, :, 4 * s:4 * s + 4].rearrange("p h j c -> p (h j) c")
                    seen = mask[:, 4 * s:4 * s + 4].rearrange("p (a c) -> p a c", a=1).to_broadcast(
                        [P, H * (DR - 1), 4])
                    cols = bank[B_S[s % 2]][:, 0:4 * H * (DR - 1)].rearrange("p (c n) -> p n c", c=4)
                    dve.tensor_tensor(dst, cols, seen, ALU.add).then_inc(t_evac, 1)
                elif what == "krope":
                    dve.wait_ge(kr_rot, 1)
                    dve.wait_ge(rope_in, 16)
                    dve.tensor_tensor(krt[:, 2, :], tb[0:ROPE_D, :], rope[0:ROPE_D, 1, :], ALU.mult
                                      ).then_inc(kr_sin, 1)
                elif what == "lstat":
                    dve.wait_ge(l_stat, 2)
                    dve.tensor_copy(var[:, 0:2 * ST], tb[:, 0:2 * ST]).then_inc(l_var, 1)
                elif what[:5] == "lstat":
                    j = int(what[5:])
                    if j not in (0, QB):
                        done = j - 1 if j < QB else j - 2
                        dve.wait_ge(l_sq, j + 1)
                        wait(dve, l_add, done)
                        total = lsum[:, int(j > QB), :]
                        dve.tensor_tensor(total, total, lsq[:, j % 2, :], ALU.add).then_inc(l_add, 1)
                elif what[:5] == "lnorm":
                    j = int(what[5:])
                    dve.wait_ge(l_spread, 1 if j < QB else 2)
                    wait(dve, l_lo, j)
                    dve.scalar_tensor_tensor(lat_tmp[:, :], lat_raw[:, j, :], lat_gain[:, j:j + 1], tb[:, :],
                                             ALU.mult, ALU.mult).then_inc(l_mul, 1)
                    dve.wait_ge(l_hi, j + 1)
                    rest(lat_lo[:, j, :], lat_tmp[:, :], lat_hi[:, j, :]).then_inc(l_lo, 1)

            def gate_of(dst, th, src, n):
                dve.wait_ge(th_made, n)
                return dve.scalar_tensor_tensor(dst, th, 1.0, src, ALU.add, ALU.mult)

            def evac(part, i):
                w = work_of(part)
                if part in ("A", "C"):
                    t = i if part == "A" else 2 * H + i
                    dve.wait_ge(q_hi_s, t + 1)
                    rest(w.q_lo[:, :], bank[0][:, :], w.q_hi[:, :]).then_inc(bank_free[0], 1)
                    dve.wait_ge(k_hi_s, t + 1)
                    rest(w.k_lo[:, :], bank[1][:, :], w.k_hi[:, :]).then_inc(bank_free[1], 1)
                    wait(dve, o_lo_s, t)
                    gate_of(w.g[:, :], w.th[:, :], bank[3][:, :], t + 1).then_inc(bank_free[3], 1)
                elif part == "prep" and i >= 3:
                    for j, b in enumerate(gate_banks(i)):
                        gate_of(gates_b[:, 4 * (i - 3) + b, :], th_b[j % 2], bank[b][:, :], H + 4 * (i - 3) + j + 1
                                ).then_inc(bank_free[b], 1)
                elif part == "B":
                    t = H + i
                    dve.wait_ge(k_hi_s, t + 1)
                    rest(w.k_lo[:, :], bank[0][:, :], w.k_hi[:, :]).then_inc(bank_free[0], 1)
                elif part == "D":
                    t = 3 * H + i
                    dve.wait_ge(o_lo_s, t)
                    b = q_bank(i) + 1
                    gate_of(w.g[:, :], w.th[:, :], bank[b][:, :], t + 1).then_inc(bank_free[b], 1)
                elif part in ("out0", "out1"):
                    layer = 0 if part == "out0" else 1
                    if i_is_zero(i):
                        dve.wait_ge(gain_in, 16 * (layer + 1))
                    for b in range(ST):
                        block_done(dve, b, part, i)
                        dve.tensor_tensor(mrow[:, b, bass.ds(i * 512, 512)], bank[b][:, :],
                                          post_gain[:, bass.ds(i * 512, 512)], ALU.mult).then_inc(m_copied, 1)

            def queries_out(i):
                dve.wait_ge(q_hi_s, H + i + 1)
                rest(w_b.q_lo[:, :], bank[2][:, :], w_b.q_hi[:, :]).then_inc(bank_free[2], 1)
                if isinstance(i, int):
                    dve.wait_ge(kpe_hi_s, 1)
                    rest(kpe_lo[:, :], krt[:, 3, :], kpe_hi[:, :]).then_inc(kpe_lo_s, 1)

            def chunk(part, i, woven, att, t):
                first, turn_units, turn = units_of(part, i)
                late = part == "D" and i % 4 > 0
                for s, (u, place_in, _, _) in enumerate(ktiles(part, i)):
                    if place_in == 0 and not late:
                        split(first, turn_units, turn, u + AHEAD)
                    for what in WOVEN[woven].get(s, []):
                        if what == "own q":
                            queries_out(i)
                        elif what == "own rot":
                            item("rot", "B", H + i)
                            item("rsum", "B", H + i)
                        else:
                            item(what, att, t)
                    if place_in == 0 and late:
                        split(first, turn_units, turn, u + AHEAD)
                evac(part, i)
                for what in WOVEN[woven].get("end", []):
                    item(what, att, t)

            dve.wait_ge(rpb_turned, 1)
            dve.tensor_copy(rpbT[:, :, :].rearrange("p h r -> p (h r)"), tb[0:DC, 0:H * DR]).then_inc(rpb_copied, 1)
            for what in ("tab0", "tab1", "norm0", "tab2", "tab3", "norm1", "tab4", "norm2", "tab5", "tab6", "norm3"):
                item(what, None, 0)
            split(U_A, KT, 0, 0)
            split(U_A, KT, 0, 1)
            for k in range(4):
                item(f"turn{k}", None, 0)
            dve.wait_ge(lam_in, 64)
            for j in range(2):
                dve.tensor_tensor_reduce(lamp[:, j, :], lamv[:, 2 * j, :], lamv[:, 2 * j + 1, :], 1.0, 0.0, ALU.mult,
                                         ALU.add, lam[:, j:j + 1]).then_inc(lam_dot, 1)
            dve.wait_ge(consts_in, 16 * 5)
            dve.tensor_scalar(gate_gain, sub_gain, 0.5 * (1.0 - LAMBDA_INIT), None, ALU.mult).then_inc(lam_sum, 1)
            chunk("A", 0, "turn0", None, 0)
            dve.wait_ge(lam_exp, 1)
            dve.tensor_tensor(lam[:, 0:1], lam[:, 3:4], lam[:, 2:3], ALU.subtract).then_inc(lam_sum, 1)
            dve.wait_ge(lam_sum, 2)
            dve.tensor_scalar(neglam, lam[:, 0:1], -LAMBDA_INIT, None, ALU.add).then_inc(lam_sum, 1)
            dve.wait_ge(lam_sum, 3)
            with dve.Fori(1, H) as i:
                chunk("A", i, "A", "A", i - 1)
            chunk("prep", 0, "A", "A", H - 1)
            chunk("prep", 1, None, None, None)
            chunk("prep", 2, None, None, None)
            chunk("prep", 3, "lstat", None, None)
            chunk("prep", 4, "lnorm", None, None)
            chunk("B", 0, "Bfirst", None, None)
            with dve.Fori(1, H) as i:
                chunk("B", i, "B", "B", i + (H - 1))
            chunk("out0", 0, "C", "B", 2 * H - 1)
            with dve.Fori(1, 4) as c:
                chunk("out0", c, None, None, None)
            new_rows(0)
            item("h0", None, 1)
            item("h1", None, 1)
            for k in range(4):
                item(f"turn{k}", None, 1)
            chunk("C", 0, "turn1", None, 1)
            with dve.Fori(1, H) as i:
                chunk("C", i, "C", "C", i + (2 * H - 1))
            for n in range(H):
                chunk("D", n, "C" if n == 0 else "Dkv" if n % 4 == 1 else "D", "D" if n else "C", 3 * H - 1 + n)
            chunk("out1", 0, "D", "D", 4 * H - 1)
            with dve.Fori(1, 3) as c:
                chunk("out1", c, None, None, None)
            chunk("out1", 3, None, None, None)
            new_rows(1)

        @block.tensor
        def _(pe):
            def three(dst, l_hi_, l_lo_, r_hi_, r_lo_, start, stop):
                pe.matmul(dst, l_hi_, r_hi_, start=start, stop=False)
                pe.matmul(dst, l_hi_, r_lo_, start=False, stop=False)
                return pe.matmul(dst, l_lo_, r_hi_, start=False, stop=stop)

            def spread(diag, done):
                for j in range(ST):
                    mm = pe.matmul(tb[:, j * P:(j + 1) * P], ones[:, :], diag[:, j, :], start=True, stop=True)
                mm.then_inc(done, 1)

            def sum_partitions(squares_, done, col=0):
                for j in range(ST):
                    mm = pe.matmul(tb[:, col + j:col + j + 1], squares_[:, j * P:(j + 1) * P], ones[:, 0:1], start=True, stop=True)
                mm.then_inc(done, 1)

            def tb_free(what, part, t):
                if part == "A":
                    if what == "pt0":
                        pe.wait_ge(v_lo_s, t + 1)
                    elif what == "stat":
                        pe.wait_ge(pT_lo_s, 4 * t + 4)
                    elif what == "spread":
                        pe.wait_ge(a_var, 2 * t + 1)
                elif part == "C":
                    if what == "v":
                        pe.wait_ge(pT_lo_s, 4 * t)
                    elif what == "pt0":
                        pe.wait_ge(v_lo_s, t + 1)
                elif part == "B":
                    if what == "v":
                        pe.wait_ge(pT_lo_s, 4 * t)
                        pe.wait_ge(l_mul, QB + KVB)
                    elif what == "rot":
                        pe.wait_ge(exped, s_before(t, part))
                    elif what == "pt0":
                        pe.wait_ge(v_lo_s, t + 1)
                else:
                    n, g = t - 3 * H, (t - 3 * H) // 4
                    if what in ("krot", "kstat") or (what == "stat" and n % 4):
                        pe.wait_ge(pT_lo_s, 4 * t)
                    elif what == "stat":
                        pe.wait_ge(k_var, g + 1)
                    elif what == "rot":
                        pe.wait_ge(exped, s_before(t, part))
                    elif what == "kspread":
                        pe.wait_ge(d_var, n + 1)
                    elif what == "v":
                        pe.wait_ge(k_scaled, g + 1)
                    elif what == "pt0":
                        pe.wait_ge(v_lo_s if n % 4 == 0 else d_var, kv_of(t, part) + 1 if n % 4 == 0 else n + 1)

            def item(what, part, t):
                w = work_of(part)
                if what[:4] == "turn":
                    k = int(what[4:])
                    n = t * KT + k
                    rows = hrow if t else xrow0
                    pe.wait_ge(h_made, ST * (k // 4 + 2) if t else ST)
                    if k >= 4:
                        pe.wait_ge(xt_lo, n - 3)
                    elif t == 0:
                        pe.wait_ge(t_evac, EARLY_TABS)
                    for j in range(ST):
                        mm = pe.transpose(bank[4 + k % 4][:, j * P:(j + 1) * P], rows[:, j, k * P:(k + 1) * P], ident)
                    mm.then_inc(xt_turned, 1)
                    return
                if what in ("h0", "h1", "h2", "h3"):
                    return
                if part is not None:
                    tb_free(what, part, t)
                if what == "v":
                    c = chunk_of(t, part)
                    block_out(pe, {"A": 2, "B": 1, "C": 2, "D": 3}[part], part, c // 4 * 4 if part == "D" else c)
                    for j in range(ST):
                        mm = pe.transpose(tb[:, j * P:(j + 1) * P], w.vT[:, j * P:(j + 1) * P], ident)
                    mm.then_inc(v_turned, 1)
                elif what[0] == "s" and what[1:].isdigit():
                    j = int(what[1:])
                    n = s_before(t, part) + j
                    dst = bank[B_S[j % 2]][:, :]
                    if j == 0:
                        if part == "D":
                            pe.wait_ge(q_lo_s, t - 3 * H + 1)
                            pe.wait_ge(k_lo_s, (t - 3 * H) // 4 + 1)
                        else:
                            block_out(pe, 2 if part == "B" else 0, part, chunk_of(t, part))
                            block_out(pe, 0 if part == "B" else 1, part, chunk_of(t, part))
                        if part == "B":
                            pe.wait_ge(pe_lo_s, t - H + 1)
                            pe.wait_ge(kpe_lo_s, 1)
                        if part == "A":
                            pe.wait_ge(t_evac, KT)
                    if j >= 2:
                        pe.wait_ge(s_read if part in ("A", "C") else exped, n - 1)
                    if part == "A":
                        rows = slice(64 * (j % 2), 64 * (j % 2) + 64)
                        cols = slice(j // 2 * P, j // 2 * P + P)
                        mm = three(dst, w.q_hi[rows, cols], w.q_lo[rows, cols], w.k_hi[rows, :], w.k_lo[rows, :],
                                   True, True)
                    else:
                        cols = slice(j * P, j * P + P)
                        mm = three(dst, w.q_hi[:, cols], w.q_lo[:, cols], w.k_hi[:, :], w.k_lo[:, :],
                                   True, part != "B")
                        if part == "B":
                            mm = three(dst, pe_hi[:, cols], pe_lo[:, cols], kpe_hi[:, :], kpe_lo[:, :], False, True)
                    mm.then_inc(scored, 1)
                elif what[:2] == "pt":
                    j = int(what[2:])
                    if j == 0:
                        pe.wait_ge(p_made, 4 * t + 4)
                    elif j >= 2:
                        pe.wait_ge(pT_lo_s, 4 * t + j - 1)
                    for q in range(ST):
                        mm = pe.transpose(turned(j)[:, q * P:(q + 1) * P], w.p[:, q, j * P:(j + 1) * P], ident)
                    mm.then_inc(p_turned, 1)
                elif what[:2] == "pv":
                    j = int(what[2:])
                    pe.wait_ge(pT_lo_s, 4 * t + j + 1)
                    if j == 0:
                        if part != "A":
                            pe.wait_ge(o_gated, t)
                        pe.wait_ge(v_lo_s, kv_of(t, part) + 1)
                    three(ob[:, :], w.v_hi[:, j, :], w.v_lo[:, j, :], w.pT_hi[:, j % 2, :], w.pT_lo[:, j % 2, :],
                          j == 0, j == ST - 1).then_inc(pv_done, 1)
                elif what == "stat" and part == "A":
                    pe.wait_ge(o_sq, t + 1)
                    sum_partitions(w.vT, a_stat)
                elif what == "spread":
                    pe.wait_ge(a_diag, 4 * t + 4)
                    spread(w.diag, a_spread)
                elif what == "rot":
                    if part == "B":
                        block_out(pe, 3, part, chunk_of(t, part))
                    else:
                        pe.wait_ge(r_in, t - 3 * H + 1)
                    rows = ROPE_D if part == "B" else P
                    pe.matmul(rb[:, :], rotT[0:rows, :], w.rq[0:rows, :], start=True, stop=True
                              ).then_inc(r_rot, 1)
                elif what == "stat":
                    block_out(pe, q_bank(t - 3 * H), part, t - 3 * H)
                    sum_partitions(w.p[:, 0, :], d_stat)
                elif what == "krot":
                    pe.wait_ge(kr_in, (t - 3 * H) // 4 + 1)
                    pe.matmul(krb[:, :], rotT, w.rk[:, :], start=True, stop=True).then_inc(kr_rot, 1)
                elif what == "kstat":
                    block_out(pe, 2, part, t - 3 * H)
                    sum_partitions(w.p[:, 1, :], k_stat)
                elif what == "kspread":
                    pe.wait_ge(k_diag, 4 * ((t - 3 * H) // 4) + 4)
                    spread(w.diag, k_spread)
                elif what[:3] == "tab":
                    s = int(what[3:])
                    if s == 0:
                        pe.wait_ge(rpb_copied, 1)
                    if s == EARLY_TABS:
                        pe.wait_ge(xt_lo, KT)
                    if s >= 2:
                        pe.wait_ge(t_evac, s - 1)
                    n = H * (DR - 1)
                    for c in range(4):
                        col = 4 * s + c
                        pick = shift[0:DC, GRID_W - 1 - col:2 * GRID_W - 1 - col]
                        for half in range(2):
                            mm = pe.matmul(bank[B_S[s % 2]][half * GRID_W:(half + 1) * GRID_W, c * n:(c + 1) * n],
                                           pick, rpbT[:, :, 1 - half:DR - half], start=True, stop=True)
                    mm.then_inc(t_done, 1)
                elif what == "krope":
                    pe.wait_ge(o_gated, H)
                    block_out(pe, 2, "prep", 2)
                    pe.matmul(tb[0:ROPE_D, :], rotT[0:ROPE_D, 0:ROPE_D], krt[:, 0, :], start=True, stop=True
                              ).then_inc(kr_rot, 1)
                elif what == "lstat":
                    pe.wait_ge(kr_sin, 1)
                    pe.wait_ge(l_add, QB + KVB - 2)
                    for side in range(2):
                        sum_partitions(lsum[:, side, :], l_stat, side * ST)
                elif what[:5] == "lstat":
                    pass
                elif what == "lspreadq":
                    pe.wait_ge(l_var, 1)
                    pe.wait_ge(l_diag, 4)
                    spread(ldiag, l_spread)
                elif what == "lspreadk":
                    pe.wait_ge(l_mul, QB)
                    pe.wait_ge(l_diag, 8)
                    spread(ldiag, l_spread)

            def chunk(part, i, woven, att, t):
                first, turn_units, turn = units_of(part, i)
                for s, (u, place_in, places, blocks) in enumerate(ktiles(part, i)):
                    slot = u % RING
                    if place_in == 0:
                        pe.wait_ge(lo_made, first + turn * turn_units + u + 1)
                    if part in ("out0", "out1"):
                        if i_is_zero(i) and (s == 0 or u >= KT - 2):
                            pe.wait_ge(o_lo_s, (0 if part == "out0" else 2 * H) + (KT - 2 if s == 0 else u + 1))
                    elif part in ("A", "C") and i_is_zero(i):
                        pe.wait_ge(xt_lo, (0 if part == "A" else KT) + s + 1)
                    elif part == "B" and i_is_zero(i):
                        pe.wait_ge(l_lo, blocks[0][5] + 1)
                    for n, (b, c0, width, opens, closes, k) in enumerate(blocks):
                        if opens:
                            wait(pe, bank_free[b], use_of(b, part, i))
                        if part in ("out0", "out1"):
                            rows = slice(b * P, (b + 1) * P)
                            mm = three(bank[b][:, :], oT_hi[:, k, rows], oT_lo[:, k, rows],
                                       w_hi[:, slot, 0:512], w_lo[:, slot, 0:512], opens, closes)
                        else:
                            x_hi, x_lo = (lat_hi, lat_lo) if part == "B" else (xT_hi, xT_lo)
                            mm = three(bank[b][0:width, :], w_hi[:, slot, c0:c0 + width], w_lo[:, slot, c0:c0 + width],
                                       x_hi[:, k, :], x_lo[:, k, :], opens, closes)
                        if closes and not (place_in == places - 1 and n == len(blocks) - 1):
                            mm.then_inc(proj[b], 1)
                    if place_in == places - 1:
                        mm.then_inc(w_used, 1)
                    for what in WOVEN[woven].get(s, []):
                        if what == "own rot":
                            item("rot", "B", H + i)
                        elif what != "own q":
                            item(what, att, t)

            pe.wait_ge(rpb_in, 48)
            pe.transpose(tb[0:DC, 0:H * DR], rpb_rows[:, :], ident[0:H * DR, 0:H * DR]).then_inc(rpb_turned, 1)
            for k in range(EARLY_TABS):
                item(f"tab{k}", None, 0)
            pe.wait_ge(ones_set, 2)
            for k in range(4):
                item(f"turn{k}", None, 0)
            chunk("A", 0, "turn0", None, 0)
            with pe.Fori(1, H) as i:
                chunk("A", i, "A", "A", i - 1)
            chunk("prep", 0, "A", "A", H - 1)
            chunk("prep", 1, None, None, None)
            chunk("prep", 2, None, None, None)
            chunk("prep", 3, "lstat", None, None)
            chunk("prep", 4, "lnorm", None, None)
            chunk("B", 0, "Bfirst", None, None)
            with pe.Fori(1, H) as i:
                chunk("B", i, "B", "B", i + (H - 1))
            chunk("out0", 0, "C", "B", 2 * H - 1)
            with pe.Fori(1, 4) as c:
                chunk("out0", c, None, None, None)
            for k in range(4):
                item(f"turn{k}", None, 1)
            chunk("C", 0, "turn1", None, 1)
            with pe.Fori(1, H) as i:
                chunk("C", i, "C", "C", i + (2 * H - 1))
            for n in range(H):
                chunk("D", n, "C" if n == 0 else "Dkv" if n % 4 == 1 else "D", "D" if n else "C", 3 * H - 1 + n)
            chunk("out1", 0, "D", "D", 4 * H - 1)
            with pe.Fori(1, 4) as c:
                chunk("out1", c, None, None, None)


_INS = ["x", "pre_norm", "post_norm", "even_w_in", "even_w_out", "diff_lambda_q1", "diff_lambda_k1",
        "diff_lambda_q2", "diff_lambda_k2", "diff_subln", "mla_q_norm", "mla_w_uq", "mla_kv_norm", "mla_w_ukv",
        "odd_w_in", "odd_w_out", "na_rpb", "gqa_q_norm", "gqa_k_norm"]


def constants():
    f = np.float32
    p = np.arange(P)
    slopes = 2.0 ** (-8.0 * np.arange(1, H + 1) / H)
    dist = np.abs(p[:, None] - (np.arange(CW)[None, :] - (ST - 1) * P))
    alibi = (-slopes[:, None, None] / SCALE_A * dist[None]).astype(f)
    rot = np.zeros((P, P), f)
    for b in range(0, P, 64):
        for d in range(32):
            rot[b + d, b + 32 + d] = -1.0
            rot[b + 32 + d, b + d] = 1.0
    c = np.arange(GRID_W)
    c0 = np.clip(c - NA_KW // 2, 0, GRID_W - NA_KW)
    seen = (c[None, :] >= c0[:, None]) & (c[None, :] < c0[:, None] + NA_KW)
    mask = np.where(seen, 0.0, NEG).astype(f)
    small = np.concatenate([np.eye(P, dtype=f), rot.T, np.concatenate([mask, mask])], axis=1)
    shift = np.zeros((32, 2 * GRID_W - 1), f)
    for m in range(DC):
        shift[m, GRID_W - 1 + NA_KW - 1 - m] = 1.0 / SCALE_CD
    tok = np.arange(SEQ)

    def angles(pos):
        inv = f(10000.0) ** (-np.arange(32, dtype=f) / f(32))
        a = pos.astype(f)[None, :] * inv[:, None]
        a = np.concatenate([a, a])
        return np.cos(a).astype(f), np.sin(a).astype(f)
    cb, sb = angles(tok)
    cr, sr = angles(tok // GRID_W)
    cc, sc = angles(tok % GRID_W)
    return {"c_alibi": alibi, "c_small": small, "c_shift": shift, "c_rope_b": np.stack([cb, sb]),
            "c_rope_d": np.stack([np.concatenate([cr, cc]), np.concatenate([sr, sc])])}


def kernel(**inputs):
    import concourse.bacc as bacc
    from concourse.bass_utils import run_bass_kernel_spmd

    nc = bacc.Bacc("TRN2", target_bir_lowering=False, num_devices=1)
    arrays = {name: np.ascontiguousarray(inputs[name]) for name in _INS}
    arrays.update(constants())
    args = [nc.dram_tensor(f"in_{n}", a.shape, F32, kind="ExternalInput").ap() for n, a in arrays.items()]
    args.append(nc.dram_tensor("x1_dram", (SEQ, DM), F32, kind="Internal").ap())
    args.append(nc.dram_tensor("tables_dram", (H, P, CW), F32, kind="Internal").ap())
    args.append(nc.dram_tensor("out_dram", (1, SEQ, DM), F32, kind="ExternalOutput").ap())
    build(nc, *args)
    r = run_bass_kernel_spmd(nc, [{f"in_{n}": a for n, a in arrays.items()}], core_ids=[0])
    return r.results[0]["out_dram"]
```

```python
import concourse.bass as bass
from concourse import mybir
from contextlib import ExitStack
import numpy as np

F32 = mybir.dt.float32
F32R = mybir.dt.float32r
ALU = mybir.AluOpType
ACT = mybir.ActivationFunctionType
AX = mybir.AxisListType

P = 128
SEQ = 512
DM = 2048
ST = SEQ // P
KT = DM // P
H = 8
GRID_W = 64
ROWS = SEQ // GRID_W
NA_KH, NA_KW = 8, 16
DR, DC = 2 * NA_KH - 1, 2 * NA_KW - 1
CW = (DR - 1) * GRID_W
Q_RANK, KV_RANK, ROPE_D = 768, 512, 64
QB, KVB = Q_RANK // P, KV_RANK // P
LAMBDA_INIT = 0.8 - 0.6
EPS = 1e-6
NEG = -1e30
SCALE_A = 64 ** -0.5
SCALE_B = 192 ** -0.5
SCALE_CD = 128 ** -0.5

RING = 4
EARLY_TABS = 7
AHEAD = 2
SLOT = 576
KEPT = 8

LAST_PIECES = [(t, slice(c, c + DM // 2)) for t in (2, 3) for c in (0, DM // 2)]

U_A = 0
U_PREP = U_A + H * KT
U_B = U_PREP + 5 * KT
U_OUT0 = U_B + H * 4
U_C = U_OUT0 + 4 * KT
U_D = U_C + H * KT
D_GROUP = KT + 3 * (KT // 2)
U_OUT1 = U_D + 2 * D_GROUP
U_END = U_OUT1 + 4 * KT

ORDER = ([("A", i) for i in range(H)] + [("prep", i) for i in range(5)] + [("B", i) for i in range(H)]
         + [("out0", i) for i in range(4)] + [("C", i) for i in range(H)] + [("D", i) for i in range(H)]
         + [("out1", i) for i in range(4)])


def count_before(test, part, i):
    if isinstance(i, int):
        return sum(test(*c) for c in ORDER[:ORDER.index((part, i))])
    return count_before(test, part, 0) + (i if test(part, 0) else 0)


def closing(bank, part, i):
    for u, place_in, places, blocks in ktiles(part, i):
        for b in blocks:
            if b[0] == bank and b[4]:
                return u, place_in == places - 1 and b is blocks[-1]
    return None


def use_of(bank, part, i):
    return count_before(lambda p, j: closing(bank, p, j) is not None, part, i)


def proj_of(bank, part, i):
    return count_before(lambda p, j: closing(bank, p, j) is not None and not closing(bank, p, j)[1], part, i)


def s_before(t, part):
    return 8 * t if part == "A" else 32 + 4 * t


def nmax_before(t, part):
    return 4 * (t - 8) if part == "B" else 4 * (t - 16)


def rot_of(t, part):
    return t - 8 if part == "B" else t - 16


def kv_of(t, part):
    return t if part != "D" else 24 + (t - 24) // 4


def units_of(part, i):
    if part == "D":
        return U_D + i // 4 * D_GROUP + (KT + (i % 4 - 1) * KT // 2 if i % 4 else 0), 0, 0
    return {"A": U_A, "prep": U_PREP, "B": U_B, "out0": U_OUT0, "C": U_C, "out1": U_OUT1}[part], \
        4 if part == "B" else KT, i


def i_is_zero(i):
    return isinstance(i, int) and i == 0


def raw_count(u):
    total = 0
    for v in range(u % RING, u + 1, RING):
        in_d = U_D <= v < U_OUT1
        total += (3 if (v - U_D) % D_GROUP < KT else 4) if in_d else 1
    return 16 * total


def wait(eng, sem, value):
    if isinstance(value, int) and value <= 0:
        return
    eng.wait_ge(sem, value)


def wait_apart(eng, sem, value):
    eng.wait_ge(sem, value)
    eng.nop(nofuse=True)


def q_bank(i):
    return 2 if i % 4 == 2 else 0


def gate_banks(i):
    return (2, 3, 0, 1) if i == 4 else (0, 1, 2, 3)


def ktiles(part, i):
    if part == "B":
        out = [(s // 3, s % 3, 3, [(2, s % 3 * 192, P, s == 0, s == QB - 1, s),
                                   (3, s % 3 * 192 + P, ROPE_D, s == 0, s == QB - 1, s)]) for s in range(QB)]
        out += [(2 + s // 2, s % 2, 2, [(0, s % 2 * 256, P, s == 0, s == KVB - 1, QB + s),
                                        (1, s % 2 * 256 + P, P, s == 0, s == KVB - 1, QB + s)]) for s in range(KVB)]
        return out
    if part == "D" and i % 4:
        return [(s // 2, s % 2, 2, [(q_bank(i) + b, s % 2 * 256 + b * P, P, s == 0, s == KT - 1, s)
                                    for b in range(2)]) for s in range(KT)]
    blocks = [(b, b * P, P) for b in range(4)]
    if part == "prep" and i == 2:
        blocks = [(0, 0, P), (1, P, P), (2, 2 * P, ROPE_D)]
    if part == "prep" and i == 4:
        blocks = blocks[2:] + blocks[:2]

    def some(s, chosen):
        return [(*b, s == 0, s == KT - 1, s) for b in chosen]
    out = [(s, 0, 1, some(s, blocks)) for s in range(KT)]
    if isinstance(i, int) and (part, i) in (("D", 4), ("out0", 0), ("out1", 0)):
        out[:2] = [(u, place_in, 2, some(u, blocks[2:] if place_in == 0 else blocks[:2]))
                   for place_in in range(2) for u in range(2)]
    if isinstance(i, int) and part in ("out0", "out1") and i == 3:
        out[KT - KEPT:] = [(u, place_in, 2, some(u, blocks[2 * place_in:2 * place_in + 2]))
                           for place_in in range(2) for u in range(KT - KEPT, KT)]
    return out


def kept(u):
    for end in (U_C, U_END):
        if isinstance(u, int) and end - KEPT <= u < end:
            return u - (end - KEPT)
    return None


def slot_used(n):
    if isinstance(n, int) and U_C <= n < U_C + RING:
        return U_C - KEPT
    return n - RING + 1


def unit_width(u):
    if U_PREP + 2 * KT <= u < U_PREP + 3 * KT:
        return 2 * P + ROPE_D
    if U_B <= u < U_OUT0 and (u - U_B) % 4 < 2:
        return SLOT
    return 512


WOVEN = {
    "A": {0: ["v"], 1: ["s0", "s1"], 2: ["s2", "s3"], 3: ["s4", "s5"], 4: ["s6", "s7"], 6: ["pt0", "pt1"],
          7: ["pv0", "pt2"], 8: ["pv1", "pt3"], 9: ["pv2"], 10: ["pv3"], 11: ["stat"], 13: ["spread"],
          14: ["gate"]},
    "C": {0: ["v"], 1: ["s0"], 2: ["s1"], 3: ["s2"], 4: ["s3"], 6: ["pt0", "pt1"],
          7: ["pv0", "pt2"], 8: ["pv1", "pt3"], 9: ["pv2"], 10: ["pv3"], 11: ["gate"]},
    "B": {0: ["late pv2", "late pv3", "late gate", "v"], 1: ["s0"], 2: ["s1"], 3: ["s2"], 4: ["s3"],
          5: ["own q"], 6: ["pt0", "pt1"], 7: ["own rot", "pv0", "pt2"], 8: ["pv1", "pt3"]},
    "B1": {1: ["v", "s0"], 2: ["s1"], 3: ["s2"], 4: ["s3"], 5: ["own q"], 6: ["pt0", "pt1"],
          7: ["own rot", "pv0", "pt2"], 8: ["pv1", "pt3"]},
    "Bout": {0: ["late pv2", "late pv3", "late gate", "v"], 1: ["s0"], 2: ["s1"], 3: ["s2"], 4: ["s3"],
             6: ["pt0", "pt1"], 7: ["pv0", "pt2"], 8: ["pv1", "pt3"], 9: ["pv2"], 10: ["pv3"], 11: ["gate"]},
    "Bfirst": {6: ["own q"], 7: ["own rot"]},
    "D": {1: ["rot"], 2: ["stat"], 4: ["rsum"], 5: ["s0"], 6: ["s1"], 7: ["s2"], 8: ["s3"], 11: ["pt0", "pt1"],
          12: ["pv0", "pt2"], 13: ["pv1", "pt3"], 14: ["pv2", "pv3"], 15: ["gate"]},
    "Dkv": {1: ["krot", "kstat"], 2: ["rot", "stat"], 4: ["rsum"], 5: ["kspread"], 6: ["v"], 7: ["s0"],
            8: ["s1"], 9: ["s2"], 10: ["s3"], 12: ["pt0", "pt1"], 13: ["pv0", "pt2"], 14: ["pv1", "pt3"],
            15: ["pv2", "pv3", "gate"]},
    "turn0": {**{s: [f"turn{2 * s + 4}", f"turn{2 * s + 5}"] for s in range(6)},
              **{s - 1: [f"tab{s}"] + {9: ["lam0"], 11: ["lam1"], 13: ["lam2"]}.get(s, [])
                 for s in range(EARLY_TABS, 16)}},
    "turn1": {s: [f"turn{s + 4}"] + ({0: ["h2"], 4: ["h3"]}.get(s, [])) for s in range(12)},
    "lstat": {0: ["krope"], **{s + 1: [f"lstat{s}"] for s in range(QB + KVB)}, QB + KVB + 2: ["lstat"]},
    "lnorm": {0: ["lspreadq"], 1: ["lnorm0"], 2: ["lnorm1"], 3: ["lnorm2"], 4: ["lnorm3"], 5: ["lnorm4"],
              6: ["lnorm5"], 7: ["lspreadk"], 8: ["lnorm6"], 9: ["lnorm7"], 10: ["lnorm8"], 11: ["lnorm9"]},
    None: {},
}


def build(nc, x, pre_norm, post_norm, even_w_in, even_w_out, lq1, lk1, lq2, lk2, subln, q_norm, w_uq,
          kv_norm, w_ukv, odd_w_in, odd_w_out, rpb, gq_norm, gk_norm, c_alibi, c_small, c_shift,
          c_rope_b, c_rope_d, x1, tables, out):
    ctx = ExitStack()
    with ctx:
        top = [(nc.sbuf_base + 31) // 32 * 32]

        def region(size):
            at = top[0]
            top[0] += size
            assert top[0] <= nc.sbuf_usable_end, top[0]
            return at

        def place(name, at, shape, dt=F32):
            return nc.alloc_sbuf_tensor_at(name, shape, dt, offset=at)

        def sem(name):
            return ctx.enter_context(nc.semaphore(name))

        KB = 1024
        X, O, W = region(64 * KB), region(64 * KB), region(42 * KB)

        xT_hi = place("xT_hi", X, [P, KT, SEQ], F32R)
        xT_lo = place("xT_lo", X + 32 * KB, [P, KT, SEQ], F32R)
        resid = place("resid", X, [P, ST, DM])
        oT_hi = place("oT_hi", O, [P, 2 * H, SEQ], F32R)
        oT_lo = place("oT_lo", O + 32 * KB, [P, 2 * H, SEQ], F32R)
        gates_b = place("gates_b", O + 16 * KB, [P, H, SEQ])
        lsq = place("lsq", O + 48 * KB, [P, 2, SEQ])
        q_hi2 = place("q_hi2", O + 48 * KB, [P, SEQ], F32R)
        k_hi2 = place("k_hi2", O + 50 * KB, [P, SEQ], F32R)
        e_odd = place("e_odd", O + 52 * KB, [P, 2, SEQ])
        th_b = (place("th_b", O + 52 * KB, [P, SEQ])[:, :], lsq[:, 0, :])
        ldiag = place("ldiag", O + 54 * KB, [P, ST, P])
        krt = place("krt", O + 56 * KB, [ROPE_D, 4, SEQ])
        hrow = place("hrow", O + 32 * KB, [P, ST, DM])
        table_all = place("table_all", O, [P, H, DR - 1, GRID_W])
        lat_hi = place("lat_hi", W, [P, QB + KVB, SEQ], F32R)
        lat_lo = place("lat_lo", W + 20 * KB, [P, QB + KVB, SEQ], F32R)
        lat_raw = place("lat_raw", W + 20 * KB, [P, QB + KVB, SEQ])
        lsum = place("lsum", W, [P, 2, SEQ])
        lat_tmp = place("lat_tmp", W + 40 * KB, [P, SEQ])
        mrow = place("mrow", W, [P, ST, DM])
        post_gain = place("post_gain", W + 32 * KB, [P, DM])
        squares = place("squares", W + 40 * KB, [P, SEQ])

        kept_hi = place("kept_hi", X + 32 * KB, [P, KEPT, 512], F32R)
        kept_lo = place("kept_lo", X + 48 * KB, [P, KEPT, 512], F32R)

        def split_of(n, slot, width):
            if kept(n) is not None:
                return kept_hi[:, kept(n), :], kept_lo[:, kept(n), :]
            return w_hi[:, slot, 0:width], w_lo[:, slot, 0:width]

        def query_parts(slot):
            return (w_split[:, slot, 0:3 * 2 * P].rearrange("p (k c) -> p k c", k=3),
                    w_split[:, slot, 3 * 2 * P:2 * SLOT].rearrange("p (k c) -> p k c", k=3))

        class Work:
            pass

        def work(tag, at):
            w = Work()
            a = [at]

            def b(name, shape, dt=F32):
                t = place(f"{name}_{tag}", a[0], shape, dt)
                a[0] += int(np.prod(shape[1:])) * 4
                return t
            w.q_hi, w.q_lo = b("q_hi", [P, SEQ], F32R), b("q_lo", [P, SEQ], F32R)
            w.k_hi, w.k_lo = b("k_hi", [P, SEQ], F32R), b("k_lo", [P, SEQ], F32R)
            w.v_hi, w.v_lo = b("v_hi", [P, ST, P], F32R), b("v_lo", [P, ST, P], F32R)
            w.vT = b("vT", [P, SEQ])
            w.p = b("p", [P, ST, SEQ])
            w.pT_hi, w.pT_lo = b("pT_hi", [P, 2, SEQ], F32R), b("pT_lo", [P, 2, SEQ], F32R)
            w.g = b("g", [P, SEQ])
            w.diag = place(f"diag_{tag}", a[0], [P, ST, P])
            w.th = b("th", [P, SEQ])
            w.sb = place(f"sb_{tag}", a[0], [P, 2, SEQ])
            w.e = place(f"e_{tag}", a[0] + 2 * SEQ * 4, [P, 2, SEQ])
            w.rq, w.rq_sin, w.rk, w.rk_sin = (b(f"r{j}", [P, SEQ]) for j in range(4))
            w.end = a[0]
            return w

        w_acd = work("w", W)
        assert w_acd.end <= W + 42 * KB, (w_acd.end - W)
        w_b = work("x", X + 20 * KB)
        pe_hi = place("pe_hi", X, [P, SEQ], F32R)
        pe_lo = place("pe_lo", X + 2 * KB, [ROPE_D, SEQ], F32R)
        res_b = place("res_b", X + 8 * KB, [P, SEQ])
        assert w_b.end <= X + 64 * KB

        raw_at, split_at = region(RING * SLOT * 4), region(2 * RING * SLOT * 4)
        raw = place("raw", raw_at, [P, RING, SLOT])
        w_split = place("w_split", split_at, [P, RING, 2 * SLOT], F32R)
        w_hi, w_lo = w_split[:, :, 0:SLOT], w_split[:, :, SLOT:2 * SLOT]

        def small(name, cols, dt=F32, parts=P):
            return place(name, region((cols * 4 + 31) // 32 * 32), [parts, cols], dt)
        bias_at = region(CW * 4)
        bias = place("bias", bias_at, [P, CW])
        rope_at = region(2 * SEQ * 4)
        rope = place("rope", rope_at, [P, 2, SEQ])
        kpe_at = X + 4 * KB
        kpe = place("kpe", kpe_at, [P, SEQ], F32R)
        consts = small("consts", P + GRID_W)
        ident = consts[:, 0:P]
        mask = consts[:, P:P + GRID_W]
        ones = small("ones", P)
        gains = small("gains", 2 * KT + QB + KVB + 3)
        pre_gain = gains[:, 0:2 * KT]
        lat_gain = gains[:, 2 * KT:2 * KT + QB + KVB]
        sub_gain = gains[:, 2 * KT + QB + KVB:2 * KT + QB + KVB + 1]
        gq_gain = gains[:, 2 * KT + QB + KVB + 1:2 * KT + QB + KVB + 2]
        gk_gain = gains[:, 2 * KT + QB + KVB + 2:2 * KT + QB + KVB + 3]
        st = small("st", 106)
        esum = st[:, 0:8]
        rsum = st[:, 8:16]
        nmax = st[:, 16:24]
        mixc = st[:, 24:28]
        var = st[:, 28:36]
        var2 = st[:, 36:44]
        rstd = st[:, 44:52]
        rscale = st[:, 52:56]
        rowsq = st[:, 56:72]
        rowvar = st[:, 72:76]
        rowstd = st[:, 76:80]
        prevar = st[:, 94:98]
        prestd = st[:, 98:102]
        tmpvar = st[:, 102:106]
        neglam = st[:, 80:81]
        lam = st[:, 81:85]
        gate_gain = st[:, 85:86]
        kstd = st[:, 86:90]
        nm = st[:, 90:94]
        expo = small("expo", 8)

        xrow0 = place("xrow0", W, [P, ST, DM])
        sq_junk = place("sq_junk", W + 32 * KB, [P, DM])
        lamv = place("lamv", W + 40 * KB, [P, 4, 64])
        lamp = place("lamp", W + 41 * KB, [P, 2, 64])
        rpb_rows = place("rpb_rows", O + 28 * KB, [H * DR, DC])
        rpbT = place("rpbT", O + 29 * KB, [DC, H, DR])
        gain_rows = place("gain_rows", O + 31 * KB, [2 * KT, P])
        shift = place("shift", O + 30 * KB, [32, 2 * GRID_W - 1])

        bank = [ctx.enter_context(nc.psum_tensor(f"bank{i}", [P, 512], F32)) for i in range(8)]
        B_S, B_T, B_O = (4, 5), 6, 7
        tb, ob = bank[B_T], bank[B_O]

        raw_in = [sem(f"raw_in{i}") for i in range(RING)]
        hi_made, lo_made = sem("hi_made"), sem("lo_made")
        w_used = sem("w_used")
        proj = [sem(f"proj{i}") for i in range(4)]
        bank_free = [sem(f"bank_free{i}") for i in range(4)]
        consts_in, rpb_in, lam_in = sem("consts_in"), sem("rpb_in"), sem("lam_in")
        x_in = [sem(f"x_in{t}") for t in range(ST)]
        resid_in, gain_in = sem("resid_in"), sem("gain_in")
        rope_in, bias_in = sem("rope_in"), sem("bias_in")
        ones_set = sem("ones_set")
        x1_out, out_out, tables_out = sem("x1_out"), sem("out_out"), sem("tables_out")
        m_copied, m_total, m_var, m_pow, last_made = (
            sem(n) for n in ("m_copied", "m_total", "m_var", "m_pow", "last_made"))
        x_made, x_sq, x_var, x_pow, h_made = (sem(n) for n in ("x_made", "x_sq", "x_var", "x_pow", "h_made"))
        xt_turned, xt_hi, xt_lo = sem("xt_turned"), sem("xt_hi"), sem("xt_lo")
        q_hi_s, q_lo_s, k_hi_s, k_lo_s = sem("q_hi_s"), sem("q_lo_s"), sem("k_hi_s"), sem("k_lo_s")
        pe_hi_s, pe_lo_s, kpe_hi_s, kpe_lo_s = sem("pe_hi_s"), sem("pe_lo_s"), sem("kpe_hi_s"), sem("kpe_lo_s")
        q_laid, k_laid = sem("q_laid"), sem("k_laid")
        v_turned, v_hi_s, v_lo_s = sem("v_turned"), sem("v_hi_s"), sem("v_lo_s")
        th_made = sem("th_made")
        scored, s_read, nmaxed, exped = sem("scored"), sem("s_read"), sem("nmaxed"), sem("exped")
        recip_s, mixc_s, p_made = sem("recip_s"), sem("mixc_s"), sem("p_made")
        p_turned, pT_hi_s, pT_lo_s, pv_done = sem("p_turned"), sem("pT_hi_s"), sem("pT_lo_s"), sem("pv_done")
        o_read, o_gated, o_hi_s, o_lo_s = sem("o_read"), sem("o_gated"), sem("o_hi_s"), sem("o_lo_s")
        o_sq, a_stat, a_var, a_pow, a_diag, a_spread = (
            sem(n) for n in ("o_sq", "a_stat", "a_var", "a_pow", "a_diag", "a_spread"))
        r_in, r_cos, r_sin, r_sum = (sem(n) for n in ("r_in", "r_cos", "r_sin", "r_sum"))
        kr_in, kr_cos, kr_sin, kr_sum = (sem(n) for n in ("kr_in", "kr_cos", "kr_sin", "kr_sum"))
        r_lower, kr_lower = sem("r_lower"), sem("kr_lower")
        d_stat, d_var, d_pow = (sem(n) for n in ("d_stat", "d_var", "d_pow"))
        k_stat, k_var, k_pow, k_diag, k_spread, k_scaled = (
            sem(n) for n in ("k_stat", "k_var", "k_pow", "k_diag", "k_spread", "k_scaled"))
        l_sq, l_add, l_stat, l_var, l_pow, l_diag, l_spread, l_mul, l_hi, l_lo = (
            sem(n) for n in ("l_sq", "l_add", "l_stat", "l_var", "l_pow", "l_diag", "l_spread", "l_mul",
                             "l_hi", "l_lo"))
        rpb_turned, rpb_copied, t_done, t_evac = (sem(n) for n in ("rpb_turned", "rpb_copied", "t_done", "t_evac"))
        lam_dot, lam_exp, lam_sum = sem("lam_dot"), sem("lam_exp"), sem("lam_sum")

        win0, wout0, win1, wout1 = even_w_in[0], even_w_out[0], odd_w_in[0], odd_w_out[0]
        block = ctx.enter_context(nc.Block())

        def block_done(eng, b, part, i):
            u, with_unit = closing(b, part, i)
            if with_unit:
                first, turn_units, turn = units_of(part, i)
                eng.wait_ge(w_used, first + turn * turn_units + u + 1)
            else:
                eng.wait_ge(proj[b], proj_of(b, part, i) + 1)

        def block_out(eng, b, part, i):
            eng.wait_ge(bank_free[b], use_of(b, part, i) + 1)

        def chunk_of(t, part):
            return t - {"A": 0, "B": H, "C": 2 * H, "D": 3 * H}[part]

        def turned(j):
            return bank[B_S[0] if j % 2 else B_T]

        def gate_out(eng, t, part):
            if part == "B":
                block_out(eng, gate_banks(4)[3], "prep", 4)
            else:
                c = chunk_of(t, part)
                block_out(eng, q_bank(c) + 1 if part == "D" else 3, part, c)

        def work_of(part):
            return w_b if part == "B" else w_acd

        def o_slot(t, part):
            return t if part in ("A", "B") else t - 2 * H

        @block.sync
        def _(sp):
            def unit(n, slot, *pieces):
                wait(sp, lo_made, n - RING + 1)
                for c0, c1, src in pieces:
                    dst = raw[:, slot, c0:c1]
                    if len(src.shape) == 3:
                        dst = dst.rearrange("p (b c) -> p b c", b=src.shape[1])
                    sp.dma_start(dst, src).then_inc(raw_in[slot], 16)

            def head_units(w, first, i):
                for s in range(KT):
                    cols = w[s * P:(s + 1) * P, 0:4 * H * P].rearrange("p (b c) -> p b c", b=4)
                    unit(first + i * KT + s, s % RING, (0, 512, cols[:, :, bass.ds(i * P, P)]))

            sp.dma_start(rpb_rows[:, :], rpb[0].rearrange("h r c -> (h r) c")).then_inc(rpb_in, 16)
            sp.dma_start(consts[:, :], c_small[:, :]).then_inc(rpb_in, 16)
            sp.dma_start(shift[:, :], c_shift[:, :]).then_inc(rpb_in, 16)
            sp.dma_start(gain_rows[:, :], pre_norm.rearrange("l (k p) -> (l k) p", p=P)).then_inc(rpb_in, 16)
            for t in range(ST):
                sp.dma_start(xrow0[:, t, :], x[0, t * P:(t + 1) * P, :]).then_inc(x_in[t], 16)
            head_units(win0, U_A, 0)
            with sp.Fori(1, H) as i:
                head_units(win0, U_A, i)
            for c in range(5):
                c0 = 4 * H * P + (c * 512 if c < 3 else Q_RANK + KV_RANK + ROPE_D + (c - 3) * 512)
                width = 2 * P + ROPE_D if c == 2 else 512
                for s in range(KT):
                    unit(U_PREP + c * KT + s, s % RING, (0, width, win0[s * P:(s + 1) * P, c0:c0 + width]))

            def latent_units(i):
                for s in range(2):
                    src = w_uq[0, s * 384:(s + 1) * 384, bass.ds(i * 192, 192)]
                    unit(U_B + i * 4 + s, s, (0, 576, src.rearrange("(k p) c -> p k c", p=P)))
                for s in range(2):
                    src = w_ukv[0, s * 256:(s + 1) * 256, bass.ds(i * 256, 256)]
                    unit(U_B + i * 4 + 2 + s, 2 + s, (0, 512, src.rearrange("(k p) c -> p k c", p=P)))
            latent_units(0)
            with sp.Fori(1, H) as i:
                latent_units(i)

            def out_units(w, first):
                with sp.Fori(0, 4) as c:
                    for s in range(KT):
                        unit(first + c * KT + s, s % RING, (0, 512, w[s * P:(s + 1) * P, bass.ds(c * 512, 512)]))
            out_units(wout0, U_OUT0)
            with sp.Fori(0, H) as i:
                head_units(win1, U_C, i)
            q0 = 4 * H * P
            k0, g0 = q0 + H * P, q0 + H * P + 4 * P
            for g in range(2):
                for j in range(4):
                    h = 4 * g + j

                    def cols(s, c0):
                        return win1[s * P:(s + 1) * P, c0:c0 + P]
                    if j == 0:
                        for s in range(KT):
                            kv = win1[s * P:(s + 1) * P, k0:k0 + 4 * P].rearrange("p (b c) -> p b c", b=2)
                            unit(U_D + g * D_GROUP + s, s % RING, (0, P, cols(s, q0 + h * P)),
                                 (P, 2 * P, cols(s, g0 + h * P)), (2 * P, 4 * P, kv[:, :, g * P:(g + 1) * P]))
                    else:
                        for s in range(0, KT, 2):
                            unit(U_D + g * D_GROUP + KT + (j - 1) * KT // 2 + s // 2, s // 2 % RING,
                                 (0, P, cols(s, q0 + h * P)), (P, 2 * P, cols(s, g0 + h * P)),
                                 (2 * P, 3 * P, cols(s + 1, q0 + h * P)), (3 * P, 4 * P, cols(s + 1, g0 + h * P)))
            out_units(wout1, U_OUT1)

        @block.gpsimd
        def _(pool):
            pool.memset(ones[:, :], 1.0).then_inc(ones_set, 1)
            pool.memset(expo[:, :], -0.5).then_inc(ones_set, 1)
            pool.wait_ge(ones_set, 2)

            def inv_root(dst, src, scale, tmp, mid, mid_value, done):
                pool.tensor_scalar(tmp, src, scale, EPS, ALU.mult, ALU.add).then_inc(mid, 1)
                pool.wait_ge(mid, mid_value)
                pool.tensor_tensor(dst, tmp, expo[:, 0:src.shape[1]], ALU.pow).then_inc(done, 1)

            def diagonals(diag, column, done):
                for j in range(ST):
                    pool.tensor_scalar(diag[:, j, :], ident, column[:, j:j + 1], 0.0, ALU.mult, ALU.add
                                       ).then_inc(done, 1)

            def pre_rows(layer, tiles=range(ST)):
                for t in tiles:
                    n = layer * ST + t + 1
                    pool.wait_ge(x_sq, n)
                    inv_root(prestd[:, t:t + 1], prevar[:, t:t + 1], 1.0 / DM, tmpvar[:, t:t + 1], x_var, n, x_pow)

            def post_rows(layer, half):
                n = 2 * layer + half + 1
                tiles = slice(2 * half, 2 * half + 2)
                pool.wait_ge(m_total, n)
                inv_root(rowstd[:, tiles], rowvar[:, tiles], 1.0 / DM, tmpvar[:, tiles], m_var, n, m_pow)

            def post_loads(layer):
                if layer == 0:
                    pool.wait_ge(w_used, U_OUT0)
                else:
                    pool.wait_ge(o_lo_s, 4 * H)
                pool.dma_start(post_gain[:, :], post_norm[layer:layer + 1, :].to_broadcast([P, DM])
                               ).then_inc(gain_in, 16)
                if layer == 0:
                    pool.wait_ge(o_lo_s, 2 * H)
                else:
                    pool.wait_ge(w_used, U_OUT1)
                for t in range(ST):
                    pool.wait_ge(w_used, (U_OUT0 if layer == 0 else U_OUT1) + KT + 6 * t)
                    pool.dma_start(resid[:, t, :], (x[0] if layer == 0 else x1)[t * P:(t + 1) * P, :]
                                   ).then_inc(resid_in, 16)

            pre_rows(0)
            for dst, src, k in ((lat_gain[:, 0:QB], q_norm[0], QB), (lat_gain[:, QB:QB + KVB], kv_norm[0], KVB),
                                (sub_gain, subln[0], 1), (gq_gain, gq_norm[0], 1), (gk_gain, gk_norm[0], 1)):
                pool.dma_start(dst, src.rearrange("(k p) -> p k", p=P), allow_slow_non_contiguous=True
                               ).then_inc(consts_in, 16)
            for j, v in enumerate((lq1, lk1, lq2, lk2)):
                pool.dma_start(lamv[:, j, :], v[0:1, :].to_broadcast([P, 64])).then_inc(lam_in, 16)
            pool.dma_start(bias[:, :], c_alibi[0]).then_inc(bias_in, 16)
            pool.dma_start(rope[0:ROPE_D, :, :], c_rope_b.rearrange("a p s -> p a s")).then_inc(rope_in, 16)
            pool.wait_ge(t_evac, KT)
            pool.dma_start(tables.rearrange("h p c -> p h c"),
                           table_all[:, :, :, :].rearrange("p h j c -> p h (j c)")).then_inc(tables_out, 16)

            def next_bias(src, i, t, part):
                pool.wait_ge(s_read, s_before(t + 1, part))
                pool.dma_start(bias[:, :], src[bass.ds(i, 1), :, :].rearrange("a p c -> (a p) c")
                               ).then_inc(bias_in, 16)

            def a_factors(t):
                wait_apart(pool, a_var, 2 * t + 2)
                pool.tensor_scalar(var2[:, 0:ST], var[:, 0:ST], 1.0 / P, EPS, ALU.mult, ALU.add).then_inc(a_pow, 1)
                pool.wait_ge(a_pow, 3 * t + 1)
                pool.tensor_tensor(rstd[:, ST:2 * ST], var2[:, 0:ST], expo[:, 0:ST], ALU.pow).then_inc(a_pow, 1)
                pool.wait_ge(a_pow, 3 * t + 2)
                pool.tensor_tensor(rstd[:, 0:ST], rstd[:, ST:2 * ST], rsum[:, 0:ST], ALU.mult).then_inc(a_pow, 1)
                gate_out(pool, t, "A")
                wait_apart(pool, a_pow, 3 * t + 3)
                diagonals(w_acd.diag, rstd, a_diag)

            with pool.Fori(1, H) as i:
                next_bias(c_alibi, i, i - 1, "A")
                a_factors(i - 1)
            a_factors(H - 1)

            block_out(pool, 2, "prep", 2)
            pool.wait_ge(rope_in, 16)
            pool.tensor_tensor(krt[:, 1, :], krt[:, 0, :], rope[0:ROPE_D, 0, :], ALU.mult).then_inc(kr_cos, 1)
            pool.wait_ge(kr_sin, 1)
            pool.wait_ge(kr_cos, 1)
            pool.tensor_tensor(krt[:, 3, :], krt[:, 1, :], krt[:, 2, :], ALU.add).then_inc(kr_sum, 1)
            pool.wait_ge(l_var, 1)
            inv_root(rstd[:, 0:ST], var[:, 0:ST], 1.0 / Q_RANK, var2[:, 0:ST], l_pow, 1, l_pow)
            inv_root(rstd[:, ST:2 * ST], var[:, ST:2 * ST], 1.0 / KV_RANK, var2[:, ST:2 * ST], l_pow, 3, l_pow)
            pool.wait_ge(l_pow, 4)
            diagonals(ldiag, rstd[:, 0:ST], l_diag)
            pool.wait_ge(l_spread, 1)
            diagonals(ldiag, rstd[:, ST:2 * ST], l_diag)

            with pool.Fori(0, H) as i:
                block_out(pool, 3, "B", i)
                pool.tensor_tensor(w_b.rk[0:ROPE_D, :], w_b.rq[0:ROPE_D, :], rope[0:ROPE_D, 0, :], ALU.mult
                                   ).then_inc(r_cos, 1)
                pool.wait_ge(r_sin, i + 1)
                pool.wait_ge(r_cos, i + 1)
                pool.tensor_tensor(w_b.rk_sin[0:ROPE_D, :], w_b.rk[0:ROPE_D, :], w_b.rq_sin[0:ROPE_D, :], ALU.add
                                   ).then_inc(r_sum, 1)
            pool.dma_start(rope[:, :, :], c_rope_d.rearrange("a p s -> p a s")).then_inc(rope_in, 16)
            pool.wait_ge(tables_out, 16)
            pool.dma_start(bias[:, :], tables[0]).then_inc(bias_in, 16)
            post_loads(0)
            for half in range(2):
                post_rows(0, half)
                pre_rows(1, (2 * half, 2 * half + 1))
            with pool.Fori(1, H) as i:
                next_bias(tables, i, 2 * H - 1 + i, "C")

            pool.wait_ge(rope_in, 32)

            def cos_of_query(n):
                pool.wait_ge(r_in, n + 1)
                pool.tensor_tensor(w_acd.p[:, 2, :], w_acd.rq[:, :], rope[:, 0, :], ALU.mult).then_inc(r_cos, 1)

            for n in range(H):
                g = n // 4
                if n % 4 == 0:
                    pool.wait_ge(kr_in, g + 1)
                    pool.tensor_tensor(w_acd.p[:, 3, :], w_acd.rk[:, :], rope[:, 0, :], ALU.mult).then_inc(kr_cos, 1)
                    cos_of_query(n)
                    pool.wait_ge(kr_sin, g + 2)
                    pool.wait_ge(kr_cos, g + 2)
                    pool.tensor_tensor(w_acd.rk[:, :], w_acd.p[:, 3, :], w_acd.rk_sin[:, :], ALU.add
                                       ).then_inc(kr_sum, 1)
                    pool.wait_ge(k_var, g + 1)
                    inv_root(kstd, var[:, ST:2 * ST], 1.0 / P, var2[:, ST:2 * ST], k_pow, 2 * g + 1, k_pow)
                    pool.wait_ge(k_pow, 2 * g + 2)
                    gate_out(pool, 3 * H + n, "D")
                    diagonals(w_acd.diag, kstd, k_diag)
                else:
                    cos_of_query(n)
                pool.wait_ge(r_sin, H + n + 1)
                pool.wait_ge(r_cos, H + n + 1)
                pool.tensor_tensor(w_acd.rq[:, :], w_acd.p[:, 2, :], w_acd.rq_sin[:, :], ALU.add).then_inc(r_sum, 1)
                pool.wait_ge(d_var, n + 1)
                inv_root(rstd[:, 0:ST], var[:, 0:ST], 1.0 / P, var2[:, 0:ST], d_pow, 3 * n + 1, d_pow)
                pool.wait_ge(d_pow, 3 * n + 2)
                pool.tensor_scalar(rscale, rstd[:, 0:ST], SCALE_CD, 0.0, ALU.mult, ALU.add).then_inc(d_pow, 1)
            post_loads(1)
            post_rows(1, 0)
            post_rows(1, 1)
            pool.wait_ge(m_pow, 4)
            t, cols = LAST_PIECES[3]
            pool.wait_ge(resid_in, 16 * ST * 2)
            pool.tensor_scalar(mrow[:, t, cols], mrow[:, t, cols], rowstd[:, t:t + 1], 0.0, ALU.mult, ALU.add
                               ).then_inc(last_made, 1)
            pool.wait_ge(last_made, 1)
            pool.tensor_tensor(mrow[:, t, cols], mrow[:, t, cols], resid[:, t, cols], ALU.add).then_inc(last_made, 1)

        def unit_of(first, turn_units, i, s):
            n = first + i * turn_units + s
            return n, (n if isinstance(n, int) else first + s % turn_units)

        @block.scalar
        def _(act):
            def split(first, turn_units, i, s):
                n, like = unit_of(first, turn_units, i, s)
                if isinstance(n, int) and n >= U_END:
                    return
                slot, width = s % RING, unit_width(like)
                if isinstance(n, int):
                    act.wait_ge(raw_in[slot], raw_count(n))
                else:
                    act.wait_ge(raw_in[slot], raw_count(first + s) + i * (16 * turn_units // RING))
                if kept(n) is None:
                    wait(act, w_used, slot_used(n))
                if width == SLOT:
                    act.activation(query_parts(slot)[0][:, :, 0:SLOT // 3],
                                   raw[:, slot, :].rearrange("p (k c) -> p k c", k=3), ACT.Copy).then_inc(hi_made, 1)
                else:
                    act.activation(split_of(n, slot, width)[0], raw[:, slot, 0:width], ACT.Copy).then_inc(hi_made, 1)

            def rows_norm(layer, tiles=range(ST)):
                for t in tiles:
                    if layer == 0:
                        act.wait_ge(x_in[t], 16)
                    else:
                        act.wait_ge(x_made, t + 1)
                    wait(act, x_sq, ST * layer + t)
                    rows, junk = (xrow0, sq_junk[:, :]) if layer == 0 else (mrow, resid[:, 0, :])
                    act.activation(junk, rows[:, t, :], ACT.Square, accum_out=prevar[:, t:t + 1]).then_inc(x_sq, 1)
                    if layer == 1:
                        act.dma_start(x1[t * P:(t + 1) * P, :], mrow[:, t, :]).then_inc(x1_out, 16)

            def item(what, part, t):
                w = work_of(part)
                if what[:4] == "turn":
                    k = int(what[4:])
                    n = t * KT + k
                    act.wait_ge(xt_turned, n + 1)
                    act.activation(xT_hi[:, k, :], bank[4 + k % 4][:, :], ACT.Copy, scale=pre_gain[:, n:n + 1]
                                   ).then_inc(xt_hi, 1)
                    return
                if what == "lam1":
                    act.wait_ge(lam_dot, 2)
                    act.activation(lam[:, 2:4], lam[:, 0:2], ACT.Exp).then_inc(lam_exp, 1)
                    act.wait_ge(consts_in, 16 * 5)
                    return
                if what in ("lam0", "lam2"):
                    return
                if what in ("h0", "h1", "h2", "h3"):
                    return
                if what == "v":
                    act.wait_ge(v_turned, kv_of(t, part) + 1)
                    act.activation(w.v_hi[:, :, :], tb[:, :].rearrange("p (a b) -> p a b", a=ST), ACT.Copy
                                   ).then_inc(v_hi_s, 1)
                elif what[0] == "s" and what[1:].isdigit():
                    j = int(what[1:])
                    n = s_before(t, part) + j
                    if part == "A":
                        act.wait_ge(s_read, n + 1)
                        if j >= 4:
                            act.wait_ge(p_made, 4 * t + j // 2 - 1)
                        cell = j % 2 * 4 + j // 2
                        e = e_odd if j // 2 % 2 else w.e
                        act.activation(e[:, j % 2, :], w.sb[:, j % 2, :], ACT.Exp, bias=nmax[:, j:j + 1],
                                       scale=-1.0, accum_out=esum[:, cell:cell + 1]).then_inc(exped, 1)
                    elif part == "C":
                        act.wait_ge(s_read, n + 1)
                        act.wait_ge(p_turned, 4 * t)
                        act.activation(w.p[:, j, :], w.sb[:, j % 2, :], ACT.Exp, bias=nmax[:, j:j + 1],
                                       scale=-1.0, accum_out=esum[:, j:j + 1]).then_inc(exped, 1)
                    else:
                        act.wait_ge(nmaxed, nmax_before(t, part) + j + 1)
                        act.wait_ge(p_turned, 4 * t)
                        act.activation(w.p[:, j, :], bank[B_S[j % 2]][:, :], ACT.Exp, bias=nmax[:, j:j + 1],
                                       scale=SCALE_B if part == "B" else rscale[:, j:j + 1],
                                       accum_out=esum[:, j:j + 1]).then_inc(exped, 1)
                elif what[:2] == "pt":
                    j = int(what[2:])
                    act.wait_ge(p_turned, 4 * t + j + 1)
                    if j >= 2:
                        act.wait_ge(pv_done, 4 * t + j - 1)
                    act.activation(w.pT_hi[:, j % 2, :], turned(j)[:, :], ACT.Copy).then_inc(pT_hi_s, 1)
                elif what == "stat" and part == "A":
                    act.wait_ge(pv_done, 4 * t + 4)
                    act.activation(w.vT[:, :], ob[:, :], ACT.Square).then_inc(o_sq, 1)
                elif what == "rsum":
                    act.wait_ge(r_sum, rot_of(t, part) + 1)
                    if part == "B":
                        for half in range(2):
                            op = act.activation(pe_hi[half * ROPE_D:(half + 1) * ROPE_D, :], w.rk_sin[0:ROPE_D, :],
                                                ACT.Copy)
                        op.then_inc(pe_hi_s, 1)
                    else:
                        act.activation(w.q_hi[:, :], w.rq[:, :], ACT.Copy).then_inc(q_hi_s, 1)
                elif what == "kspread":
                    act.wait_ge(k_scaled, (t - 24) // 4 + 1)
                    act.activation(w.k_hi[:, :], w.rk_sin[:, :], ACT.Copy).then_inc(k_hi_s, 1)
                elif what == "gate":
                    act.wait_ge(o_gated, t + 1)
                    if part == "A":
                        act.wait_ge(tables_out, 16)
                    act.activation(oT_hi[:, bass.ds(o_slot(t, part), 1), :].rearrange("p a s -> p (a s)"),
                                   (res_b if part == "B" else w.g)[:, :], ACT.Copy).then_inc(o_hi_s, 1)
                elif what[:5] == "lstat" and what != "lstat":
                    j = int(what[5:])
                    block_out(act, j % 4, "prep", j // 4)
                    if j in (0, QB):
                        dst = lsum[:, int(j == QB), :]
                    else:
                        dst = lsq[:, j % 2, :]
                        wait(act, l_add, j - 2 if j < QB else max(QB - 1, j - 3))
                    act.activation(dst, lat_raw[:, j, :], ACT.Square).then_inc(l_sq, 1)
                elif what[:5] == "lnorm":
                    j = int(what[5:])
                    act.wait_ge(l_mul, j + 1)
                    act.activation(lat_hi[:, j, :], lat_tmp[:, :], ACT.Copy).then_inc(l_hi, 1)

            def evac(part, i, banks=range(4)):
                w = work_of(part)

                def done(b):
                    block_done(act, b, part, i)
                if part in ("A", "C"):
                    t = i if part == "A" else 2 * H + i
                    done(0)
                    wait(act, scored, s_before(t, part))
                    if part == "C" and isinstance(i, int):
                        act.wait_ge(x1_out, 16 * ST)
                    act.activation(w.q_hi[:, :], bank[0][:, :], ACT.Copy).then_inc(q_hi_s, 1)
                    done(1)
                    act.activation(w.k_hi[:, :], bank[1][:, :], ACT.Copy).then_inc(k_hi_s, 1)
                    done(2)
                    if part == "A":
                        wait(act, a_stat, t)
                    wait(act, v_turned, t)
                    act.activation(w.vT[:, :], bank[2][:, :], ACT.Copy).then_inc(bank_free[2], 1)
                    done(3)
                    if part == "A":
                        wait(act, a_spread, t)
                    act.activation(w.th[:, :], bank[3][:, :], ACT.Tanh, scale=0.5).then_inc(th_made, 1)
                    if part == "A":
                        act.wait_ge(q_hi_s, t + 1)
                        act.activation(q_hi2[64:P, :], w.q_hi[64:P, :], ACT.Copy).then_inc(q_laid, 1)
                        act.activation(q_hi2[0:64, :], w.q_hi[64:P, :], ACT.Copy).then_inc(q_laid, 1)
                        act.wait_ge(q_laid, 3 * t + 2)
                        block_out(act, 0, part, i)
                        act.activation(w.q_hi[64:P, :], w.q_hi[0:64, :], ACT.Copy).then_inc(q_laid, 1)
                elif part == "prep" and i < 3:
                    if i == 0:
                        act.wait_ge(o_lo_s, H)
                    for b in range(4 if i < 2 else 2):
                        done(b)
                        act.activation(lat_raw[:, 4 * i + b, :], bank[b][:, :], ACT.Copy
                                       ).then_inc(bank_free[b], 1)
                    if i == 2:
                        done(2)
                        act.activation(krt[:, 1, :], bank[2][ROPE_D:P, :], ACT.Copy).then_inc(kr_lower, 1)
                elif part == "prep":
                    for j, b in enumerate(gate_banks(i)):
                        done(b)
                        if j >= 2:
                            block_out(act, gate_banks(i)[j - 2], "prep", i)
                        elif i > 3:
                            block_out(act, gate_banks(i - 1)[j + 2], "prep", i - 1)
                        act.activation(th_b[j % 2], bank[b][:, :], ACT.Tanh, scale=0.5).then_inc(th_made, 1)
                elif part == "B":
                    done(0)
                    act.activation(w.k_hi[:, :], bank[0][:, :], ACT.Copy).then_inc(k_hi_s, 1)
                    done(1)
                    act.activation(w.vT[:, :], bank[1][:, :], ACT.Copy).then_inc(bank_free[1], 1)
                elif part == "D":
                    t = 3 * H + i
                    b = q_bank(i)
                    done(b)
                    act.wait_ge(exped, s_before(t, part))
                    wait(act, p_turned, 4 * t)
                    act.activation(w.rq[:, :], bank[b][:, :], ACT.Copy, scale=gq_gain).then_inc(r_in, 1)
                    act.activation(w.p[:, 0, :], bank[b][:, :], ACT.Square).then_inc(bank_free[b], 1)
                    done(b + 1)
                    act.activation(w.th[:, :], bank[b + 1][:, :], ACT.Tanh, scale=0.5).then_inc(th_made, 1)
                    if i % 4 == 0:
                        done(2)
                        act.activation(w.rk[:, :], bank[2][:, :], ACT.Copy, scale=gk_gain).then_inc(kr_in, 1)
                        act.activation(w.p[:, 1, :], bank[2][:, :], ACT.Square
                                       ).then_inc(bank_free[2], 1)
                        done(3)
                        act.activation(w.vT[:, :], bank[3][:, :], ACT.Copy).then_inc(bank_free[3], 1)
                else:
                    layer = 0 if part == "out0" else 1
                    for b in banks:
                        if b:
                            block_out(act, b - 1, part, i)
                        elif not i_is_zero(i):
                            block_out(act, 3, part, i - 1)
                        act.wait_ge(m_copied, 16 * layer + 4 * i + b + 1)
                        act.activation(squares[:, :], bank[b][:, :], ACT.Square,
                                       accum_out=rowsq[:, bass.ds(i + 4 * b, 1)]
                                       ).then_inc(bank_free[b], 1)

            def queries_out(i):
                w, t = w_b, H + i
                block_done(act, 3, "B", i)
                if i_is_zero(i):
                    act.wait_ge(w_used, U_B)
                act.wait_ge(scored, s_before(t, "B"))
                act.activation(w.rq[0:ROPE_D, :], bank[3][ROPE_D:P, :], ACT.Copy).then_inc(r_lower, 1)
                block_done(act, 2, "B", i)
                act.activation(w.q_hi[:, :], bank[2][:, :], ACT.Copy).then_inc(q_hi_s, 1)
                if i_is_zero(i):
                    act.wait_ge(kr_sum, 1)
                    act.activation(kpe[0:ROPE_D, :], krt[:, 3, :], ACT.Copy).then_inc(kpe_hi_s, 1)

            def chunk(part, i, woven, att, t):
                first, turn_units, turn = units_of(part, i)
                late = part == "D" and i % 4 > 0
                for s, (u, place_in, _, _) in enumerate(ktiles(part, i)):
                    if place_in == 0 and not late:
                        split(first, turn_units, turn, u + AHEAD)
                    for what in WOVEN[woven].get(s, []):
                        if what == "own q":
                            queries_out(i)
                        elif what == "own rot":
                            item("rot", "B", H + i)
                            item("rsum", "B", H + i)
                        elif what[:5] == "late ":
                            item(what[5:], att, t - 1)
                        else:
                            item(what, att, t)
                    if place_in == 0 and late:
                        split(first, turn_units, turn, u + AHEAD)
                if isinstance(i, int) and part in ("out0", "out1") and i == 3:
                    return
                evac(part, i)

            rows_norm(0)
            split(U_A, KT, 0, 0)
            split(U_A, KT, 0, 1)
            act.wait_ge(rpb_copied, 2)
            for k in range(4):
                item(f"turn{k}", None, 0)
            chunk("A", 0, "turn0", None, 0)
            with act.Fori(1, H) as i:
                chunk("A", i, "A", "A", i - 1)
            chunk("prep", 0, "A", "A", H - 1)
            chunk("prep", 1, None, None, None)
            chunk("prep", 2, None, None, None)
            chunk("prep", 3, "lstat", None, None)
            chunk("prep", 4, "lnorm", None, None)
            chunk("B", 0, "Bfirst", None, None)
            chunk("B", 1, "B1", "B", H)
            with act.Fori(2, H - 1) as i:
                chunk("B", i, "B", "B", i + (H - 1))
            chunk("B", H - 1, "B", "B", 2 * H - 2)
            chunk("out0", 0, "Bout", "B", 2 * H - 1)
            with act.Fori(1, 3) as c:
                chunk("out0", c, None, None, None)
            chunk("out0", 3, None, None, None)
            for tiles in ((0, 1), (2, 3)):
                evac("out0", 3, tiles)
                rows_norm(1, tiles)
            for k in range(4):
                item(f"turn{k}", None, 1)
            chunk("C", 0, "turn1", None, 1)
            with act.Fori(1, H - 1) as i:
                chunk("C", i, "C", "C", i + (2 * H - 1))
            chunk("C", H - 1, "C", "C", 3 * H - 2)
            for n in range(H):
                chunk("D", n, "C" if n == 0 else "Dkv" if n % 4 == 1 else "D", "D" if n else "C", 3 * H - 1 + n)
            chunk("out1", 0, "D", "D", 4 * H - 1)
            with act.Fori(1, 3) as c:
                chunk("out1", c, None, None, None)
            chunk("out1", 3, None, None, None)
            evac("out1", 3, (0, 1))
            for t in range(2):
                act.wait_ge(x_made, ST + t + 1)
                act.dma_start(out[0, t * P:(t + 1) * P, :], mrow[:, t, :]).then_inc(out_out, 16)
            evac("out1", 3, (2, 3))
            for n, (t, cols) in enumerate(LAST_PIECES):
                if n < 3:
                    act.wait_ge(x_made, ST + 2 + n + 1)
                else:
                    act.wait_ge(last_made, 2)
                act.dma_start(out[0, t * P:(t + 1) * P, cols], mrow[:, t, cols]).then_inc(out_out, 16)
            act.wait_ge(out_out, 16 * (2 + len(LAST_PIECES)))

        @block.vector
        def _(dve):
            def split(first, turn_units, i, s):
                n, like = unit_of(first, turn_units, i, s)
                if isinstance(n, int) and n >= U_END:
                    return
                slot, width = s % RING, unit_width(like)
                dve.wait_ge(hi_made, n + 1)
                if kept(n) is None:
                    wait(dve, w_used, slot_used(n))
                if width == SLOT:
                    parts, wide_lo = query_parts(slot)
                    raw3 = raw[:, slot, :].rearrange("p (k c) -> p k c", k=3)
                    rest(wide_lo, raw3[:, :, 0:P], parts[:, :, 0:P])
                    rest(parts[:, :, SLOT // 3:2 * P], raw3[:, :, P:SLOT // 3], parts[:, :, P:SLOT // 3]
                         ).then_inc(lo_made, 1)
                    return
                if width == 2 * P + ROPE_D:
                    rest(w_hi[:, slot, width:width + ROPE_D], raw[:, slot, 2 * P:width], w_hi[:, slot, 2 * P:width])
                    width = 2 * P
                hi, lo = split_of(n, slot, width)
                dve.tensor_tensor(lo, raw[:, slot, 0:width], hi.bitcast(F32), ALU.subtract).then_inc(lo_made, 1)

            def rest(dst, src, hi):
                return dve.tensor_tensor(dst, src, hi.bitcast(F32), ALU.subtract)

            def new_rows(layer, half):
                tiles = slice(2 * half, 2 * half + 2)
                for b in (2 * half, 2 * half + 1):
                    block_out(dve, b, "out0" if layer == 0 else "out1", 3)
                dve.tensor_reduce(rowvar[:, tiles], rowsq.rearrange("p (t c) -> p t c", t=ST)[:, tiles, :], AX.X,
                                  ALU.add).then_inc(m_total, 1)
                dve.wait_ge(m_pow, 2 * layer + half + 1)
                dve.wait_ge(resid_in, 16 * ST * (layer + 1))
                pieces = [(t, slice(0, DM)) for t in (2 * half, 2 * half + 1)]
                if (layer, half) == (1, 1):
                    pieces = LAST_PIECES[:3]
                for t, cols in pieces:
                    dve.scalar_tensor_tensor(mrow[:, t, cols], mrow[:, t, cols], rowstd[:, t:t + 1],
                                             resid[:, t, cols], ALU.mult, ALU.add).then_inc(x_made, 1)

            def turned_sines(dst, src, rows):
                for b in range(0, rows, 32):
                    p = b ^ 32
                    op = dve.tensor_tensor(dst[b:b + 32, :], src[p:p + 32, :], rope[p:p + 32, 1, :], ALU.mult)
                return op

            def normalise(w, t, j, n):
                dve.wait_ge(exped, n)
                dve.reciprocal(rsum[:, j:j + 1], esum[:, j:j + 1]).then_inc(recip_s, 1)
                dve.wait_ge(recip_s, 4 * t + j + 1)
                dve.tensor_scalar(w.p[:, j, :], w.p[:, j, :], rsum[:, j:j + 1], None, ALU.mult).then_inc(p_made, 1)

            def mix(w, t, j, n):
                dve.wait_ge(exped, n)
                dve.reciprocal(rsum.rearrange("p (m j) -> p m j", m=2)[:, :, j],
                               esum.rearrange("p (m j) -> p m j", m=2)[:, :, j]).then_inc(recip_s, 1)
                dve.wait_ge(recip_s, 4 * t + j + 1)
                dve.scalar_tensor_tensor(mixc[:, j:j + 1], esum[:, j:j + 1], neglam, rsum[:, ST + j:ST + j + 1],
                                         ALU.mult, ALU.mult).then_inc(mixc_s, 1)
                dve.wait_ge(mixc_s, 4 * t + j + 1)
                e = e_odd if j % 2 else w.e
                dve.scalar_tensor_tensor(w.p[:, j, :], e[:, 1, :], mixc[:, j:j + 1], e[:, 0, :],
                                         ALU.mult, ALU.add).then_inc(p_made, 1)

            def item(what, part, t):
                w = work_of(part)
                if what[:4] == "turn":
                    k = int(what[4:])
                    n = t * KT + k
                    dve.wait_ge(xt_hi, n + 1)
                    dve.scalar_tensor_tensor(xT_lo[:, k, :], bank[4 + k % 4][:, :], pre_gain[:, n:n + 1],
                                             xT_hi[:, k, :].bitcast(F32), ALU.mult, ALU.subtract).then_inc(xt_lo, 1)
                    return
                if what[:4] == "norm":
                    j = int(what[4:])
                    dve.wait_ge(x_pow, j + 1)
                    dve.tensor_scalar(xrow0[:, j, :], xrow0[:, j, :], prestd[:, j:j + 1], None, ALU.mult
                                      ).then_inc(h_made, 1)
                    return
                if what == "lam0":
                    dve.wait_ge(lam_in, 64)
                    for j in range(2):
                        dve.tensor_tensor_reduce(lamp[:, j, :], lamv[:, 2 * j, :], lamv[:, 2 * j + 1, :], 1.0, 0.0,
                                                 ALU.mult, ALU.add, lam[:, j:j + 1]).then_inc(lam_dot, 1)
                    dve.wait_ge(consts_in, 16 * 5)
                    dve.tensor_scalar(gate_gain, sub_gain, 0.5 * (1.0 - LAMBDA_INIT), None, ALU.mult
                                      ).then_inc(lam_sum, 1)
                    return
                if what == "lam2":
                    dve.wait_ge(lam_exp, 1)
                    dve.tensor_tensor(lam[:, 0:1], lam[:, 3:4], lam[:, 2:3], ALU.subtract).then_inc(lam_sum, 1)
                    dve.wait_ge(lam_sum, 2)
                    dve.tensor_scalar(neglam, lam[:, 0:1], -LAMBDA_INIT, None, ALU.add).then_inc(lam_sum, 1)
                    dve.wait_ge(lam_sum, 3)
                    return
                if what == "lam1":
                    return
                if what in ("h0", "h1", "h2", "h3"):
                    cols = slice(int(what[1]) * 512, int(what[1]) * 512 + 512)
                    for j in range(ST):
                        dve.wait_ge(x_pow, ST + j + 1)
                        dve.tensor_scalar(hrow[:, j, cols], mrow[:, j, cols], prestd[:, j:j + 1], None, ALU.mult
                                          ).then_inc(h_made, 1)
                    return
                if what == "v":
                    dve.wait_ge(v_hi_s, kv_of(t, part) + 1)
                    rest(w.v_lo[:, :, :], tb[:, :].rearrange("p (a b) -> p a b", a=ST), w.v_hi[:, :, :]
                         ).then_inc(v_lo_s, 1)
                elif what[0] == "s" and what[1:].isdigit():
                    j = int(what[1:])
                    n = s_before(t, part) + j
                    if part == "C" and j >= 1:
                        normalise(w, t, j - 1, n)
                    if part in ("A", "C"):
                        if j == 0:
                            dve.wait_ge(bias_in, 16 * (t + 1) if part == "A" else 16 * (t - (H - 1)))
                        if j >= 2:
                            dve.wait_ge(exped, n - 1)
                        wait_apart(dve, scored, n + 1)
                        tile = j // 2 if part == "A" else j
                        if part == "A":
                            table = bias[:, (ST - 1 - tile) * P:(ST - 1 - tile) * P + SEQ]
                        else:
                            table = bias[:, (ROWS - 2 - 2 * tile) * GRID_W:(ROWS - 2 - 2 * tile) * GRID_W + SEQ]
                        dve.tensor_tensor_reduce(w.sb[:, j % 2, :], bank[B_S[j % 2]][:, :], table,
                                                 -(SCALE_A if part == "A" else SCALE_CD), 3e38, ALU.add, ALU.min,
                                                 nmax[:, j:j + 1]).then_inc(s_read, 1)
                    else:
                        dve.wait_ge(scored, n + 1)
                        dve.tensor_reduce(nm[:, j:j + 1], bank[B_S[j % 2]][:, :], AX.X, ALU.max, negate=True
                                          ).then_inc(s_read, 1)
                        dve.wait_ge(s_read, n + 1)
                        if part == "D":
                            dve.wait_ge(d_pow, 3 * (t - 3 * H) + 3)
                        dve.tensor_scalar(nmax[:, j:j + 1], nm[:, j:j + 1],
                                          SCALE_B if part == "B" else rscale[:, j:j + 1], None, ALU.mult
                                          ).then_inc(nmaxed, 1)
                        if j >= 1:
                            normalise(w, t, j - 1, n)
                    if part == "A" and j >= 3 and j % 2:
                        mix(w, t, j // 2 - 1, n - 1)
                    if part == "A" and j == 7:
                        mix(w, t, 3, n + 1)
                    if part != "A" and j == 3:
                        normalise(w, t, 3, n + 1)
                elif what[:2] == "pt":
                    j = int(what[2:])
                    dve.wait_ge(pT_hi_s, 4 * t + j + 1)
                    if j >= 2:
                        dve.wait_ge(pv_done, 4 * t + j - 1)
                    rest(w.pT_lo[:, j % 2, :], turned(j)[:, :], w.pT_hi[:, j % 2, :]).then_inc(pT_lo_s, 1)
                elif what == "stat" and part == "A":
                    dve.wait_ge(a_stat, t + 1)
                    dve.tensor_tensor(var2[:, ST:2 * ST], tb[:, 0:ST], rsum[:, 0:ST], ALU.mult).then_inc(a_var, 1)
                    dve.wait_ge(a_var, 2 * t + 1)
                    dve.tensor_tensor(var[:, 0:ST], var2[:, ST:2 * ST], rsum[:, 0:ST], ALU.mult).then_inc(a_var, 1)
                elif what == "stat":
                    dve.wait_ge(d_stat, t - 3 * H + 1)
                    dve.tensor_copy(var[:, 0:ST], tb[:, 0:ST]).then_inc(d_var, 1)
                elif what == "kstat":
                    dve.wait_ge(k_stat, (t - 3 * H) // 4 + 1)
                    dve.tensor_copy(var[:, ST:2 * ST], tb[:, 0:ST]).then_inc(k_var, 1)
                elif what == "rot":
                    n = rot_of(t, part)
                    rows = ROPE_D if part == "B" else P
                    if part == "B":
                        block_out(dve, 3, part, chunk_of(t, part))
                    else:
                        dve.wait_ge(r_in, t - 3 * H + 1)
                        dve.wait_ge(rope_in, 32)
                    turned_sines(w.rq_sin, w.rq, rows).then_inc(r_sin, 1)
                elif what == "rsum":
                    n = rot_of(t, part)
                    rows = ROPE_D if part == "B" else P
                    if part == "B":
                        dve.wait_ge(pe_hi_s, n + 1)
                        rest(pe_lo[:, :], w.rk_sin[0:rows, :], pe_hi[0:rows, :]).then_inc(pe_lo_s, 1)
                    else:
                        dve.wait_ge(q_hi_s, t + 1)
                        rest(w.q_lo[:, :], w.rq[:, :], w.q_hi[:, :]).then_inc(q_lo_s, 1)
                elif what == "krot":
                    dve.wait_ge(kr_in, (t - 3 * H) // 4 + 1)
                    dve.wait_ge(rope_in, 32)
                    turned_sines(w.rk_sin, w.rk, P).then_inc(kr_sin, 1)
                elif what == "kspread":
                    g = (t - 3 * H) // 4
                    dve.wait_ge(k_spread, g + 1)
                    dve.wait_ge(kr_sum, g + 2)
                    dve.tensor_tensor(w.rk_sin[:, :], w.rk[:, :], tb[:, :], ALU.mult).then_inc(k_scaled, 1)
                    dve.wait_ge(k_hi_s, kv_of(t, part) + 1)
                    rest(w.k_lo[:, :], w.rk_sin[:, :], w.k_hi[:, :]).then_inc(k_lo_s, 1)
                elif what == "gate":
                    dve.wait_ge(pv_done, 4 * t + 4)
                    gate_out(dve, t, part)
                    slot = bass.ds(o_slot(t, part), 1)
                    if part == "A":
                        dve.scalar_tensor_tensor(w.g[:, :], ob[:, :], gate_gain, w.g[:, :], ALU.mult, ALU.mult
                                                 ).then_inc(o_read, 1)
                        dve.wait_ge(o_read, t + 1)
                        dve.wait_ge(a_spread, t + 1)
                        dve.tensor_tensor(w.g[:, :], w.g[:, :], tb[:, :], ALU.mult).then_inc(o_gated, 1)
                        dve.wait_ge(tables_out, 16)
                        src = w.g
                    elif part == "B":
                        dve.wait_ge(o_lo_s, t)
                        gate = gates_b[:, bass.ds(t - H, 1), :].rearrange("p a s -> p (a s)")
                        dve.scalar_tensor_tensor(res_b[:, :], ob[:, :], 0.5, gate, ALU.mult, ALU.mult
                                                 ).then_inc(o_gated, 1)
                        src = res_b
                    else:
                        dve.scalar_tensor_tensor(w.g[:, :], ob[:, :], 0.5, w.g[:, :], ALU.mult, ALU.mult
                                                 ).then_inc(o_gated, 1)
                        src = w.g
                    dve.wait_ge(o_hi_s, t + 1)
                    rest(oT_lo[:, slot, :].rearrange("p a s -> p (a s)"), src[:, :],
                         oT_hi[:, slot, :].rearrange("p a s -> p (a s)")).then_inc(o_lo_s, 1)
                elif what[:3] == "tab":
                    s = int(what[3:])
                    dve.wait_ge(t_done, s + 1)
                    dst = table_all[:, :, :, 4 * s:4 * s + 4].rearrange("p h j c -> p (h j) c")
                    seen = mask[:, 4 * s:4 * s + 4].rearrange("p (a c) -> p a c", a=1).to_broadcast(
                        [P, H * (DR - 1), 4])
                    cols = bank[B_S[s % 2]][:, 0:4 * H * (DR - 1)].rearrange("p (c n) -> p n c", c=4)
                    dve.tensor_tensor(dst, cols, seen, ALU.add).then_inc(t_evac, 1)
                elif what == "krope":
                    block_out(dve, 2, "prep", 2)
                    dve.wait_ge(rope_in, 16)
                    turned_sines(krt[:, 2, :], krt[:, 0, :], ROPE_D).then_inc(kr_sin, 1)
                elif what == "lstat":
                    dve.wait_ge(l_stat, 2)
                    dve.tensor_copy(var[:, 0:2 * ST], tb[:, 0:2 * ST]).then_inc(l_var, 1)
                elif what[:5] == "lstat":
                    j = int(what[5:])
                    if j not in (0, QB):
                        done = j - 1 if j < QB else j - 2
                        dve.wait_ge(l_sq, j + 1)
                        wait(dve, l_add, done)
                        total = lsum[:, int(j > QB), :]
                        dve.tensor_tensor(total, total, lsq[:, j % 2, :], ALU.add).then_inc(l_add, 1)
                elif what[:5] == "lnorm":
                    j = int(what[5:])
                    dve.wait_ge(l_spread, 1 if j < QB else 2)
                    wait(dve, l_lo, j)
                    dve.scalar_tensor_tensor(lat_tmp[:, :], lat_raw[:, j, :], lat_gain[:, j:j + 1], tb[:, :],
                                             ALU.mult, ALU.mult).then_inc(l_mul, 1)
                    dve.wait_ge(l_hi, j + 1)
                    rest(lat_lo[:, j, :], lat_tmp[:, :], lat_hi[:, j, :]).then_inc(l_lo, 1)

            def gate_of(dst, th, src, n):
                dve.wait_ge(th_made, n)
                return dve.scalar_tensor_tensor(dst, th, 1.0, src, ALU.add, ALU.mult)

            def evac(part, i, banks=range(4)):
                w = work_of(part)
                if part in ("A", "C"):
                    t = i if part == "A" else 2 * H + i
                    dve.wait_ge(q_hi_s, t + 1)
                    rest(w.q_lo[:, :], bank[0][:, :], w.q_hi[:, :]).then_inc(bank_free[0], 1)
                    dve.wait_ge(k_hi_s, t + 1)
                    rest(w.k_lo[:, :], bank[1][:, :], w.k_hi[:, :]).then_inc(bank_free[1], 1)
                    wait(dve, o_lo_s, t)
                    gate_of(w.g[:, :], w.th[:, :], bank[3][:, :], t + 1).then_inc(bank_free[3], 1)
                    if part == "A":
                        block_out(dve, 1, part, i)
                        dve.tensor_copy(k_hi2[64:P, :], w.k_hi[64:P, :]).then_inc(k_laid, 1)
                        dve.tensor_copy(k_hi2[0:64, :], w.k_lo[64:P, :]).then_inc(k_laid, 1)
                        dve.wait_ge(k_laid, 3 * t + 2)
                        dve.tensor_copy(w.k_hi[64:P, :], w.k_lo[0:64, :]).then_inc(k_laid, 1)
                elif part == "prep" and i == 2:
                    dve.wait_ge(kr_lower, 1)
                    dve.tensor_tensor(krt[:, 0, :], bank[2][0:ROPE_D, :], krt[:, 1, :], ALU.add
                                      ).then_inc(bank_free[2], 1)
                elif part == "prep" and i >= 3:
                    for j, b in enumerate(gate_banks(i)):
                        gate_of(gates_b[:, 4 * (i - 3) + b, :], th_b[j % 2], bank[b][:, :], H + 4 * (i - 3) + j + 1
                                ).then_inc(bank_free[b], 1)
                elif part == "B":
                    t = H + i
                    dve.wait_ge(k_hi_s, t + 1)
                    rest(w.k_lo[:, :], bank[0][:, :], w.k_hi[:, :]).then_inc(bank_free[0], 1)
                elif part == "D":
                    t = 3 * H + i
                    dve.wait_ge(o_lo_s, t)
                    b = q_bank(i) + 1
                    gate_of(w.g[:, :], w.th[:, :], bank[b][:, :], t + 1).then_inc(bank_free[b], 1)
                elif part in ("out0", "out1"):
                    layer = 0 if part == "out0" else 1
                    if i_is_zero(i):
                        dve.wait_ge(gain_in, 16 * (layer + 1))
                    for b in banks:
                        block_done(dve, b, part, i)
                        dve.tensor_tensor(mrow[:, b, bass.ds(i * 512, 512)], bank[b][:, :],
                                          post_gain[:, bass.ds(i * 512, 512)], ALU.mult).then_inc(m_copied, 1)

            def queries_out(i):
                dve.wait_ge(r_lower, i + 1)
                dve.tensor_tensor(w_b.rq[0:ROPE_D, :], bank[3][0:ROPE_D, :], w_b.rq[0:ROPE_D, :], ALU.add
                                  ).then_inc(bank_free[3], 1)
                dve.wait_ge(q_hi_s, H + i + 1)
                rest(w_b.q_lo[:, :], bank[2][:, :], w_b.q_hi[:, :]).then_inc(bank_free[2], 1)
                if i_is_zero(i):
                    dve.wait_ge(kpe_hi_s, 1)
                    rest(kpe[ROPE_D:P, :], krt[:, 3, :], kpe[0:ROPE_D, :]).then_inc(kpe_lo_s, 1)

            def chunk(part, i, woven, att, t):
                first, turn_units, turn = units_of(part, i)
                late = part == "D" and i % 4 > 0
                for s, (u, place_in, _, _) in enumerate(ktiles(part, i)):
                    if place_in == 0 and not late:
                        split(first, turn_units, turn, u + AHEAD)
                    for what in WOVEN[woven].get(s, []):
                        if what == "own q":
                            queries_out(i)
                        elif what == "own rot":
                            item("rot", "B", H + i)
                            item("rsum", "B", H + i)
                        elif what[:5] == "late ":
                            item(what[5:], att, t - 1)
                        else:
                            item(what, att, t)
                    if place_in == 0 and late:
                        split(first, turn_units, turn, u + AHEAD)
                if isinstance(i, int) and part in ("out0", "out1") and i == 3:
                    return
                evac(part, i)

            dve.wait_ge(rpb_turned, 1)
            dve.tensor_copy(rpbT[:, :, :].rearrange("p h r -> p (h r)"), tb[0:DC, 0:H * DR]).then_inc(rpb_copied, 1)
            dve.tensor_copy(pre_gain, tb[:, P:P + 2 * KT]).then_inc(rpb_copied, 1)
            for what in ("tab0", "tab1", "norm0", "tab2", "tab3", "norm1", "tab4", "norm2", "tab5", "tab6", "norm3"):
                item(what, None, 0)
            split(U_A, KT, 0, 0)
            split(U_A, KT, 0, 1)
            for k in range(4):
                item(f"turn{k}", None, 0)
            chunk("A", 0, "turn0", None, 0)
            with dve.Fori(1, H) as i:
                chunk("A", i, "A", "A", i - 1)
            chunk("prep", 0, "A", "A", H - 1)
            chunk("prep", 1, None, None, None)
            chunk("prep", 2, None, None, None)
            chunk("prep", 3, "lstat", None, None)
            chunk("prep", 4, "lnorm", None, None)
            chunk("B", 0, "Bfirst", None, None)
            chunk("B", 1, "B1", "B", H)
            with dve.Fori(2, H - 1) as i:
                chunk("B", i, "B", "B", i + (H - 1))
            chunk("B", H - 1, "B", "B", 2 * H - 2)
            chunk("out0", 0, "Bout", "B", 2 * H - 1)
            with dve.Fori(1, 3) as c:
                chunk("out0", c, None, None, None)
            chunk("out0", 3, None, None, None)
            for half in range(2):
                evac("out0", 3, (2 * half, 2 * half + 1))
                new_rows(0, half)
            item("h0", None, 1)
            item("h1", None, 1)
            for k in range(4):
                item(f"turn{k}", None, 1)
            chunk("C", 0, "turn1", None, 1)
            with dve.Fori(1, H) as i:
                chunk("C", i, "C", "C", i + (2 * H - 1))
            for n in range(H):
                chunk("D", n, "C" if n == 0 else "Dkv" if n % 4 == 1 else "D", "D" if n else "C", 3 * H - 1 + n)
            chunk("out1", 0, "D", "D", 4 * H - 1)
            with dve.Fori(1, 3) as c:
                chunk("out1", c, None, None, None)
            chunk("out1", 3, None, None, None)
            for half in range(2):
                evac("out1", 3, (2 * half, 2 * half + 1))
                new_rows(1, half)

        @block.tensor
        def _(pe):
            def three(dst, l_hi_, l_lo_, r_hi_, r_lo_, start, stop):
                pe.matmul(dst, l_hi_, r_hi_, start=start, stop=False)
                pe.matmul(dst, l_hi_, r_lo_, start=False, stop=False)
                return pe.matmul(dst, l_lo_, r_hi_, start=False, stop=stop)

            def spread(diag, done):
                for j in range(ST):
                    mm = pe.matmul(tb[:, j * P:(j + 1) * P], ones[:, :], diag[:, j, :], start=True, stop=True)
                mm.then_inc(done, 1)

            def sum_partitions(squares_, done, col=0):
                for j in range(ST):
                    mm = pe.matmul(tb[:, col + j:col + j + 1], squares_[:, j * P:(j + 1) * P], ones[:, 0:1],
                                   start=True, stop=True)
                mm.then_inc(done, 1)

            def scores_a(dst, w, j):
                cols = slice(j // 2 * P, j // 2 * P + P)
                rows = slice(64 * (j % 2), 64 * (j % 2) + 64)
                q, k = (q_hi2, k_hi2) if j % 2 else (w.q_hi, w.k_hi)
                pe.matmul(dst, q[:, cols], k[:, :], start=True, stop=False)
                return pe.matmul(dst, w.q_lo[rows, cols], k[rows, :], start=False, stop=True)

            def tb_free(what, part, t):
                if part == "A":
                    if what == "pt0":
                        pe.wait_ge(v_lo_s, t + 1)
                    elif what == "stat":
                        pe.wait_ge(pT_lo_s, 4 * t + 4)
                    elif what == "spread":
                        pe.wait_ge(a_var, 2 * t + 1)
                elif part == "C":
                    if what == "v":
                        pe.wait_ge(pT_lo_s, 4 * t)
                    elif what == "pt0":
                        pe.wait_ge(v_lo_s, t + 1)
                elif part == "B":
                    if what == "v":
                        pe.wait_ge(pT_lo_s, 4 * t)
                        pe.wait_ge(l_mul, QB + KVB)
                    elif what == "pt0":
                        pe.wait_ge(v_lo_s, t + 1)
                else:
                    n, g = t - 3 * H, (t - 3 * H) // 4
                    if what == "kstat" or (what == "stat" and n % 4):
                        pe.wait_ge(pT_lo_s, 4 * t)
                    elif what == "stat":
                        pe.wait_ge(k_var, g + 1)
                    elif what == "kspread":
                        pe.wait_ge(d_var, n + 1)
                    elif what == "v":
                        pe.wait_ge(k_scaled, g + 1)
                    elif what == "pt0":
                        pe.wait_ge(v_lo_s if n % 4 == 0 else d_var, kv_of(t, part) + 1 if n % 4 == 0 else n + 1)

            def item(what, part, t):
                w = work_of(part)
                if what[:4] == "turn":
                    k = int(what[4:])
                    n = t * KT + k
                    rows = hrow if t else xrow0
                    pe.wait_ge(h_made, ST * (k // 4 + 2) if t else ST)
                    if k >= 4:
                        pe.wait_ge(xt_lo, n - 3)
                    elif t == 0:
                        pe.wait_ge(t_evac, EARLY_TABS)
                    for j in range(ST):
                        mm = pe.transpose(bank[4 + k % 4][:, j * P:(j + 1) * P], rows[:, j, k * P:(k + 1) * P], ident)
                    mm.then_inc(xt_turned, 1)
                    return
                if what in ("lam0", "lam1", "lam2"):
                    return
                if what in ("h0", "h1", "h2", "h3"):
                    return
                if part is not None:
                    tb_free(what, part, t)
                if what == "v":
                    c = chunk_of(t, part)
                    block_out(pe, {"A": 2, "B": 1, "C": 2, "D": 3}[part], part, c // 4 * 4 if part == "D" else c)
                    for j in range(ST):
                        mm = pe.transpose(tb[:, j * P:(j + 1) * P], w.vT[:, j * P:(j + 1) * P], ident)
                    mm.then_inc(v_turned, 1)
                elif what[0] == "s" and what[1:].isdigit():
                    j = int(what[1:])
                    n = s_before(t, part) + j
                    dst = bank[B_S[j % 2]][:, :]
                    if j == 0:
                        if part == "D":
                            pe.wait_ge(q_lo_s, t - 3 * H + 1)
                            pe.wait_ge(k_lo_s, (t - 3 * H) // 4 + 1)
                        else:
                            block_out(pe, 2 if part == "B" else 0, part, chunk_of(t, part))
                            block_out(pe, 0 if part == "B" else 1, part, chunk_of(t, part))
                        if part == "B":
                            pe.wait_ge(pe_lo_s, t - H + 1)
                            pe.wait_ge(kpe_lo_s, 1)
                        if part == "A":
                            pe.wait_ge(q_laid, 3 * t + 3)
                            pe.wait_ge(k_laid, 3 * t + 3)
                            pe.wait_ge(t_evac, KT)
                    if j >= 2:
                        pe.wait_ge(s_read if part in ("A", "C") else exped, n - 1)
                    if part == "A":
                        mm = scores_a(dst, w, j)
                    else:
                        cols = slice(j * P, j * P + P)
                        mm = three(dst, w.q_hi[:, cols], w.q_lo[:, cols], w.k_hi[:, :], w.k_lo[:, :],
                                   True, part != "B")
                        if part == "B":
                            pe.matmul(dst, pe_hi[:, cols], kpe[:, :], start=False, stop=False)
                            mm = pe.matmul(dst, pe_lo[:, cols], kpe[0:ROPE_D, :], start=False, stop=True)
                    mm.then_inc(scored, 1)
                elif what[:2] == "pt":
                    j = int(what[2:])
                    if j == 0:
                        pe.wait_ge(p_made, 4 * t + 4)
                    elif j >= 2:
                        pe.wait_ge(pT_lo_s, 4 * t + j - 1)
                    for q in range(ST):
                        mm = pe.transpose(turned(j)[:, q * P:(q + 1) * P], w.p[:, q, j * P:(j + 1) * P], ident)
                    mm.then_inc(p_turned, 1)
                elif what[:2] == "pv":
                    j = int(what[2:])
                    pe.wait_ge(pT_lo_s, 4 * t + j + 1)
                    if j == 0:
                        if part != "A":
                            pe.wait_ge(o_gated, t)
                        pe.wait_ge(v_lo_s, kv_of(t, part) + 1)
                    three(ob[:, :], w.v_hi[:, j, :], w.v_lo[:, j, :], w.pT_hi[:, j % 2, :], w.pT_lo[:, j % 2, :],
                          j == 0, j == ST - 1).then_inc(pv_done, 1)
                elif what == "stat" and part == "A":
                    pe.wait_ge(o_sq, t + 1)
                    sum_partitions(w.vT, a_stat)
                elif what == "spread":
                    pe.wait_ge(a_diag, 4 * t + 4)
                    spread(w.diag, a_spread)
                elif what == "stat":
                    block_out(pe, q_bank(t - 3 * H), part, t - 3 * H)
                    sum_partitions(w.p[:, 0, :], d_stat)
                elif what == "kstat":
                    block_out(pe, 2, part, t - 3 * H)
                    sum_partitions(w.p[:, 1, :], k_stat)
                elif what == "kspread":
                    pe.wait_ge(k_diag, 4 * ((t - 3 * H) // 4) + 4)
                    spread(w.diag, k_spread)
                elif what[:3] == "tab":
                    s = int(what[3:])
                    if s == 0:
                        pe.wait_ge(rpb_copied, 2)
                    if s == EARLY_TABS:
                        pe.wait_ge(xt_lo, KT)
                    if s >= 2:
                        pe.wait_ge(t_evac, s - 1)
                    n = H * (DR - 1)
                    for c in range(4):
                        col = 4 * s + c
                        pick = shift[0:DC, GRID_W - 1 - col:2 * GRID_W - 1 - col]
                        for half in range(2):
                            mm = pe.matmul(bank[B_S[s % 2]][half * GRID_W:(half + 1) * GRID_W, c * n:(c + 1) * n],
                                           pick, rpbT[:, :, 1 - half:DR - half], start=True, stop=True)
                    mm.then_inc(t_done, 1)
                elif what == "lstat":
                    pe.wait_ge(o_gated, H)
                    pe.wait_ge(l_add, QB + KVB - 2)
                    for side in range(2):
                        sum_partitions(lsum[:, side, :], l_stat, side * ST)
                elif what[:5] == "lstat":
                    pass
                elif what == "lspreadq":
                    pe.wait_ge(l_var, 1)
                    pe.wait_ge(l_diag, 4)
                    spread(ldiag, l_spread)
                elif what == "lspreadk":
                    pe.wait_ge(l_mul, QB)
                    pe.wait_ge(l_diag, 8)
                    spread(ldiag, l_spread)

            def chunk(part, i, woven, att, t):
                first, turn_units, turn = units_of(part, i)
                for s, (u, place_in, places, blocks) in enumerate(ktiles(part, i)):
                    slot = u % RING
                    if place_in == 0:
                        pe.wait_ge(lo_made, first + turn * turn_units + u + 1)
                    if part in ("out0", "out1"):
                        if i_is_zero(i) and (s == 0 or u >= KT - 2):
                            pe.wait_ge(o_lo_s, (0 if part == "out0" else 2 * H) + (KT - 2 if s == 0 else u + 1))
                    elif part in ("A", "C") and i_is_zero(i):
                        pe.wait_ge(xt_lo, (0 if part == "A" else KT) + s + 1)
                    elif part == "B" and i_is_zero(i):
                        pe.wait_ge(l_lo, blocks[0][5] + 1)
                    for n, (b, c0, width, opens, closes, k) in enumerate(blocks):
                        if opens:
                            wait(pe, bank_free[b], use_of(b, part, i))
                        if part in ("out0", "out1"):
                            rows = slice(b * P, (b + 1) * P)
                            unit_hi, unit_lo = split_of(first + turn * turn_units + u, slot, 512)
                            mm = three(bank[b][:, :], oT_hi[:, k, rows], oT_lo[:, k, rows], unit_hi, unit_lo,
                                       opens, closes)
                        elif width == ROPE_D:
                            x_hi, x_lo = (lat_hi, lat_lo) if part == "B" else (xT_hi, xT_lo)
                            c0 = place_in * 2 * P + P if part == "B" else c0
                            pe.matmul(bank[b][:, :], w_split[:, slot, c0:c0 + 2 * width], x_hi[:, k, :],
                                      start=opens, stop=False, skip_group_check=True)
                            mm = pe.matmul(bank[b][0:width, :], w_split[:, slot, c0:c0 + width], x_lo[:, k, :],
                                           start=False, stop=closes, skip_group_check=True)
                        elif part == "B" and u < 2:
                            parts, wide_lo = query_parts(slot)
                            mm = three(bank[b][:, :], parts[:, place_in, 0:P], wide_lo[:, place_in, :],
                                       lat_hi[:, k, :], lat_lo[:, k, :], opens, closes)
                        else:
                            x_hi, x_lo = (lat_hi, lat_lo) if part == "B" else (xT_hi, xT_lo)
                            mm = three(bank[b][0:width, :], w_hi[:, slot, c0:c0 + width], w_lo[:, slot, c0:c0 + width],
                                       x_hi[:, k, :], x_lo[:, k, :], opens, closes)
                        if closes and not (place_in == places - 1 and n == len(blocks) - 1):
                            mm.then_inc(proj[b], 1)
                    if place_in == places - 1:
                        mm.then_inc(w_used, 1)
                    for what in WOVEN[woven].get(s, []):
                        if what == "own rot":
                            item("rot", "B", H + i)
                        elif what[:5] == "late ":
                            item(what[5:], att, t - 1)
                        elif what != "own q":
                            item(what, att, t)

            pe.wait_ge(rpb_in, 64)
            pe.transpose(tb[0:DC, 0:H * DR], rpb_rows[:, :], ident[0:H * DR, 0:H * DR])
            pe.transpose(tb[:, P:P + 2 * KT], gain_rows[:, :], ident[0:2 * KT, 0:2 * KT]).then_inc(rpb_turned, 1)
            for k in range(EARLY_TABS):
                item(f"tab{k}", None, 0)
            pe.wait_ge(ones_set, 2)
            for k in range(4):
                item(f"turn{k}", None, 0)
            chunk("A", 0, "turn0", None, 0)
            with pe.Fori(1, H) as i:
                chunk("A", i, "A", "A", i - 1)
            chunk("prep", 0, "A", "A", H - 1)
            chunk("prep", 1, None, None, None)
            chunk("prep", 2, None, None, None)
            chunk("prep", 3, "lstat", None, None)
            chunk("prep", 4, "lnorm", None, None)
            chunk("B", 0, "Bfirst", None, None)
            chunk("B", 1, "B1", "B", H)
            with pe.Fori(2, H) as i:
                chunk("B", i, "B", "B", i + (H - 1))
            chunk("out0", 0, "Bout", "B", 2 * H - 1)
            with pe.Fori(1, 3) as c:
                chunk("out0", c, None, None, None)
            chunk("out0", 3, None, None, None)
            for k in range(4):
                item(f"turn{k}", None, 1)
            chunk("C", 0, "turn1", None, 1)
            with pe.Fori(1, H) as i:
                chunk("C", i, "C", "C", i + (2 * H - 1))
            for n in range(H):
                chunk("D", n, "C" if n == 0 else "Dkv" if n % 4 == 1 else "D", "D" if n else "C", 3 * H - 1 + n)
            chunk("out1", 0, "D", "D", 4 * H - 1)
            with pe.Fori(1, 3) as c:
                chunk("out1", c, None, None, None)
            chunk("out1", 3, None, None, None)


_INS = ["x", "pre_norm", "post_norm", "even_w_in", "even_w_out", "diff_lambda_q1", "diff_lambda_k1",
        "diff_lambda_q2", "diff_lambda_k2", "diff_subln", "mla_q_norm", "mla_w_uq", "mla_kv_norm", "mla_w_ukv",
        "odd_w_in", "odd_w_out", "na_rpb", "gqa_q_norm", "gqa_k_norm"]


def constants():
    f = np.float32
    p = np.arange(P)
    slopes = 2.0 ** (-8.0 * np.arange(1, H + 1) / H)
    dist = np.abs(p[:, None] - (np.arange(CW)[None, :] - (ST - 1) * P))
    alibi = (-slopes[:, None, None] / SCALE_A * dist[None]).astype(f)
    c = np.arange(GRID_W)
    c0 = np.clip(c - NA_KW // 2, 0, GRID_W - NA_KW)
    seen = (c[None, :] >= c0[:, None]) & (c[None, :] < c0[:, None] + NA_KW)
    mask = np.where(seen, 0.0, NEG).astype(f)
    small = np.concatenate([np.eye(P, dtype=f), np.concatenate([mask, mask])], axis=1)
    shift = np.zeros((32, 2 * GRID_W - 1), f)
    for m in range(DC):
        shift[m, GRID_W - 1 + NA_KW - 1 - m] = 1.0 / SCALE_CD
    tok = np.arange(SEQ)

    def angles(pos):
        inv = f(10000.0) ** (-np.arange(32, dtype=f) / f(32))
        a = pos.astype(f)[None, :] * inv[:, None]
        a = np.concatenate([a, a])
        return np.cos(a).astype(f), np.sin(a).astype(f)
    cb, sb = angles(tok)
    cr, sr = angles(tok // GRID_W)
    cc, sc = angles(tok % GRID_W)

    def partners(sin):
        return np.concatenate([np.concatenate([sin[b + 32:b + 64], -sin[b:b + 32]])
                               for b in range(0, len(sin), 64)])
    return {"c_alibi": alibi, "c_small": small, "c_shift": shift, "c_rope_b": np.stack([cb, partners(sb)]),
            "c_rope_d": np.stack([np.concatenate([cr, cc]), partners(np.concatenate([sr, sc]))])}


def kernel(**inputs):
    import concourse.bacc as bacc
    from concourse.bass_utils import run_bass_kernel_spmd

    nc = bacc.Bacc("TRN2", target_bir_lowering=False, num_devices=1)
    arrays = {name: np.ascontiguousarray(inputs[name]) for name in _INS}
    arrays.update(constants())
    args = [nc.dram_tensor(f"in_{n}", a.shape, F32, kind="ExternalInput").ap() for n, a in arrays.items()]
    args.append(nc.dram_tensor("x1_dram", (SEQ, DM), F32, kind="Internal").ap())
    args.append(nc.dram_tensor("tables_dram", (H, P, CW), F32, kind="Internal").ap())
    args.append(nc.dram_tensor("out_dram", (1, SEQ, DM), F32, kind="ExternalOutput").ap())
    build(nc, *args)
    r = run_bass_kernel_spmd(nc, [{f"in_{n}": a for n, a in arrays.items()}], core_ids=[0])
    return r.results[0]["out_dram"]
```
